# Optimizing a Trainium2 kernel written in Bass

```python
import math, functools
import jax, jax.numpy as jnp
from jax import lax
import numpy as np

D_MODEL = 1024
BATCH = 1
SEQ = 512
DEPTH = 2
DEC_BATCH = 8
DEC_SEQ = 1
PAST_LEN = 512
PAGE_SIZE = 128

N_A_LAYERS = DEPTH // 2
N_B_LAYERS = DEPTH - N_A_LAYERS
SSM_EXPAND = 2
SSM_WIDTH = SSM_EXPAND * D_MODEL
SSM_GROUP = 16
SSM_GROUPS = SSM_WIDTH // SSM_GROUP
SSM_STATE = 64
SSM_CHUNK = 128
DT_MIN = 0.001
DT_MAX = 0.1
HEAD_DIM = 64
N_HEADS = D_MODEL // HEAD_DIM
ATTN_WIDTH = N_HEADS * HEAD_DIM
DILATION_GROUPS = ((128, 1), (512, 4), (2048, 16))
N_GROUPS = len(DILATION_GROUPS)
MAX_WINDOW = max(w for w, _ in DILATION_GROUPS)
ALIBI_MAX_EXP = 8.0
RMS_EPS = 1e-6
NEG_INF = -1e30

kernel_name = 'yoco_s5_dilated_alibi_step'

def rms_norm(x, g):
    xf = x.astype(jnp.float32)
    y = xf * lax.rsqrt(jnp.mean(xf * xf, axis=-1, keepdims=True) + RMS_EPS)
    return (y * g.astype(jnp.float32)).astype(x.dtype)

def alibi_slopes():
    n = N_GROUPS * N_HEADS
    e = jnp.arange(1, n + 1, dtype=jnp.float32)
    return jnp.exp2(-ALIBI_MAX_EXP * e / n).reshape(N_GROUPS, N_HEADS)

def s5_discretize(lam_re, lam_im, log_dt, b_re, b_im):
    lam_re = lam_re.astype(jnp.float32)
    lam_im = lam_im.astype(jnp.float32)
    dt = jnp.exp(log_dt.astype(jnp.float32))[:, None]
    mag = jnp.exp(lam_re * dt)
    ab_re = mag * jnp.cos(lam_im * dt)
    ab_im = mag * jnp.sin(lam_im * dt)
    den = lam_re * lam_re + lam_im * lam_im
    num_re = ab_re - 1.0
    coef_re = (num_re * lam_re + ab_im * lam_im) / den
    coef_im = (ab_im * lam_re - num_re * lam_im) / den
    b_re = b_re.astype(jnp.float32)
    b_im = b_im.astype(jnp.float32)
    bb_re = coef_re[..., None] * b_re - coef_im[..., None] * b_im
    bb_im = coef_re[..., None] * b_im + coef_im[..., None] * b_re
    return ab_re, ab_im, bb_re, bb_im

def _complex_affine_combine(e1, e2):
    a1r, a1i, b1r, b1i = e1
    a2r, a2i, b2r, b2i = e2
    return (a2r * a1r - a2i * a1i,
            a2r * a1i + a2i * a1r,
            a2r * b1r - a2i * b1i + b2r,
            a2r * b1i + a2i * b1r + b2i)

def s5_scan(u, h0_re, h0_im, ab_re, ab_im, bb_re, bb_im, c_re, c_im):
    bsz, seq_len, _ = u.shape
    chunk = SSM_CHUNK if seq_len % SSM_CHUNK == 0 else seq_len
    n_chunks = seq_len // chunk
    ug = u.astype(jnp.float32).reshape(bsz, n_chunks, chunk, SSM_GROUPS, SSM_GROUP).transpose(1, 0, 2, 3, 4)
    a_re = jnp.broadcast_to(ab_re, (bsz, chunk) + ab_re.shape)
    a_im = jnp.broadcast_to(ab_im, (bsz, chunk) + ab_im.shape)

    def step(carry, u_blk):
        hr, hi = carry
        bu_r = jnp.einsum('bcgi,gpi->bcgp', u_blk, bb_re)
        bu_i = jnp.einsum('bcgi,gpi->bcgp', u_blk, bb_im)
        bu_r = bu_r.at[:, 0].add(ab_re * hr - ab_im * hi)
        bu_i = bu_i.at[:, 0].add(ab_re * hi + ab_im * hr)
        _, _, sr, si = lax.associative_scan(_complex_affine_combine, (a_re, a_im, bu_r, bu_i), axis=1)
        y = jnp.einsum('bcgp,gip->bcgi', sr, c_re) - jnp.einsum('bcgp,gip->bcgi', si, c_im)
        return (sr[:, -1], si[:, -1]), y

    (hr, hi), ys = lax.scan(step, (h0_re.astype(jnp.float32), h0_im.astype(jnp.float32)), ug)
    y = ys.transpose(1, 0, 2, 3, 4).reshape(bsz, seq_len, SSM_WIDTH)
    return y, hr, hi

def ssm_layer(x, h0_re, h0_im, norm_pre, w_in, lam_re, lam_im, log_dt, b_re, b_im,
              c_re, c_im, d_skip, w_glu, b_glu, w_out, norm_post):
    h = rms_norm(x, norm_pre)
    u, z = jnp.split(h @ w_in, 2, axis=-1)
    ab_re, ab_im, bb_re, bb_im = s5_discretize(lam_re, lam_im, log_dt, b_re, b_im)
    y, hr, hi = s5_scan(u, h0_re, h0_im, ab_re, ab_im, bb_re, bb_im,
                        c_re.astype(jnp.float32), c_im.astype(jnp.float32))
    y = (y + d_skip.astype(jnp.float32) * u.astype(jnp.float32)).astype(x.dtype)
    ga, gb = jnp.split(jax.nn.gelu(y) @ w_glu + b_glu, 2, axis=-1)
    y = ga * jax.nn.sigmoid(gb) * jax.nn.silu(z)
    out = y @ w_out
    return x + rms_norm(out, norm_post), hr, hi

def shared_kv(x, kv_norm, w_kv):
    bsz, seq_len, _ = x.shape
    kv = rms_norm(x, kv_norm) @ w_kv
    return kv.reshape(bsz, seq_len, 2, N_HEADS, HEAD_DIM)

def dilated_prompt_attn(q, slopes, n_strides, dilation, k, v):
    bsz, seq_len, nh, dh = q.shape
    n = seq_len // dilation
    qb_len = n_strides
    nb = -(-n // qb_len)
    n_pad = nb * qb_len
    rb = bsz * dilation

    def to_res(a):
        return a.reshape(bsz, n, dilation, nh, dh).transpose(0, 2, 1, 3, 4).reshape(rb, n, nh, dh).astype(jnp.float32)

    qr = jnp.pad(to_res(q), ((0, 0), (0, n_pad - n), (0, 0), (0, 0)))
    kr = jnp.pad(to_res(k), ((0, 0), (qb_len, n_pad - n), (0, 0), (0, 0)))
    vr = jnp.pad(to_res(v), ((0, 0), (qb_len, n_pad - n), (0, 0), (0, 0)))
    qb = qr.reshape(rb, nb, qb_len, nh, dh)

    def band(a):
        return jnp.concatenate([a[:, :n_pad].reshape(rb, nb, qb_len, nh, dh),
                                a[:, qb_len:].reshape(rb, nb, qb_len, nh, dh)], axis=2)

    kb, vb = band(kr), band(vr)
    scores = jnp.einsum('nbqhd,nbkhd->nbhqk', qb, kb) * (1.0 / math.sqrt(dh))
    qi = jnp.arange(qb_len)[:, None]
    kj = jnp.arange(2 * qb_len)[None, :]
    dist = qi + qb_len - kj
    key_idx = jnp.arange(nb)[:, None, None] * qb_len - qb_len + kj[None]
    mask = (dist >= 0) & (dist <= n_strides) & (key_idx >= 0)
    bias = -slopes.astype(jnp.float32)[:, None, None] * (dist * dilation).astype(jnp.float32)
    scores = jnp.where(mask[None, :, None], scores + bias[None, None], NEG_INF)
    lse = jax.nn.logsumexp(scores, axis=-1)
    p = jnp.exp(scores - lse[..., None])
    o = jnp.einsum('nbhqk,nbkhd->nbqhd', p, vb).reshape(rb, n_pad, nh, dh)[:, :n]
    o = o.reshape(bsz, dilation, n, nh, dh).transpose(0, 2, 1, 3, 4).reshape(bsz, seq_len, nh, dh)
    lse = lse.transpose(0, 1, 3, 2).reshape(rb, n_pad, nh)[:, :n]
    lse = lse.reshape(bsz, dilation, n, nh).transpose(0, 2, 1, 3).reshape(bsz, seq_len, nh)
    return o, lse

def dilated_sample_attn(q, slopes, n_strides, dilation, k_all, v_all, n_buf):
    _, t_new, _, dh = q.shape
    j = jnp.arange(n_strides + 1)
    rows = n_buf + jnp.arange(t_new)[:, None] - j[None, :] * dilation
    valid = rows >= 0
    rows_c = jnp.maximum(rows, 0)
    kg = k_all[:, rows_c].astype(jnp.float32)
    vg = v_all[:, rows_c].astype(jnp.float32)
    scores = jnp.einsum('bthd,btjhd->bhtj', q.astype(jnp.float32), kg) * (1.0 / math.sqrt(dh))
    scores = scores - slopes.astype(jnp.float32)[:, None, None] * (j * dilation).astype(jnp.float32)[None, None, :]
    scores = jnp.where(valid[None, None], scores, NEG_INF)
    lse = jax.nn.logsumexp(scores, axis=-1)
    p = jnp.exp(scores - lse[..., None])
    o = jnp.einsum('bhtj,btjhd->bthd', p, vg)
    return o, lse.transpose(0, 2, 1)

def dilated_mixer_layer(x, attn_fn, norm_pre, w_in, w_out, norm_post):
    bsz, seq_len, _ = x.shape
    h = rms_norm(x, norm_pre)
    proj = h @ w_in
    q = proj[..., :N_GROUPS * ATTN_WIDTH].reshape(bsz, seq_len, N_GROUPS, N_HEADS, HEAD_DIM)
    z = proj[..., N_GROUPS * ATTN_WIDTH:]
    slopes = alibi_slopes()
    outs, lses = [], []
    for g, (window, dilation) in enumerate(DILATION_GROUPS):
        o, lse = attn_fn(q[:, :, g], slopes[g], window // dilation, dilation)
        outs.append(o)
        lses.append(lse)
    wgt = jax.nn.softmax(jnp.stack(lses), axis=0)
    o = jnp.einsum('gblh,gblhd->blhd', wgt, jnp.stack(outs))
    o = o.reshape(bsz, seq_len, ATTN_WIDTH).astype(x.dtype) * jax.nn.silu(z)
    return x + rms_norm(o @ w_out, norm_post)

def trunk(x, h0_re, h0_im, kv_past, a_norm_pre, a_w_in, a_lam_re, a_lam_im, a_log_dt,
          a_b_re, a_b_im, a_c_re, a_c_im, a_d, a_w_glu, a_b_glu, a_w_out, a_norm_post,
          kv_norm, w_kv, b_norm_pre, b_w_in, b_w_out, b_norm_post):
    new_re, new_im = [], []
    attn_fn, kv_state = None, None
    for layer in range(DEPTH):
        if layer < N_A_LAYERS:
            x, hr, hi = ssm_layer(x, h0_re[layer], h0_im[layer], a_norm_pre[layer], a_w_in[layer],
                                  a_lam_re[layer], a_lam_im[layer], a_log_dt[layer], a_b_re[layer],
                                  a_b_im[layer], a_c_re[layer], a_c_im[layer], a_d[layer],
                                  a_w_glu[layer], a_b_glu[layer], a_w_out[layer], a_norm_post[layer])
            new_re.append(hr.astype(h0_re.dtype))
            new_im.append(hi.astype(h0_im.dtype))
            continue
        if layer == N_A_LAYERS:
            kv = shared_kv(x, kv_norm, w_kv)
            if kv_past is None:
                seq_len = x.shape[1]
                n_keep = min(MAX_WINDOW, seq_len)
                attn_fn = functools.partial(dilated_prompt_attn, k=kv[:, :, 0], v=kv[:, :, 1])
                kv_state = kv[:, seq_len - n_keep:]
            else:
                n_buf = kv_past.shape[1]
                kv_all = jnp.concatenate([kv_past.astype(kv.dtype), kv], axis=1)
                attn_fn = functools.partial(dilated_sample_attn, k_all=kv_all[:, :, 0],
                                            v_all=kv_all[:, :, 1], n_buf=n_buf)
                kv_state = kv_all[:, kv_all.shape[1] - n_buf:]
        lb = layer - N_A_LAYERS
        x = dilated_mixer_layer(x, attn_fn, b_norm_pre[lb], b_w_in[lb], b_w_out[lb], b_norm_post[lb])
    return x, jnp.stack(new_re), jnp.stack(new_im), kv_state

def setup_inputs(seed: int = 0) -> dict:
    key = jax.random.key(seed)
    ks = jax.random.split(key, 32)
    f32 = jnp.float32
    n_buf = min(MAX_WINDOW, PAST_LEN)
    nrm = lambda k, shape, s: jax.random.normal(k, shape, f32) * s
    lam_im = math.pi * jnp.arange(SSM_STATE, dtype=f32)
    return {
        'x_prompt': nrm(ks[0], (BATCH, SEQ, D_MODEL), 1.0),
        'x_sample': nrm(ks[1], (DEC_BATCH, DEC_SEQ, D_MODEL), 1.0),
        'state_s5_re': nrm(ks[2], (N_A_LAYERS, DEC_BATCH, SSM_GROUPS, SSM_STATE), 0.5),
        'state_s5_im': nrm(ks[3], (N_A_LAYERS, DEC_BATCH, SSM_GROUPS, SSM_STATE), 0.5),
        'cache_kv': nrm(ks[4], (DEC_BATCH, n_buf, 2, N_HEADS, HEAD_DIM), 1.0),
        'a_norm_pre': 1.0 + nrm(ks[5], (N_A_LAYERS, D_MODEL), 0.05),
        'a_w_in': nrm(ks[6], (N_A_LAYERS, D_MODEL, 2 * SSM_WIDTH), D_MODEL ** -0.5),
        'a_lam_re': -0.5 + nrm(ks[7], (N_A_LAYERS, SSM_GROUPS, SSM_STATE), 0.01),
        'a_lam_im': lam_im + nrm(ks[8], (N_A_LAYERS, SSM_GROUPS, SSM_STATE), 0.01),
        'a_log_dt': jax.random.uniform(ks[9], (N_A_LAYERS, SSM_GROUPS), f32, math.log(DT_MIN), math.log(DT_MAX)),
        'a_b_re': nrm(ks[10], (N_A_LAYERS, SSM_GROUPS, SSM_STATE, SSM_GROUP), (2 * SSM_GROUP) ** -0.5),
        'a_b_im': nrm(ks[11], (N_A_LAYERS, SSM_GROUPS, SSM_STATE, SSM_GROUP), (2 * SSM_GROUP) ** -0.5),
        'a_c_re': nrm(ks[12], (N_A_LAYERS, SSM_GROUPS, SSM_GROUP, SSM_STATE), SSM_STATE ** -0.5),
        'a_c_im': nrm(ks[13], (N_A_LAYERS, SSM_GROUPS, SSM_GROUP, SSM_STATE), SSM_STATE ** -0.5),
        'a_d': nrm(ks[14], (N_A_LAYERS, SSM_WIDTH), 1.0),
        'a_w_glu': nrm(ks[15], (N_A_LAYERS, SSM_WIDTH, 2 * SSM_WIDTH), SSM_WIDTH ** -0.5),
        'a_b_glu': nrm(ks[16], (N_A_LAYERS, 2 * SSM_WIDTH), 0.01),
        'a_w_out': nrm(ks[17], (N_A_LAYERS, SSM_WIDTH, D_MODEL), SSM_WIDTH ** -0.5),
        'a_norm_post': 1.0 + nrm(ks[18], (N_A_LAYERS, D_MODEL), 0.05),
        'kv_norm': 1.0 + nrm(ks[19], (D_MODEL,), 0.05),
        'w_kv': nrm(ks[20], (D_MODEL, 2 * ATTN_WIDTH), D_MODEL ** -0.5),
        'b_norm_pre': 1.0 + nrm(ks[21], (N_B_LAYERS, D_MODEL), 0.05),
        'b_w_in': nrm(ks[22], (N_B_LAYERS, D_MODEL, (N_GROUPS + 1) * ATTN_WIDTH), D_MODEL ** -0.5),
        'b_w_out': nrm(ks[23], (N_B_LAYERS, ATTN_WIDTH, D_MODEL), ATTN_WIDTH ** -0.5),
        'b_norm_post': 1.0 + nrm(ks[24], (N_B_LAYERS, D_MODEL), 0.05),
    }

def reference(x_prompt, x_sample, state_s5_re, state_s5_im, cache_kv, a_norm_pre, a_w_in,
              a_lam_re, a_lam_im, a_log_dt, a_b_re, a_b_im, a_c_re, a_c_im, a_d, a_w_glu,
              a_b_glu, a_w_out, a_norm_post, kv_norm, w_kv, b_norm_pre, b_w_in, b_w_out,
              b_norm_post):
    h0 = jnp.zeros((N_A_LAYERS, x_prompt.shape[0], SSM_GROUPS, SSM_STATE), x_prompt.dtype)
    y_prompt, p_re, p_im, p_kv = trunk(
        x_prompt, h0, h0, None, a_norm_pre, a_w_in, a_lam_re, a_lam_im, a_log_dt,
        a_b_re, a_b_im, a_c_re, a_c_im, a_d, a_w_glu, a_b_glu, a_w_out, a_norm_post,
        kv_norm, w_kv, b_norm_pre, b_w_in, b_w_out, b_norm_post)
    y_sample, s_re, s_im, s_kv = trunk(
        x_sample, state_s5_re, state_s5_im, cache_kv, a_norm_pre, a_w_in, a_lam_re, a_lam_im,
        a_log_dt, a_b_re, a_b_im, a_c_re, a_c_im, a_d, a_w_glu, a_b_glu, a_w_out, a_norm_post,
        kv_norm, w_kv, b_norm_pre, b_w_in, b_w_out, b_norm_post)
    return (y_prompt, y_sample, p_re, p_im, p_kv, s_re, s_im, s_kv)


_drawn_inputs = setup_inputs


def setup_inputs(seed=0):
    import zlib

    import numpy as np

    out = dict(_drawn_inputs(seed))
    spreads = {}
    factors = {'a_lam_re': 3.764, 'a_b_glu': 3.905}
    for name, (base, spread) in spreads.items():
        noise = np.random.default_rng([zlib.crc32(name.encode()), seed]).standard_normal(out[name].shape)
        drawn = base * np.exp(spread * noise) if base else spread * noise
        out[name] = __import__('jax').numpy.asarray(drawn.astype(out[name].dtype))
    for name, factor in factors.items():
        out[name] = (out[name] * factor).astype(out[name].dtype)
    return out
```

```python
import math
from contextlib import ExitStack

import concourse.bass as bass
from concourse import mybir

F32 = mybir.dt.float32
F32R = mybir.dt.float32r
ALU = mybir.AluOpType
ACT = mybir.ActivationFunctionType
AX_X = mybir.AxisListType.X

P = 128
D = 1024
DT = D // P
W2 = 2048
WT = W2 // P
SEQ = 512
NS = 8
TOK = SEQ + NS
CUTS = ((0, 256), (256, TOK))
G = 128
NP = G // 2
CH = 16
ST = 64
L = 8
NC = SEQ // L
EPS = 1e-6

C_FIRST = NC + 1
C_LAST = C_FIRST + NS
YC = C_FIRST + NS
UC = C_LAST + NS

V_APRE, V_APOST, V_KV, V_BPRE, V_BPOST, V_D, V_BGLU = 0, 8, 16, 24, 32, 40, 56
NVEC = 88

N_HEADS = 16
HD = 64
SLOPE = [[2.0 ** (-8.0 * (g * N_HEADS + h + 1) / 48) for h in range(N_HEADS)] for g in range(3)]


class Memory:

    def __init__(self, nc):
        self.nc = nc
        self.base = (nc.sbuf_base + 63) // 64 * 64
        self.end = nc.sbuf_usable_end

    def at(self, name, shape, offset, dtype=F32):
        size = 4
        for n in shape[1:]:
            size *= n
        size = (size + 31) // 32 * 32
        assert self.base + offset + size <= self.end, (name, offset, size, self.end - self.base)
        return self.nc.alloc_sbuf_tensor_at(name, shape, dtype, offset=self.base + offset), offset + size


class Dense:

    def __init__(self, ctx, nc, mem, name, units):
        def sem(x):
            return nc.alloc_semaphore(f"{name}_{x}")

        self.nc = nc
        self.mem = mem
        self.units = units
        self.landed = [sem("weights_landed0"), sem("weights_landed1")]
        self.hi_ready = sem("hi_ready")
        self.lo_ready = sem("lo_ready")
        self.unit_read = sem("unit_read")
        self.acc_free = [sem("acc_free0"), sem("acc_free1")]

    def load(self, sp, n, s, block):
        sp.wait_ge(self.lo_ready, n + 1)
        sp.dma_start(self.mem.raw[s][:, :, :], block).then_inc(self.landed[s], 16)

    def split_hi(self, act, n, s, turn):
        act.wait_ge(self.landed[s], 16 * (turn + 1))
        act.wait_ge(self.unit_read, n + 1)
        act.activation(self.mem.wh[s][:, :, :], self.mem.raw[s][:, :, :], ACT.Copy).then_inc(self.hi_ready, 1)

    def split_lo(self, pool, n, s):
        pool.wait_ge(self.hi_ready, n + 1)
        pool.tensor_tensor(self.mem.wl[s][:, :, :], self.mem.raw[s][:, :, :],
                           self.mem.wh[s][:, :, :].bitcast(F32), ALU.subtract).then_inc(self.lo_ready, 1)

    def start(self, pe):
        pe.sem_inc(self.unit_read, 2)
        for a in range(2):
            pe.sem_inc(self.acc_free[a], 1)

    def start_raw(self, pool):
        pool.sem_inc(self.lo_ready, 2)

    def wait_tile(self, eng, t):
        eng.wait_ge(self.unit_read, (t + 1) * self.units + 2)

    def multiply(self, pe, n, s, a, xh, xl, k0, first, last):
        nc, mem = self.nc, self.mem
        pe.wait_ge(self.lo_ready, n + 3)
        for k in range(8):
            terms = ((mem.wh, xh), (mem.wh, xl), (mem.wl, xh))
            for i, (w, x) in enumerate(terms):
                for lo, hi in CUTS:
                    ins = nc.tensor.matmul(
                        mem.acc[a][:, 256 + lo:256 + hi], w[s][:, k, :], x[:, k0 + k, lo:hi],
                        start=first and k == 0 and i == 0, stop=last and k == 7 and i == 2)
        ins.then_inc(self.unit_read, 1)

    def tile(self, pe, t, a, turn, xh, xl):
        pe.wait_ge(self.acc_free[a], turn + 1)
        for u in range(self.units):
            slot = u if self.units == 2 else a
            self.multiply(pe, self.units * t + u, slot, a, xh, xl, 8 * u, u == 0, u == self.units - 1)


def columns(acc):
    return acc[:, 256:256 + TOK]


def blocks(w):
    return w.rearrange("(k p) m -> p k m", p=P)


def cols(i, n=P):
    return bass.ds(i * n, n)


def paired(eng, start, end, body):
    if start % 2:
        body(start, 1, start // 2)
        start += 1
    if end - start >= 4:
        with eng.Fori(start // 2, end // 2) as h:
            body(2 * h, 0, h)
            body(2 * h + 1, 1, h)
    else:
        for i in range(start, end // 2 * 2):
            body(i, i % 2, i // 2)
    if end % 2:
        body(end - 1, 0, end // 2)


def plan(nc):
    mem = Memory(nc)
    o = 0
    mem.ident, o = mem.at("ident", [P, P], o)
    mem.ones, o = mem.at("ones", [P, P], o)
    mem.vec, o = mem.at("vec", [P, NVEC], o)
    mem.cst, o = mem.at("cst", [P, 8], o)
    o = 2048
    mem.xT, o = mem.at("xT", [P, DT, TOK], o)
    mem.acth_at = o
    mem.acth, o = mem.at("act_hi", [P, WT, TOK], o, F32R)
    mem.actl_at = o
    mem.actl, o = mem.at("act_lo", [P, WT, TOK], o, F32R)
    mem.ring_at = o
    mem.raw, mem.wh, mem.wl = [], [], []
    for s in range(2):
        t, o = mem.at(f"raw{s}", [P, 8, P], o)
        mem.raw.append(t)
    for s in range(2):
        t, o = mem.at(f"w_hi{s}", [P, 8, P], o, F32R)
        mem.wh.append(t)
        t, o = mem.at(f"w_lo{s}", [P, 8, P], o, F32R)
        mem.wl.append(t)
    mem.rest = o
    return mem


def setup(nc, mem, ten, dram):
    R = mem.rest
    mem.XH, o = mem.at("XH", [P, C_LAST, 2, NP], R)
    mem.Ct, o = mem.at("Ct", [P, 2, NP, CH], o)
    mem.apow, o = mem.at("apow", [P, L + 1, 2, NP], o)
    mem.p3_at = o
    mem.Bt, o = mem.at("Bt", [P, 2, NP, CH], o)
    mem.cb, o = mem.at("cb", [P, L, 2, NP], o)
    mem.Xs, o = mem.at("Xs", [P, NS, 2, NP], o)
    mem.Ksb, o = mem.at("Ksb", [P, G, CH], o)
    mem.p1_at = o
    a = mem.acth_at
    xtok, a = mem.at("xtok", [P, SEQ // P, D], a)
    xsam, a = mem.at("xsam", [NS, D], a)
    crow, a = mem.at("crow", [P, 2, 8, P], a)
    h0row, a = mem.at("h0row", [NP, 2, NS, P], a)
    vrow, a = mem.at("vrow", [NVEC, P], a)
    lam, a = mem.at("lam", [NP, 2, P], a)
    ldt, a = mem.at("ldt", [NP, 2], a)
    dtr, a = mem.at("dtr", [NP, 2], a)
    lrow, a = mem.at("lrow", [NP, 4, P], a)
    ls, a = mem.at("ls", [P, 4, NP], a)
    w, a = mem.at("disc", [P, 16, NP], a)
    tm, a = mem.at("powtmp", [P, 4, 4, NP], a)
    acc = mem.acc

    with ExitStack() as ctx:
        def sem(x):
            return nc.alloc_semaphore(f"setup_{x}")

        x_in, v_in, c_in, h_in, l_in, b_in = (sem(x) for x in ("x_in", "vec_in", "c_in", "h0_in", "lam_in", "b_in"))
        masks = sem("masks")
        full, free = sem("transposed"), sem("moved")
        rows = sem("rows")
        dve = sem("dve_chain")
        a_in, a_out = sem("act_ask"), sem("act_done")
        block = ctx.enter_context(nc.Block())

        @block.sync
        def _(sp):
            xp = ten["x_prompt"][0, :, :].rearrange("(c j) d -> j c d", j=L)
            for j in range(L):
                sp.dma_start(xtok[64 * (j % 2):64 * (j % 2) + 64, j // 2, :], xp[j]).then_inc(x_in, 16)
            sp.dma_start(xsam[:, :], ten["x_sample"][:, 0, :]).then_inc(x_in, 16)
            for ri, name in enumerate(("a_lam_re", "a_lam_im")):
                sp.dma_start(lam[:, ri, :], ten[name][0, :, :].rearrange("(c e) p -> c (e p)", e=2)).then_inc(l_in, 16)
            sp.dma_start(ldt[:, :], ten["a_log_dt"][0, :].rearrange("(c e) -> c e", e=2)).then_inc(l_in, 16)
            at = 0
            for name in ("a_norm_pre", "a_norm_post", "kv_norm", "b_norm_pre", "b_norm_post", "a_d", "a_b_glu"):
                v = ten[name] if name == "kv_norm" else ten[name][0, :]
                n = v.shape[0] // P
                sp.dma_start(vrow[at:at + n, :], v.rearrange("(f p) -> f p", p=P)).then_inc(v_in, 16)
                at += n
            for ri, name in enumerate(("state_s5_re", "state_s5_im")):
                sp.dma_start(h0row[:, ri, :, :], ten[name][0, :, :, :].rearrange("s (c e) p -> c s (e p)", e=2)).then_inc(h_in, 16)

        @block.gpsimd
        def _(pool):
            pool.memset(mem.ident[:, :], 0.0).then_inc(masks, 1)
            pool.memset(mem.ones[:, :], 1.0)
            pool.memset(mem.cst[:, :], EPS)
            pool.memset(mem.XH[:, 0, :, :], 0.0).then_inc(masks, 1)
            pool.wait_ge(masks, 2)
            pool.affine_select(out=mem.ident[:, :], in_=mem.ident[:, :], compare_op=ALU.not_equal, fill=1.0,
                               base=0, pattern=[[-1, P]], channel_multiplier=1).then_inc(masks, 1)
            for ri, name in enumerate(("a_c_re", "a_c_im")):
                c = ten[name][0, :, :, :].rearrange("(c e) o p -> e c o p", e=2)
                for t in range(8):
                    for e in range(2):
                        pool.dma_start(crow[:, ri, t, 64 * e:64 * e + 64], c[e, 8 * t:8 * t + 8, :, :]).then_inc(c_in, 16)
            for ri, name in enumerate(("a_b_re", "a_b_im")):
                b = ten[name][0, :, :, :].rearrange("(c e) p i -> e p c i", e=2)
                for e in range(2):
                    pool.dma_start(mem.Bt[64 * e:64 * e + 64, ri, :, :], b[e]).then_inc(b_in, 16)
            pool.wait_ge(b_in, 64)

        @block.tensor
        def _(pe):
            pe.wait_ge(masks, 3)
            pe.wait_ge(x_in, 16 * 9)
            for f in range(DT):
                if f >= 2:
                    pe.wait_ge(free, f - 1)
                for b in range(4):
                    nc.tensor.transpose(acc[f % 2][:, P * b:P * b + P], xtok[:, b, P * f:P * f + P], mem.ident[:, :])
                nc.tensor.transpose(acc[f % 2][:, SEQ:SEQ + NS], xsam[:, P * f:P * f + P],
                                    mem.ident[0:NS, 0:NS]).then_inc(full, 1)
            pe.wait_ge(v_in, 16 * 7)
            pe.wait_ge(rows, 1)
            pe.wait_ge(free, 7)
            nc.tensor.transpose(acc[0][:, 0:NVEC], vrow[:, :], mem.ident[0:NVEC, 0:NVEC])
            for q in range(4):
                ins = nc.tensor.transpose(acc[0][:, 512 + NP * q:512 + NP * q + NP], lrow[:, q, :], mem.ident[0:NP, 0:NP])
            ins.then_inc(full, 1)
            pe.wait_ge(c_in, 16 * 32)
            for ri in range(2):
                pe.wait_ge(free, 8 + ri)
                for t in range(8):
                    ins = nc.tensor.transpose(acc[1 - ri][:, P * t:P * t + P], crow[:, ri, t, :], mem.ident[:, :])
                ins.then_inc(full, 1)
            pe.wait_ge(h_in, 32)
            pe.wait_ge(free, 10)
            for ri in range(2):
                for s in range(NS):
                    q = ri * NS + s
                    ins = nc.tensor.transpose(acc[1][:, NP * q:NP * q + NP], h0row[:, ri, s, :], mem.ident[0:NP, 0:NP])
            ins.then_inc(full, 1)

        @block.scalar
        def _(act):
            act.wait_ge(l_in, 48)
            act.activation(dtr[:, :], ldt[:, :], ACT.Exp).then_inc(a_out, 1)
            act.wait_ge(a_in, 1)
            act.activation(w[:, 0, :], ls[:, 0, :], ACT.Exp).then_inc(a_out, 1)
            act.wait_ge(a_in, 2)
            act.activation(w[:, 5:7, :], w[:, 3:5, :], ACT.Sin).then_inc(a_out, 1)

        @block.vector
        def _(v):
            count = [0]

            def link(ins):
                count[0] += 1
                ins.then_inc(dve, 1)
                v.wait_ge(dve, count[0])

            v.wait_ge(a_out, 1)
            dtb = dtr[:, :].unsqueeze(2).broadcast_to([NP, 2, ST])
            for q in range(2):
                v.tensor_tensor(lrow[:, q, :].rearrange("c (e p) -> c e p", e=2),
                                lam[:, q, :].rearrange("c (e p) -> c e p", e=2), dtb, ALU.mult)
            v.tensor_copy(lrow[:, 2:4, :], lam[:, :, :]).then_inc(rows, 1)
            for f in range(DT):
                v.wait_ge(full, f + 1)
                v.tensor_copy(mem.xT[:, f, :], acc[f % 2][:, 0:TOK]).then_inc(free, 1)
            v.wait_ge(full, 9)
            v.tensor_copy(mem.vec[:, :], acc[0][:, 0:NVEC])
            link(v.tensor_copy(ls[:, :, :], acc[0][:, 512:768].rearrange("p (q c) -> p q c", q=4)))
            v.sem_inc(free, 1)
            v.sem_inc(a_in, 1)
            for ri in range(2):
                v.wait_ge(full, 10 + ri)
                v.tensor_copy(mem.Ct[:, ri, :, :], acc[1 - ri][:, :].rearrange("p (c o) -> p c o", o=CH)).then_inc(free, 1)
            v.wait_ge(full, 12)
            for ri in range(2):
                v.tensor_copy(mem.XH[:, C_FIRST:C_LAST, ri, :],
                              acc[1][:, 512 * ri:512 * ri + 512].rearrange("p (s c) -> p s c", s=NS))
            magic = 1.5 * 2.0 ** 23
            parts = (6.28125, 0.0019340515136718750, 2 * math.pi - 6.28125 - 0.0019340515136718750)
            link(v.tensor_scalar(w[:, 1, :], ls[:, 1, :], 1.0 / (2 * math.pi), magic, ALU.mult, ALU.add))
            link(v.tensor_scalar(w[:, 1, :], w[:, 1, :], -magic, None, ALU.add))
            link(v.scalar_tensor_tensor(w[:, 2, :], w[:, 1, :], -parts[0], ls[:, 1, :], ALU.mult, ALU.add))
            link(v.scalar_tensor_tensor(w[:, 2, :], w[:, 1, :], -parts[1], w[:, 2, :], ALU.mult, ALU.add))
            link(v.scalar_tensor_tensor(w[:, 2, :], w[:, 1, :], -parts[2], w[:, 2, :], ALU.mult, ALU.add))
            top = 3.1415925
            link(v.tensor_scalar(w[:, 3, :], w[:, 2, :], top, -top, ALU.min, ALU.max))
            link(v.tensor_scalar(w[:, 7, :], w[:, 3, :], -1.0, None, ALU.mult))
            link(v.tensor_tensor(w[:, 7, :], w[:, 7, :], w[:, 3, :], ALU.max))
            link(v.tensor_scalar(w[:, 4, :], w[:, 7, :], -1.0, math.pi / 2, ALU.mult, ALU.add))
            v.sem_inc(a_in, 1)
            v.memset(mem.apow[:, 0, 0, :], 1.0)
            link(v.memset(mem.apow[:, 0, 1, :], 0.0))
            v.wait_ge(a_out, 3)
            v.tensor_tensor(mem.apow[:, 1, 0, :], w[:, 0, :], w[:, 6, :], ALU.mult)
            link(v.tensor_tensor(mem.apow[:, 1, 1, :], w[:, 0, :], w[:, 5, :], ALU.mult))
            nr, ar, ai, lr, li = w[:, 8, :], mem.apow[:, 1, 0, :], mem.apow[:, 1, 1, :], ls[:, 2, :], ls[:, 3, :]
            v.tensor_scalar(nr, ar, -1.0, None, ALU.add)
            v.tensor_tensor(w[:, 9, :], lr, lr, ALU.mult)
            link(v.tensor_tensor(w[:, 10, :], li, li, ALU.mult))
            link(v.tensor_tensor(w[:, 9, :], w[:, 9, :], w[:, 10, :], ALU.add))
            v.reciprocal(w[:, 11, :], w[:, 9, :])
            v.tensor_tensor(w[:, 12, :], nr, lr, ALU.mult)
            v.tensor_tensor(w[:, 13, :], ai, li, ALU.mult)
            v.tensor_tensor(w[:, 14, :], ai, lr, ALU.mult)
            link(v.tensor_tensor(w[:, 15, :], nr, li, ALU.mult))
            v.tensor_tensor(w[:, 12, :], w[:, 12, :], w[:, 13, :], ALU.add)
            link(v.tensor_tensor(w[:, 14, :], w[:, 14, :], w[:, 15, :], ALU.subtract))
            cr, ci = w[:, 1, :], w[:, 2, :]
            v.tensor_tensor(cr, w[:, 12, :], w[:, 11, :], ALU.mult)
            link(v.tensor_tensor(ci, w[:, 14, :], w[:, 11, :], ALU.mult))
            for n in (1, 2, 4):
                ar, ai = mem.apow[:, 1:n + 1, 0, :], mem.apow[:, 1:n + 1, 1, :]
                br = mem.apow[:, n, 0, :].unsqueeze(1).broadcast_to([P, n, NP])
                bi = mem.apow[:, n, 1, :].unsqueeze(1).broadcast_to([P, n, NP])
                v.tensor_tensor(tm[:, 0, 0:n, :], ar, br, ALU.mult)
                v.tensor_tensor(tm[:, 1, 0:n, :], ai, bi, ALU.mult)
                v.tensor_tensor(tm[:, 2, 0:n, :], ar, bi, ALU.mult)
                link(v.tensor_tensor(tm[:, 3, 0:n, :], ai, br, ALU.mult))
                v.tensor_tensor(mem.apow[:, n + 1:2 * n + 1, 0, :], tm[:, 0, 0:n, :], tm[:, 1, 0:n, :], ALU.subtract)
                link(v.tensor_tensor(mem.apow[:, n + 1:2 * n + 1, 1, :], tm[:, 2, 0:n, :], tm[:, 3, 0:n, :], ALU.add))
            for j in range(L):
                ar, ai = mem.apow[:, L - 1 - j, 0, :], mem.apow[:, L - 1 - j, 1, :]
                v.tensor_tensor(tm[:, 0, 0, :], ar, cr, ALU.mult)
                v.tensor_tensor(tm[:, 1, 0, :], ai, ci, ALU.mult)
                v.tensor_tensor(tm[:, 2, 0, :], ar, ci, ALU.mult)
                link(v.tensor_tensor(tm[:, 3, 0, :], ai, cr, ALU.mult))
                v.tensor_tensor(mem.cb[:, j, 0, :], tm[:, 0, 0, :], tm[:, 1, 0, :], ALU.subtract)
                link(v.tensor_tensor(mem.cb[:, j, 1, :], tm[:, 2, 0, :], tm[:, 3, 0, :], ALU.add))


class Norm:

    def __init__(self, ctx, nc, mem, name, at):
        def sem(x):
            return nc.alloc_semaphore(f"{name}_{x}")

        self.nc, self.mem, self.name = nc, mem, name
        self.sq = []
        self.tmp = []
        for s in range(2):
            t, at = mem.at(f"{name}_sq{s}", [P, TOK], at)
            self.sq.append(t)
        for s in range(2):
            t, at = mem.at(f"{name}_tmp{s}", [P, TOK], at)
            self.tmp.append(t)
        self.root, at = mem.at(f"{name}_root", [P, TOK], at)
        self.rstd, at = mem.at(f"{name}_rstd", [P, TOK], at)
        self.end = at
        self.squared, self.summed = sem("squared"), sem("summed")
        self.rooted, self.rstd_ready = sem("rooted"), sem("rstd_ready")
        self.scaled, self.act_hi, self.act_lo = sem("scaled"), sem("act_hi"), sem("act_lo")

    def square(self, act, f, x):
        if f >= 2:
            act.wait_ge(self.summed, f - 1)
        act.activation(self.sq[f % 2][:, :], x, ACT.Square).then_inc(self.squared, 1)

    def add(self, pe, f):
        pe.wait_ge(self.squared, f + 1)
        for h, (lo, hi) in enumerate(CUTS):
            ins = self.nc.tensor.matmul(self.mem.aux[h][:, 0:hi - lo], self.mem.ones[:, :],
                                        self.sq[f % 2][:, lo:hi], start=f == 0, stop=f == DT - 1)
        ins.then_inc(self.summed, 1)

    def take_root(self, act):
        act.wait_ge(self.summed, DT)
        for h, (lo, hi) in enumerate(CUTS):
            ins = act.activation(self.root[:, lo:hi], self.mem.aux[h][:, 0:hi - lo], ACT.Sqrt,
                                 scale=1.0 / D, bias=self.mem.cst[:, 0:1])
        ins.then_inc(self.rooted, 1)

    def invert(self, v):
        v.wait_ge(self.rooted, 1)
        v.reciprocal(self.rstd[:, :], self.root[:, :]).then_inc(self.rstd_ready, 1)
        v.wait_ge(self.rstd_ready, 1)

    def apply(self, v, gains, first, n0=0):
        mem = self.mem

        def low(f):
            v.wait_ge(self.act_hi, n0 + f + 1)
            v.tensor_tensor(mem.actl[:, first + f, :], self.tmp[f % 2][:, :],
                            mem.acth[:, first + f, :].bitcast(F32), ALU.subtract).then_inc(self.act_lo, 1)

        for f in range(DT):
            if f >= 2:
                v.wait_ge(self.act_lo, n0 + f - 1)
            v.scalar_tensor_tensor(self.tmp[f % 2][:, :], mem.xT[:, f, :], mem.vec[:, gains + f:gains + f + 1],
                                   self.rstd[:, :], ALU.mult, ALU.mult).then_inc(self.scaled, 1)
            if f >= 1:
                low(f - 1)
        low(DT - 1)
        v.wait_ge(self.act_lo, n0 + DT)

    def apply_hi(self, act, first, n0=0):
        for f in range(DT):
            act.wait_ge(self.scaled, n0 + f + 1)
            act.activation(self.mem.acth[:, first + f, :], self.tmp[f % 2][:, :], ACT.Copy).then_inc(self.act_hi, 1)


NB = 8
BG = G // NB
BP = BG // 2


def states(nc, mem, ten, dram):
    U = []
    o = mem.p1_at
    for s in range(2):
        t, o = mem.at(f"Ux{s}", [P, BG, UC], o)
        U.append(t)
    tab, o = mem.at("b_tab", [P, BP, 2, P], o)
    tabT, o = mem.at("b_tabT", [P, BP, 2, P], o)
    a = mem.acth_at + DT * TOK * 4
    cbd, a = mem.at("c_blockdiag", [P, BP, 2, 2, CH], a)
    ust = []
    for s in range(2):
        t, a = mem.at(f"u_out{s}", [P, TOK], a)
        ust.append(t)
    t1, a = mem.at("tab_t1", [P, BP, L, CH], a)
    t2, a = mem.at("tab_t2", [P, BP, L, CH], a)
    assert a <= mem.actl_at
    aux = mem.aux
    su, w = dram["u"], blocks(ten["a_w_in"][0, :, :])
    su_p = su[:, 0:SEQ].rearrange("(g i) (j c) -> j i g c", i=CH, j=L)
    su_s = su[:, SEQ:TOK].rearrange("(g i) s -> i g s", i=CH)

    with ExitStack() as ctx:
        def sem(x):
            return nc.alloc_semaphore(f"states_{x}")

        dn = Dense(ctx, nc, mem, "u_proj", 1)
        nm = Norm(ctx, nc, mem, "norm_a", mem.actl_at + DT * TOK * 4)
        zeroed = sem("zeroed")
        u_copied, u_stored = sem("u_copied"), sem("u_stored")
        U_in = [sem("U_in0"), sem("U_in1")]
        tab_ready, mul_done = sem("tab_ready"), sem("mul_done")
        tr_full, tr_free = sem("tr_full"), sem("tr_free")
        k_full, k_free = sem("k_full"), sem("k_free")
        x_full, x_free = sem("x_full"), sem("x_free")
        block = ctx.enter_context(nc.Block())

        @block.sync
        def _(sp):
            def load(b):
                for i in range(2):
                    dn.load(sp, 2 * b + i, i, w[:, :, cols(2 * b + i)])

            def store_and_gather(b, s):
                for i in range(2):
                    sp.wait_ge(u_copied, 2 * b + i + 1)
                    sp.dma_start(su[cols(2 * b + i), :], ust[i][:, :]).then_inc(u_stored, 16)
                sp.wait_ge(u_stored, 32 * b + 64)
                sp.wait_ge(x_full, 4 * b + 4)
                for j in range(L):
                    sp.dma_start(U[s][CH * j:CH * j + CH, :, 0:NC], su_p[j, :, cols(b, BG), :]).then_inc(U_in[s], 16)
                sp.dma_start(U[s][0:CH, :, C_FIRST:C_LAST], su_s[:, cols(b, BG), :]).then_inc(U_in[s], 16)
                sp.dma_start(U[s][P - CH:P, :, C_LAST:UC], su_s[:, cols(b, BG), :]).then_inc(U_in[s], 16)

            sp.sem_inc(u_stored, 32)
            load(0)
            sp.wait_ge(zeroed, 2)

            def batch(b, q, h):
                load(b)
                store_and_gather(b - 1, 1 - q)
            paired(sp, 1, NB, batch)
            store_and_gather(NB - 1, 1)

        @block.gpsimd
        def _(pool):
            dn.start_raw(pool)
            for s in range(2):
                pool.memset(U[s][:, :, :], 0.0).then_inc(zeroed, 1)
            pool.memset(cbd[:, :, :, :, :], 0.0).then_inc(zeroed, 1)
            paired(pool, 0, WT, lambda n, q, h: dn.split_lo(pool, n, q))

        @block.scalar
        def _(act):
            for f in range(DT):
                nm.square(act, f, mem.xT[:, f, :])
            nm.take_root(act)
            nm.apply_hi(act, 0)
            for n in range(2):
                dn.split_hi(act, n, n, 0)

            def copy_u(m, i, b):
                dn.wait_tile(act, m)
                act.wait_ge(u_stored, 32 * b + 32)
                act.activation(ust[i][:, :], columns(mem.acc[i]), ACT.Copy).then_inc(u_copied, 1)
                act.wait_ge(u_copied, m + 1)
                act.sem_inc(dn.acc_free[i], 1)

            def copy_tab(b):
                for r in range(4):
                    act.wait_ge(tr_full, 4 * b + r + 1)
                    act.activation(tabT[:, 2 * r:2 * r + 2, :, :],
                                   aux[r % 2][:, :].rearrange("p (c z m) -> p c z m", c=2, z=2),
                                   ACT.Copy).then_inc(tr_free, 1)

            def batch(b, q, h):
                for i in range(2):
                    copy_u(2 * b - 2 + i, i, b - 1)
                    dn.split_hi(act, 2 * b + i, i, b)
                copy_tab(b - 1)
            paired(act, 1, NB, batch)
            for i in range(2):
                copy_u(WT - 2 + i, i, NB - 1)
            copy_tab(NB - 1)

        @block.vector
        def _(v):
            v.sem_inc(mul_done, 1)
            nm.invert(v)
            nm.apply(v, V_APRE, 0)
            v.wait_ge(zeroed, 3)

            def pairs(x, b):
                return x[:, cols(b, BP)]

            def build(b):
                def coef(z):
                    return mem.cb[:, :, z, cols(b, BP)].rearrange("p j c -> p c j").unsqueeze(3).broadcast_to([P, BP, L, CH])

                def inp(z):
                    return mem.Bt[:, z, cols(b, BP), :].unsqueeze(2).broadcast_to([P, BP, L, CH])

                for z in range(2):
                    v.wait_ge(mul_done, 6 * b + 3 * z + 1)
                    v.tensor_tensor(t1[:, :, :, :], coef(0), inp(z), ALU.mult).then_inc(mul_done, 1)
                    v.tensor_tensor(t2[:, :, :, :], coef(1), inp(1 - z), ALU.mult).then_inc(mul_done, 1)
                    v.wait_ge(mul_done, 6 * b + 3 * z + 3)
                    v.tensor_tensor(tab[:, :, z, :], t1[:, :, :, :].rearrange("p c j i -> p c (j i)"),
                                    t2[:, :, :, :].rearrange("p c j i -> p c (j i)"),
                                    ALU.subtract if z == 0 else ALU.add).then_inc(mul_done, 1)
                v.wait_ge(mul_done, 6 * b + 7)
                for e in range(2):
                    q = slice(64 * e, 64 * e + 64)
                    v.tensor_copy(cbd[q, :, 0, e, :], mem.Ct[q, 0, cols(b, BP), :])
                    ins = v.tensor_scalar(cbd[q, :, 1, e, :], mem.Ct[q, 1, cols(b, BP), :], -1.0, None, ALU.mult)
                ins.then_inc(tab_ready, 1)

            def copy_k(b):
                v.wait_ge(k_full, b + 1)
                v.tensor_copy(mem.Ksb[:, cols(b, BG), :], aux[2][:, 0:BG * CH].rearrange("p (g o) -> p g o", o=CH)).then_inc(k_free, 1)

            def copy_x(b):
                for r in range(4):
                    v.wait_ge(x_full, 4 * (b + 2) + r + 1)
                    x = aux[2 + r % 2][:, 0:4 * UC].rearrange("p (c z n) -> p c z n", c=2, z=2)
                    for z in range(2):
                        pair = bass.ds(b * BP + 2 * r, 2)
                        v.tensor_copy(mem.XH[:, 1:NC + 1, z, pair].rearrange("p n c -> p c n"), x[:, :, z, 0:NC])
                        ins = v.tensor_copy(mem.Xs[:, :, z, pair].rearrange("p n c -> p c n"), x[:, :, z, C_LAST:UC])
                    ins.then_inc(x_free, 1)

            build(0)
            copy_k(0)

            def batch(b, q, h):
                build(b)
                copy_x(b - 1)
                copy_k(b)
            paired(v, 1, NB, batch)
            copy_x(NB - 1)

        @block.tensor
        def _(pe):
            dn.start(pe)
            pe.sem_inc(x_full, 8)
            pe.sem_inc(x_free, 2)
            pe.sem_inc(tr_free, 2)
            for f in range(DT):
                nm.add(pe, f)
            pe.wait_ge(nm.act_lo, DT)

            def tables(b):
                pe.wait_ge(tab_ready, b + 1)
                for r in range(4):
                    pe.wait_ge(tr_free, 4 * b + r + 1)
                    for c in range(2):
                        for z in range(2):
                            ins = nc.tensor.transpose(aux[r % 2][:, 256 * c + P * z:256 * c + P * z + P],
                                                      tab[:, 2 * r + c, z, :], mem.ident[:, :])
                    ins.then_inc(tr_full, 1)
                pe.wait_ge(x_free, 4 * b + 2)
                for c in range(BP):
                    for z in range(2):
                        ins = nc.tensor.matmul(aux[2][:, 32 * c:32 * c + 32], tab[:, c, z, :],
                                               cbd[:, c, z, :, :].rearrange("p e o -> p (e o)"), start=z == 0, stop=z == 1)
                ins.then_inc(k_full, 1)

            def inputs(b, s, turn):
                pe.wait_ge(U_in[s], 160 * turn + 160)
                pe.wait_ge(tr_free, 4 * b + 6)
                pe.wait_ge(k_free, b + 1)
                for r in range(4):
                    pe.wait_ge(x_free, 4 * b + r + 1)
                    for c in range(2 * r, 2 * r + 2):
                        for z in range(2):
                            for e in range(2):
                                at = UC * (2 * (c % 2) + z)
                                ins = nc.tensor.matmul(aux[2 + r % 2][64 * e:64 * e + 64, at:at + UC],
                                                       tabT[:, c, z, 64 * e:64 * e + 64], U[s][:, 2 * c + e, :],
                                                       start=True, stop=True)
                    ins.then_inc(x_full, 1)

            for i in range(2):
                dn.tile(pe, i, i, 0, mem.acth, mem.actl)
            tables(0)

            def batch(b, q, h):
                for i in range(2):
                    dn.tile(pe, 2 * b + i, i, b, mem.acth, mem.actl)
                inputs(b - 1, 1 - q, h if q == 1 else h - 1)
                tables(b)
            paired(pe, 1, NB, batch)
            inputs(NB - 1, 1, NB // 2 - 1)


def gate_and_scan(nc, mem, ten, dram):
    o = mem.p1_at
    zst = []
    for s in range(2):
        t, o = mem.at(f"z_out{s}", [P, TOK], o)
        zst.append(t)
    a8i, o = mem.at("a8_im_signed", [P, 2, NP], o)
    m1, o = mem.at("scan_m1", [P, 2, NP], o)
    m2, o = mem.at("scan_m2", [P, 2, NP], o)
    so, o = mem.at("state_out", [P, 2, NS + 1, NP], o)
    s1, o = mem.at("state_t1", [P, NS, NP], o)
    s2, o = mem.at("state_t2", [P, NS, NP], o)
    srow, o = mem.at("state_rows", [NP, 2, NS + 1, P], o)
    zer = mem.Bt
    aux = mem.aux
    w = blocks(ten["a_w_in"][0, :, :])
    kk = dram["k"].rearrange("i g (t o) -> i g t o", o=CH)
    with ExitStack() as ctx:
        def sem(x):
            return nc.alloc_semaphore(f"scan_{x}")

        dn = Dense(ctx, nc, mem, "z_proj", 1)
        z_copied, k_stored = sem("z_copied"), sem("k_stored")
        z_stored = [sem("z_stored0"), sem("z_stored1")]
        zeroed, step, fin, ended = sem("zeroed"), sem("step"), sem("final"), sem("states_ready")
        s_full, s_free, s_out = sem("rows_full"), sem("rows_moved"), sem("rows_stored")
        block = ctx.enter_context(nc.Block())

        @block.sync
        def _(sp):
            for s in range(2):
                sp.sem_inc(z_stored[s], 16)
            for n in range(2):
                dn.load(sp, n, n, w[:, :, W2 + P * n:W2 + P * n + P])
            for j in range(L):
                sp.dma_start(kk[:, :, 14 - j, :], mem.Ksb[CH * j:CH * j + CH, :, :]).then_inc(k_stored, 16)
            sp.wait_ge(zeroed, 1)
            for t in range(7):
                sp.dma_start(kk[:, :, t, :], zer[0:CH, :, :, :].rearrange("p z c o -> p (z c) o")).then_inc(k_stored, 16)

            def store(m, i):
                sp.wait_ge(z_copied, m + 1)
                sp.dma_start(dram["z"][cols(m), :], zst[i][:, :]).then_inc(z_stored[i], 16)

            def tile(m, i, h):
                dn.load(sp, m, i, w[:, :, bass.ds(W2 + m * P, P)])
                store(m - 2, i)
            paired(sp, 2, WT, tile)
            for i in range(2):
                store(WT - 2 + i, i)
            sp.wait_ge(s_free, 5)
            for z, (pn, sn) in enumerate((("p_re", "s_re"), ("p_im", "s_im"))):
                sp.dma_start(ten[pn][0, 0, :, :].rearrange("(c e) p -> c (e p)", e=2), srow[:, z, 0, :]).then_inc(s_out, 16)
                sp.dma_start(ten[sn][0, :, :, :].rearrange("s (c e) p -> c s (e p)", e=2), srow[:, z, 1:NS + 1, :]).then_inc(s_out, 16)
            sp.wait_ge(s_out, 64)
            sp.wait_ge(k_stored, 16 * 15)
            for s in range(2):
                sp.wait_ge(z_stored[s], 16 * (WT // 2) + 16)

        @block.gpsimd
        def _(pool):
            dn.start_raw(pool)
            pool.memset(zer[0:CH, :, :, :], 0.0).then_inc(zeroed, 1)
            paired(pool, 0, WT, lambda n, q, h: dn.split_lo(pool, n, q))

        @block.scalar
        def _(act):
            for n in range(2):
                dn.split_hi(act, n, n, 0)

            def silu(m, i, h):
                dn.wait_tile(act, m)
                act.wait_ge(z_stored[i], 16 * h + 16)
                act.activation(zst[i][:, :], columns(mem.acc[i]), ACT.Silu).then_inc(z_copied, 1)
                act.wait_ge(z_copied, m + 1)
                act.sem_inc(dn.acc_free[i], 1)

            def tile(m, i, h):
                silu(m - 2, i, h - 1)
                dn.split_hi(act, m, i, h)
            paired(act, 2, WT, tile)
            for i in range(2):
                silu(WT - 2 + i, i, WT // 2 - 1)

        @block.vector
        def _(v):
            a8 = mem.apow[:, L, 0, :].unsqueeze(1).broadcast_to([P, 2, NP])
            v.tensor_scalar(a8i[:, 0, :], mem.apow[:, L, 1, :], -1.0, None, ALU.mult)
            v.tensor_copy(a8i[:, 1, :], mem.apow[:, L, 1, :]).then_inc(step, 1)
            v.wait_ge(step, 1)
            with v.Fori(0, NC // 4) as h:
                for q in range(4):
                    c = 4 * h + q
                    was = mem.XH[:, bass.ds(c, 1), :, :].rearrange("p n z c -> p (n z) c")
                    now = mem.XH[:, bass.ds(c + 1, 1), :, :].rearrange("p n z c -> p (n z) c")
                    v.tensor_tensor(m1[:, :, :], was, a8, ALU.mult)
                    v.tensor_tensor(m2[:, 0, :], was[:, 1, :], a8i[:, 0, :], ALU.mult)
                    v.tensor_tensor(m2[:, 1, :], was[:, 0, :], a8i[:, 1, :], ALU.mult).then_inc(step, 1)
                    v.wait_ge(step, 3 * c + 2)
                    v.tensor_tensor(m1[:, :, :], m1[:, :, :], m2[:, :, :], ALU.add).then_inc(step, 1)
                    v.wait_ge(step, 3 * c + 3)
                    v.tensor_tensor(now, now, m1[:, :, :], ALU.add).then_inc(step, 1)
                    v.wait_ge(step, 3 * c + 4)
            count = [0]

            def link(ins):
                count[0] += 1
                ins.then_inc(fin, 1)
                v.wait_ge(fin, count[0])

            hr = mem.XH[:, C_FIRST:C_LAST, 0, :]
            hi = mem.XH[:, C_FIRST:C_LAST, 1, :]
            ar = mem.apow[:, 1, 0, :].unsqueeze(1).broadcast_to([P, NS, NP])
            ai = mem.apow[:, 1, 1, :].unsqueeze(1).broadcast_to([P, NS, NP])
            for z, (x, y, op) in enumerate(((hr, hi, ALU.subtract), (hi, hr, ALU.add))):
                v.tensor_copy(so[:, z, 0, :], mem.XH[:, NC, z, :])
                v.tensor_tensor(s1[:, :, :], x, ar, ALU.mult)
                link(v.tensor_tensor(s2[:, :, :], y, ai, ALU.mult))
                link(v.tensor_tensor(s1[:, :, :], s1[:, :, :], s2[:, :, :], op))
                link(v.tensor_tensor(so[:, z, 1:NS + 1, :], s1[:, :, :], mem.Xs[:, :, z, :], ALU.add))
            v.sem_inc(ended, 1)
            rows = srow[:, :, :, :].rearrange("p z s m -> p (z s) m")
            for r in range(5):
                n = min(4, 18 - 4 * r)
                v.wait_ge(s_full, r + 1)
                v.tensor_copy(rows[:, 4 * r:4 * r + n, :],
                              aux[r % 4][0:NP, 0:P * n].rearrange("p (s m) -> p s m", m=P)).then_inc(s_free, 1)

        @block.tensor
        def _(pe):
            dn.start(pe)
            paired(pe, 0, WT, lambda m, a, h: dn.tile(pe, m, a, h, mem.acth, mem.actl))
            pe.wait_ge(ended, 1)
            flat = so[:, :, :, :].rearrange("p z s c -> p (z s) c")
            for r in range(5):
                if r == 4:
                    pe.wait_ge(s_free, 1)
                for q in range(4 * r, min(4 * r + 4, 18)):
                    ins = nc.tensor.transpose(aux[r % 4][0:NP, P * (q % 4):P * (q % 4) + P], flat[:, q, :], mem.ident[:, :])
                ins.then_inc(s_full, 1)


def outputs(nc, mem, ten, dram):
    o = mem.p3_at
    T, U, C8, Y = [], [], [], []
    for s in range(2):
        t, o = mem.at(f"toeplitz{s}", [P, BG, P], o)
        T.append(t)
        t, o = mem.at(f"Uy{s}", [P, BG, UC], o)
        U.append(t)
        t, o = mem.at(f"c_tab{s}", [P, BP, 2, P], o)
        C8.append(t)
        t, o = mem.at(f"Y{s}", [P, BG, YC], o)
        Y.append(t)
    o = mem.ring_at
    hb, o = mem.at("h_dense", [P, 2, BP, YC], o)
    t1, o = mem.at("c_t1", [P, BP, L, CH], o)
    t2, o = mem.at("c_t2", [P, BP, L, CH], o)
    yt, ut = [], []
    for s in range(2):
        t, o = mem.at(f"y_in{s}", [P, TOK], o)
        yt.append(t)
    for s in range(1):
        t, o = mem.at(f"u_in{s}", [P, TOK], o)
        ut.append(t)
    assert o <= mem.rest
    aux = mem.aux
    kk, su, sy = dram["k"], dram["u"], dram["y"]
    su_p = su[:, 0:SEQ].rearrange("(g i) (j c) -> j i g c", i=CH, j=L)
    su_s = su[:, SEQ:TOK].rearrange("(g i) s -> i g s", i=CH)
    sy_p = sy[:, 0:SEQ].rearrange("(g i) (j c) -> j i g c", i=CH, j=L)
    sy_s = sy[:, SEQ:TOK].rearrange("(g i) s -> i g s", i=CH)
    with ExitStack() as ctx:
        def sem(x):
            return nc.alloc_semaphore(f"outputs_{x}")

        zeroed = sem("zeroed")
        T_in = [sem("T_in0"), sem("T_in1")]
        U_in = [sem("U_in0"), sem("U_in1")]
        y_full, y_copied, y_stored = sem("y_full"), sem("y_copied"), sem("y_stored")
        y_in, u_in = [sem("y_in0"), sem("y_in1")], sem("u_in")
        mul, tab, dense = sem("mul_done"), sem("tab_ready"), sem("h_dense")
        skip, gel, hi_r, lo_r = sem("skip_added"), sem("gelu_done"), sem("hi_ready"), sem("lo_ready")
        block = ctx.enter_context(nc.Block())

        @block.sync
        def _(sp):
            sp.sem_inc(y_stored, 288)
            sp.wait_ge(zeroed, 2)

            def load(b, s):
                sp.wait_ge(y_full, 2 * b + 2)
                for j in range(L):
                    sp.dma_start(T[s][CH * j:CH * j + CH, :, :], kk[:, cols(b, BG), CH * (7 - j):CH * (15 - j)]).then_inc(T_in[s], 16)
                    sp.dma_start(U[s][CH * j:CH * j + CH, :, 0:NC], su_p[j, :, cols(b, BG), :]).then_inc(U_in[s], 16)
                sp.dma_start(U[s][0:CH, :, C_FIRST:C_LAST], su_s[:, cols(b, BG), :]).then_inc(U_in[s], 16)

            def regroup(b, s):
                sp.wait_ge(y_copied, 4 * b + 8)
                for j in range(L):
                    sp.dma_start(sy_p[j, :, cols(b, BG), :], Y[s][CH * j:CH * j + CH, :, 0:NC]).then_inc(y_stored, 16)
                sp.dma_start(sy_s[:, cols(b, BG), :], Y[s][0:CH, :, C_FIRST:C_LAST]).then_inc(y_stored, 16)
                sp.wait_ge(y_stored, 144 * b + 432)
                for i in range(2):
                    m = 2 * b + i
                    sp.wait_ge(lo_r, m + 1)
                    sp.dma_start(yt[i][:, :], sy[cols(m), :]).then_inc(y_in[i], 16)
                    sp.wait_ge(skip, m + 1)
                    sp.dma_start(ut[0][:, :], su[cols(m), :]).then_inc(u_in, 16)

            load(0, 0)
            load(1, 1)

            def batch(b, q, h):
                regroup(b - 2, q)
                load(b, q)
            paired(sp, 2, NB, batch)
            regroup(NB - 2, 0)
            regroup(NB - 1, 1)

        @block.gpsimd
        def _(pool):
            for s in range(2):
                pool.memset(U[s][:, :, :], 0.0).then_inc(zeroed, 1)

        @block.tensor
        def _(pe):
            pe.sem_inc(y_full, 4)

            def batch(b, s, turn):
                pe.wait_ge(T_in[s], 128 * turn + 128)
                pe.wait_ge(U_in[s], 144 * turn + 144)
                pe.wait_ge(tab, b + 1)
                pe.wait_ge(dense, b + 1)
                for r in range(2):
                    pe.wait_ge(y_copied, 4 * b + 2 * r + 2)
                    for c in range(4 * r, 4 * r + 4):
                        y = [aux[2 * r + e][:, P * (c % 4):P * (c % 4) + YC] for e in range(2)]
                        for e in range(2):
                            nc.tensor.matmul(y[e], T[s][:, 2 * c + e, :], U[s][:, 2 * c + e, 0:YC], start=True, stop=False)
                        for z in range(2):
                            for e in range(2):
                                rows = slice(64 * e, 64 * e + 64)
                                ins = nc.tensor.matmul(y[e], C8[s][rows, c, z, :], hb[rows, z, c, :],
                                                       start=False, stop=z == 1)
                    ins.then_inc(y_full, 1)
            paired(pe, 0, NB, batch)

        @block.scalar
        def _(act):
            def copy_y(b, s):
                act.wait_ge(y_stored, 144 * b + 144)
                for r in range(2):
                    act.wait_ge(y_full, 2 * b + 5 + r)
                    for e in range(2):
                        act.activation(Y[s][:, 8 * r:8 * r + 8, :].rearrange("p (c e) n -> p e c n", e=2)[:, e, :, :],
                                       aux[2 * r + e][:, :].rearrange("p (g n) -> p g n", g=4)[:, :, 0:YC],
                                       ACT.Copy).then_inc(y_copied, 1)

            def gelu(m, i):
                act.wait_ge(skip, m + 2)
                act.activation(yt[i][:, :], yt[i][:, :], ACT.Gelu_apprx_tanh).then_inc(gel, 1)
                act.wait_ge(gel, m + 1)
                act.activation(mem.acth[:, bass.ds(m, 1), :].rearrange("p o n -> p (o n)"), yt[i][:, :], ACT.Copy).then_inc(hi_r, 1)

            act.sem_inc(y_copied, 4)
            copy_y(0, 0)
            copy_y(1, 1)

            def batch(b, q, h):
                for i in range(2):
                    gelu(2 * b - 4 + i, i)
                copy_y(b, q)
            paired(act, 2, NB, batch)
            for m in range(WT - 4, WT):
                gelu(m, m % 2)

        @block.vector
        def _(v):
            v.sem_inc(lo_r, 2)
            v.sem_inc(skip, 1)
            v.sem_inc(mul, 1)

            def build(b, s):
                def power(z):
                    return mem.apow[:, 1:L + 1, z, cols(b, BP)].rearrange("p j c -> p c j").unsqueeze(3).broadcast_to([P, BP, L, CH])

                def c(z):
                    return mem.Ct[:, z, cols(b, BP), :].unsqueeze(2).broadcast_to([P, BP, L, CH])

                v.wait_ge(y_full, 2 * b + 2)
                for z in range(2):
                    v.wait_ge(mul, 6 * b + 3 * z + 1)
                    v.tensor_tensor(t1[:, :, :, :], c(z), power(0), ALU.mult).then_inc(mul, 1)
                    v.tensor_tensor(t2[:, :, :, :], c(1 - z), power(1), ALU.mult).then_inc(mul, 1)
                    v.wait_ge(mul, 6 * b + 3 * z + 3)
                    a, d = (x[:, :, :, :].rearrange("p c j i -> p c (j i)") for x in (t1, t2))
                    if z == 0:
                        v.tensor_tensor(C8[s][:, :, 0, :], a, d, ALU.subtract).then_inc(mul, 1)
                    else:
                        v.scalar_tensor_tensor(C8[s][:, :, 1, :], a, -1.0, d, ALU.mult, ALU.subtract).then_inc(mul, 1)
                v.wait_ge(mul, 6 * b + 7)
                v.wait_ge(y_full, 2 * b + 4)
                for z in range(2):
                    ins = v.tensor_copy(hb[:, z, :, :], mem.XH[:, 0:YC, z, cols(b, BP)].rearrange("p n c -> p c n"))
                ins.then_inc(dense, 1)
                v.wait_ge(dense, b + 1)
                v.sem_inc(tab, 1)

            def add_skip(m, i, turn):
                v.wait_ge(y_in[i], 16 * turn + 16)
                v.wait_ge(u_in, 16 * m + 16)
                v.scalar_tensor_tensor(yt[i][:, :], ut[0][:, :], mem.vec[:, bass.ds(V_D + m, 1)], yt[i][:, :],
                                       ALU.mult, ALU.add).then_inc(skip, 1)

            def low(m, i):
                v.wait_ge(hi_r, m + 1)
                at = bass.ds(m, 1)
                v.tensor_tensor(mem.actl[:, at, :].rearrange("p o n -> p (o n)"), yt[i][:, :],
                                mem.acth[:, at, :].rearrange("p o n -> p (o n)").bitcast(F32), ALU.subtract).then_inc(lo_r, 1)

            build(0, 0)
            build(1, 1)

            def batch(b, q, h):
                for i in range(2):
                    add_skip(2 * b - 4 + i, i, b - 2)
                build(b, q)
                for i in range(2):
                    low(2 * b - 4 + i, i)
            paired(v, 2, NB, batch)
            for m in range(WT - 4, WT, 2):
                for i in range(2):
                    add_skip(m + i, i, m // 2)
                for i in range(2):
                    low(m + i, i)


def glu(nc, mem, ten, dram):
    o = mem.rest
    mem.yh, o = mem.at("y_hi", [P, WT, TOK], o, F32R)
    mem.yl, o = mem.at("y_lo", [P, WT, TOK], o, F32R)
    mem.glu_end = o
    sg, zt, yt = [], [], []
    for s in range(2):
        for name, l in (("sig", sg), ("z_in", zt), ("y_f32", yt)):
            t, o = mem.at(f"{name}{s}", [P, TOK], o)
            l.append(t)
    w = blocks(ten["a_w_glu"][0, :, :])
    with ExitStack() as ctx:
        def sem(x):
            return nc.alloc_semaphore(f"gate_{x}")

        dn = Dense(ctx, nc, mem, "glu", 2)
        z_in = [sem("z_in0"), sem("z_in1")]
        sig, gated, prod = sem("sigmoid"), sem("gated"), sem("product")
        hi_r, lo_r = sem("hi_ready"), sem("lo_ready")
        block = ctx.enter_context(nc.Block())

        @block.sync
        def _(sp):
            def tile(i, s, h):
                for a in range(2):
                    for u in range(2):
                        at = bass.ds((i + WT) * P - a * W2, P)
                        dn.load(sp, 4 * i + 2 * a + u, u, w[:, 8 * u:8 * u + 8, at])
                sp.wait_ge(prod, i + 1)
                sp.dma_start(zt[s][:, :], dram["z"][cols(i), :]).then_inc(z_in[s], 16)
            sp.sem_inc(prod, 2)
            paired(sp, 0, WT, tile)

        @block.gpsimd
        def _(pool):
            dn.start_raw(pool)
            paired(pool, 0, 4 * WT, lambda n, q, h: dn.split_lo(pool, n, q))

        @block.tensor
        def _(pe):
            dn.start(pe)
            paired(pe, 0, 2 * WT, lambda m, a, h: dn.tile(pe, m, a, h, mem.acth, mem.actl))

        @block.scalar
        def _(act):
            def high(i, s):
                act.wait_ge(prod, i + 3)
                act.activation(mem.yh[:, bass.ds(i, 1), :].rearrange("p o n -> p (o n)"), yt[s][:, :], ACT.Copy).then_inc(hi_r, 1)

            def tile(i, s, h, first=False):
                dn.split_hi(act, 4 * i, 0, 2 * i)
                dn.split_hi(act, 4 * i + 1, 1, 2 * i)
                if not first:
                    high(i - 1, 1 - s)
                dn.split_hi(act, 4 * i + 2, 0, 2 * i + 1)
                dn.wait_tile(act, 2 * i)
                act.wait_ge(gated, i)
                act.activation(sg[s][:, :], columns(mem.acc[0]), ACT.Sigmoid,
                               bias=mem.vec[:, bass.ds(V_BGLU + WT + i, 1)]).then_inc(dn.acc_free[0], 1)
                dn.split_hi(act, 4 * i + 3, 1, 2 * i + 1)
            act.sem_inc(gated, 1)
            tile(0, 0, 0, True)
            paired(act, 1, WT, tile)
            high(WT - 1, 1)

        @block.vector
        def _(v):
            def tile(i, s, h):
                dn.wait_tile(v, 2 * i + 1)
                v.wait_ge(dn.acc_free[0], i + 2)
                v.scalar_tensor_tensor(sg[s][:, :], columns(mem.acc[1]), mem.vec[:, bass.ds(V_BGLU + i, 1)],
                                       sg[s][:, :], ALU.add, ALU.mult).then_inc(dn.acc_free[1], 1)
                v.wait_ge(dn.acc_free[1], i + 2)
                v.sem_inc(gated, 1)
                v.wait_ge(z_in[s], 16 * h + 16)
                v.wait_ge(lo_r, i + 1)
                v.tensor_tensor(yt[s][:, :], sg[s][:, :], zt[s][:, :], ALU.mult).then_inc(prod, 1)
                v.wait_ge(hi_r, i + 1)
                at = bass.ds(i, 1)
                v.tensor_tensor(mem.yl[:, at, :].rearrange("p o n -> p (o n)"), yt[s][:, :],
                                mem.yh[:, at, :].rearrange("p o n -> p (o n)").bitcast(F32), ALU.subtract).then_inc(lo_r, 1)
            v.sem_inc(lo_r, 2)
            paired(v, 0, WT, tile)


def residual(nc, mem, name, ten_w, units, xh, xl, gains, o_at, norm_at, natural=False):
    ot, o = mem.at(f"{name}_o", [P, DT, TOK], o_at)
    w = blocks(ten_w)
    with ExitStack() as ctx:
        def sem(x):
            return nc.alloc_semaphore(f"{name}_{x}")

        dn = Dense(ctx, nc, mem, name, units)
        nm = Norm(ctx, nc, mem, name + "_post", norm_at)
        added = sem("added")
        block = ctx.enter_context(nc.Block())

        @block.sync
        def _(sp):
            def tile(m, a, h):
                for u in range(units):
                    s = u if units == 2 else a
                    dn.load(sp, units * m + u, s, w[:, 8 * u:8 * u + 8, cols(m)])
            paired(sp, 0, DT, tile)

        @block.gpsimd
        def _(pool):
            dn.start_raw(pool)
            paired(pool, 0, units * DT, lambda n, q, h: dn.split_lo(pool, n, q))

        @block.scalar
        def _(act):
            paired(act, 0, units * DT, lambda n, q, h: dn.split_hi(act, n, q, h))
            for f in range(DT):
                act.wait_ge(dn.acc_free[f % 2], f // 2 + 2)
                nm.square(act, f, ot[:, f, :])
            nm.take_root(act)

        @block.tensor
        def _(pe):
            dn.start(pe)
            paired(pe, 0, DT, lambda m, a, h: dn.tile(pe, m, a, h, xh, xl))
            for f in range(DT):
                nm.add(pe, f)

        @block.vector
        def _(v):
            def tile(m, a, h):
                dn.wait_tile(v, m)
                x = ot[:, bass.ds(m, 1), :].rearrange("p o n -> p (o n)")
                if natural:
                    v.tensor_copy(x[:, 0:SEQ].rearrange("p (j c) -> p j c", j=L),
                                  columns(mem.acc[a])[:, 0:SEQ].rearrange("p (c j) -> p j c", j=L))
                    v.tensor_copy(x[:, SEQ:TOK], columns(mem.acc[a])[:, SEQ:TOK]).then_inc(dn.acc_free[a], 1)
                else:
                    v.tensor_copy(x, columns(mem.acc[a])).then_inc(dn.acc_free[a], 1)
            paired(v, 0, DT, tile)
            nm.invert(v)
            for f in range(DT):
                if f >= 2:
                    v.wait_ge(added, 2 * f - 2)
                v.scalar_tensor_tensor(nm.tmp[f % 2][:, :], ot[:, f, :], mem.vec[:, gains + f:gains + f + 1],
                                       nm.rstd[:, :], ALU.mult, ALU.mult).then_inc(added, 1)
                v.wait_ge(added, 2 * f + 1)
                v.tensor_tensor(mem.xT[:, f, :], mem.xT[:, f, :], nm.tmp[f % 2][:, :], ALU.add).then_inc(added, 1)
            v.wait_ge(added, 2 * DT)


def ssm_out(nc, mem, ten, dram):
    residual(nc, mem, "a_out", ten["a_w_out"][0, :, :], 2, mem.yh, mem.yl, V_APOST, mem.acth_at, mem.glu_end)


def project(nc, mem, ten, dram):
    o = mem.rest
    mem.kv, o = mem.at("kvT", [P, 2 * DT, TOK], o)
    mem.v_at = mem.rest + DT * TOK * 4
    mem.q, o = mem.at("qT", [P, 3 * DT, TOK], o)
    mem.zb, o = mem.at("zb", [P, DT, TOK], o)
    mem.stat_at = o
    wk, wb = blocks(ten["w_kv"]), blocks(ten["b_w_in"][0, :, :])

    def in_token_order(op, out, tile, a, dn, *func, **scale):
        x = out[:, bass.ds(tile, 1), :].rearrange("p o n -> p (o n)")
        y = columns(mem.acc[a])
        op(x[:, 0:SEQ].rearrange("p (c j) -> p j c", j=L), y[:, 0:SEQ].rearrange("p (j c) -> p j c", j=L), *func, **scale)
        op(x[:, SEQ:TOK], y[:, SEQ:TOK], *func, **scale).then_inc(dn.acc_free[a], 1)

    with ExitStack() as ctx:
        def sem(x):
            return nc.alloc_semaphore(f"proj_{x}")

        dn = Dense(ctx, nc, mem, "proj", 1)
        nm = Norm(ctx, nc, mem, "norm_kv", mem.rest)
        block = ctx.enter_context(nc.Block())

        @block.sync
        def _(sp):
            paired(sp, 0, 2 * DT, lambda m, s, h: dn.load(sp, m, s, wk[:, :, cols(m)]))
            paired(sp, 2 * DT, 6 * DT, lambda m, s, h: dn.load(sp, m, s, wb[:, :, bass.ds(m * P - 2 * D, P)]))

        @block.gpsimd
        def _(pool):
            dn.start_raw(pool)
            paired(pool, 0, 6 * DT, lambda n, q, h: dn.split_lo(pool, n, q))

        @block.tensor
        def _(pe):
            dn.start(pe)
            for f in range(DT):
                nm.add(pe, f)
            pe.wait_ge(nm.act_lo, 2 * DT)
            paired(pe, 0, 2 * DT, lambda m, a, h: dn.tile(pe, m, a, h, mem.acth[:, 0:DT, :], mem.actl[:, 0:DT, :]))
            paired(pe, 2 * DT, 6 * DT, lambda m, a, h: dn.tile(pe, m, a, h, mem.acth[:, DT:, :], mem.actl[:, DT:, :]))

        @block.scalar
        def _(act):
            for f in range(DT):
                nm.square(act, f, mem.xT[:, f, :])
            nm.take_root(act)
            nm.apply_hi(act, 0)
            nm.apply_hi(act, DT, DT)
            paired(act, 0, 2 * DT + 2, lambda n, q, h: dn.split_hi(act, n, q, h))

            def q_tile(m, a, h):
                dn.wait_tile(act, m - 2)
                in_token_order(act.activation, mem.q, m - 2 - 2 * DT, a, dn, ACT.Copy, scale=HD ** -0.5)
                dn.split_hi(act, m, a, h)

            def z_tile(m, a):
                dn.wait_tile(act, m)
                in_token_order(act.activation, mem.zb, m - 5 * DT, a, dn, ACT.Silu)

            def z_next(m, a, h):
                z_tile(m - 2, a)
                dn.split_hi(act, m, a, h)
            paired(act, 2 * DT + 2, 5 * DT + 2, q_tile)
            paired(act, 5 * DT + 2, 6 * DT, z_next)
            z_tile(6 * DT - 2, 0)
            z_tile(6 * DT - 1, 1)

        @block.vector
        def _(v):
            nm.invert(v)
            nm.apply(v, V_KV, 0)
            nm.apply(v, V_BPRE, DT, DT)

            def kv_tile(m, a, h):
                dn.wait_tile(v, m)
                in_token_order(v.tensor_copy, mem.kv, m, a, dn)
            paired(v, 0, 2 * DT, kv_tile)


def block_tokens(x, b):
    return x[:, P * b:P * b + P]


def residue_tokens(x, r):
    return x[:, r:r + 4 * (P - 1) + 1:4]


def token_rows(nc, mem, ten, dram):
    o = mem.acth_at
    mem.vnat, o = mem.at("v_block", [P, 4, D], o)
    mem.vres, o = mem.at("v_residue", [P, 4, D], o)
    mem.attn_at = o
    knat, o = mem.at("k_block", [P, 4, D], o)
    mem.kvnew_at = o
    mem.kvnew, o = mem.at("kv_new", [NS, 2, D], o)
    assert o <= mem.rest
    acc = mem.acc
    with ExitStack() as ctx:
        def sem(x):
            return nc.alloc_semaphore(f"rows_{x}")

        full, moved_a, moved_v, stored = sem("full"), sem("moved_act"), sem("moved_dve"), sem("stored")
        block = ctx.enter_context(nc.Block())

        rounds = [("kb", b) for b in range(4)] + [("vb", b) for b in range(4)] + [("vr", r) for r in range(4)] + \
                 [("new", z) for z in range(2)]

        def target(kind, i):
            return {"kb": knat, "vb": mem.vnat, "vr": mem.vres, "new": mem.kvnew}[kind][:, i, :]

        @block.tensor
        def _(pe):
            for n, (kind, i) in enumerate(rounds):
                if n >= 2:
                    pe.wait_ge(moved_a if n % 2 == 0 else moved_v, n // 2)
                for f in range(DT):
                    src = mem.kv[:, f + (DT if kind[0] == "v" or (kind, i) == ("new", 1) else 0), :]
                    if kind == "new":
                        out, src = acc[n % 2][0:NS, P * f:P * f + P], src[:, SEQ:TOK]
                    else:
                        out = acc[n % 2][:, P * f:P * f + P]
                        src = residue_tokens(src[:, 0:SEQ], i) if kind == "vr" else block_tokens(src[:, 0:SEQ], i)
                    ins = nc.tensor.transpose(out, src, mem.ident[:, :])
                ins.then_inc(full, 1)

        @block.scalar
        def _(act):
            for n in range(0, len(rounds), 2):
                rows = NS if rounds[n][0] == "new" else P
                act.wait_ge(full, n + 1)
                act.activation(target(*rounds[n]), acc[0][0:rows, :], ACT.Copy).then_inc(moved_a, 1)

        @block.vector
        def _(v):
            for n in range(1, len(rounds), 2):
                rows = NS if rounds[n][0] == "new" else P
                v.wait_ge(full, n + 1)
                v.tensor_copy(target(*rounds[n]), acc[1][0:rows, :]).then_inc(moved_v, 1)

        @block.sync
        def _(sp):
            for s in range(NS):
                sp.dma_start(ten["s_kv"][s, 0:SEQ - 1, :, :, :], ten["cache_kv"][s, 1:SEQ, :, :, :]).then_inc(stored, 16)
            out = ten["p_kv"][0, :, :, :, :].rearrange("t z h d -> z t (h d)")
            for z, x in enumerate((knat, mem.vnat)):
                sp.wait_ge(moved_a, 2 * z + 2)
                sp.wait_ge(moved_v, 2 * z + 2)
                for b in range(4):
                    sp.dma_start(out[z, P * b:P * b + P, :], x[:, b, :]).then_inc(stored, 16)
            sp.wait_ge(moved_a, 7)
            sp.wait_ge(moved_v, 7)
            sp.dma_start(ten["s_kv"][:, SEQ - 1, :, :, :].rearrange("s z h d -> s z (h d)"), mem.kvnew[:, :, :]).then_inc(stored, 16)
            sp.wait_ge(stored, 16 * 17)


def attention(nc, mem, ten, dram):
    o = mem.attn_at
    far, o = mem.at("far_res", [P, 4, N_HEADS, HD + 2], o)
    near, o = mem.at("far_nat", [P, 4, N_HEADS, HD + 2], o)
    S, PT = [], []
    for s in range(2):
        t, o = mem.at(f"scores{s}", [P, 4, 2, P], o)
        S.append(t)
    for s in range(2):
        t, o = mem.at(f"probsT{s}", [P, 8, P], o)
        PT.append(t)
    dist, o = mem.at("distances", [P, 4, P], o)
    slope, o = mem.at("slopes", [P, 3 * N_HEADS], o)
    assert o <= mem.rest
    mem.o_nat, _ = mem.at("o_nat", [P, 4, D], mem.v_at)
    o = mem.stat_at
    nmax, o = mem.at("neg_max", [P, 2, 4], o)
    e12, o = mem.at("far_scale", [P, 2, 4], o)
    l0, o = mem.at("near_sum", [P, 2, 4], o)
    den, o = mem.at("denominator", [P, 2, 4], o)
    on, o = mem.at("joined", [P, 4, HD], o)
    aux, acc = mem.aux, mem.acc
    const = ten["constants"]

    with ExitStack() as ctx:
        def sem(x):
            return nc.alloc_semaphore(f"attn_{x}")

        c_in = sem("constants_in")
        s_full, biased, maxed, exped, summed = sem("scores"), sem("biased"), sem("maxed"), sem("exped"), sem("summed")
        t_full, t_moved, o_full, o_moved = sem("transposed"), sem("t_moved"), sem("out_full"), sem("out_moved")
        moved = sem("far_moved")
        dve = sem("dve_chain")
        scale = sem("far_scale_ready")
        ready = sem("scale_ask")
        block = ctx.enter_context(nc.Block())
        units = [("far", h) for h in range(N_HEADS)] + [("near", h) for h in range(N_HEADS)]

        @block.sync
        def _(sp):
            sp.dma_start(dist[:, :, :], const[:, 0:4 * P].rearrange("p (a k) -> p a k", a=4)).then_inc(c_in, 16)
            sp.dma_start(slope[:, :], const[:, 4 * P:4 * P + 3 * N_HEADS]).then_inc(c_in, 16)
            sp.wait_ge(o_moved, N_HEADS)
            for r in range(4):
                for b in range(4):
                    sp.dma_start(near[r:r + 4 * 31 + 1:4, b, :, :], far[32 * b:32 * b + 32, r, :, :]).then_inc(moved, 16)

        @block.tensor
        def _(pe):
            def rows(h):
                return slice(HD * (h % 2), HD * (h % 2) + HD)

            def scores(n):
                kind, h = units[n]
                if n >= 2:
                    pe.wait_ge(biased, n - 1)
                q, k = mem.q[rows(h), :, 0:SEQ], mem.kv[rows(h), h // 2, 0:SEQ]
                out = acc[n % 2][:, :].rearrange("p (i g k) -> p i g k", i=4, g=2)
                for i in range(4):
                    if kind == "far":
                        for g in range(2):
                            ins = nc.tensor.matmul(out[:, i, g, :], residue_tokens(q[:, DT * (1 + g) + h // 2, :], i),
                                                   residue_tokens(k, i), start=True, stop=True)
                    else:
                        for g in range(2 if i else 1):
                            ins = nc.tensor.matmul(out[:, i, g, :], block_tokens(q[:, h // 2, :], i),
                                                   block_tokens(k, i - g), start=True, stop=True)
                ins.then_inc(s_full, 1)

            def products(n):
                kind, h = units[n]
                s = n % 2
                probs = S[s]
                far_unit = kind == "far"
                pe.wait_ge(summed, n + 1)
                if n >= 1:
                    pe.wait_ge(t_moved, 2 * n)
                for i in range(4):
                    nc.tensor.transpose(aux[0][:, P * i:P * i + P], probs[:, i, 0, :], mem.ident[:, :])
                ins = None
                if not far_unit:
                    for i in range(1, 4):
                        ins = nc.tensor.transpose(aux[1][:, P * i:P * i + P], probs[:, i, 1, :], mem.ident[:, :])
                else:
                    ins = nc.tensor.transpose(aux[1][:, 0:P], probs[:, 0, 0, :], mem.ident[:, :])
                ins.then_inc(t_full, 1)
                pe.wait_ge(t_moved, 2 * n + 2)
                if n >= 2:
                    pe.wait_ge(o_moved, n - 1)
                v = mem.vres if far_unit else mem.vnat
                for i in range(4):
                    out = aux[2 + s][:, HD * i:HD * i + HD]
                    two_blocks = not far_unit and i > 0
                    ins = nc.tensor.matmul(out, PT[s][:, i, :], v[:, i, HD * h:HD * h + HD], start=True, stop=not two_blocks)
                    if two_blocks:
                        ins = nc.tensor.matmul(out, PT[s][:, 4 + i, :], v[:, i - 1, HD * h:HD * h + HD], start=False, stop=True)
                ins.then_inc(o_full, 1)

            scores(0)
            for n in range(len(units)):
                if n + 1 < len(units):
                    scores(n + 1)
                products(n)

        @block.vector
        def _(v):
            count = [0]

            def link(ins):
                count[0] += 1
                ins.then_inc(dve, 1)
                v.wait_ge(dve, count[0])

            v.wait_ge(c_in, 32)

            def bias(n):
                kind, h = units[n]
                s = n % 2
                src = acc[s][:, :].rearrange("p (i g k) -> p i g k", i=4, g=2)
                v.wait_ge(s_full, n + 1)
                if n >= 2:
                    v.wait_ge(t_full, n - 1)
                if kind == "near":
                    link(v.memset(S[s][:, 0, 1, :], -1e30))
                for g in range(2):
                    if kind == "far":
                        d, sl, i0 = dist[:, 2 + g, :], slope[:, N_HEADS * (1 + g) + h:N_HEADS * (1 + g) + h + 1], 0
                    else:
                        d, sl, i0 = dist[:, g, :], slope[:, h:h + 1], g
                    ins = v.scalar_tensor_tensor(S[s][:, i0:4, g, :], d.unsqueeze(1).broadcast_to([P, 4 - i0, P]), sl,
                                                 src[:, i0:4, g, :], ALU.mult, ALU.add)
                ins.then_inc(biased, 1)
                v.wait_ge(biased, n + 1)
                flat = S[s][:, :, :, :].rearrange("p i g k -> p i (g k)")
                if kind == "far":
                    m = far[:, :, h, HD:HD + 1].rearrange("p i o -> p (i o)")
                    link(v.tensor_reduce(m, flat, AX_X, ALU.max))
                else:
                    if h == 0:
                        v.wait_ge(moved, 16 * 16)
                    m = nmax[:, s, :]
                    link(v.tensor_reduce(m, flat, AX_X, ALU.max))
                    link(v.tensor_tensor(m, m, near[:, :, h, HD:HD + 1].rearrange("p i o -> p (i o)"), ALU.max))
                    link(v.tensor_tensor(e12[:, s, :], near[:, :, h, HD:HD + 1].rearrange("p i o -> p (i o)"), m, ALU.subtract))
                link(v.tensor_scalar(nmax[:, s, :], m, -1.0, None, ALU.mult))
                v.sem_inc(maxed, 1)

            def after(n):
                kind, h = units[n]
                s = n % 2
                v.wait_ge(exped, n + 1)
                if kind == "far":
                    link(v.tensor_tensor(S[s][:, :, 0, :], S[s][:, :, 0, :], S[s][:, :, 1, :], ALU.add))
                v.sem_inc(summed, 1)
                v.wait_ge(t_full, n + 1)
                if kind == "near":
                    v.tensor_copy(PT[s][:, 5:8, :], aux[1][:, P:4 * P].rearrange("p (i q) -> p i q", i=3)).then_inc(t_moved, 1)
                else:
                    v.sem_inc(t_moved, 1)

            def finish(n):
                kind, h = units[n]
                s = n % 2
                v.wait_ge(o_full, n + 1)
                out = aux[2 + s][:, 0:4 * HD].rearrange("p (i d) -> p i d", i=4)
                if kind == "far":
                    v.tensor_copy(far[:, :, h, 0:HD], out).then_inc(o_moved, 1)
                    return
                link(v.tensor_tensor(den[:, s, :], e12[:, s, :], near[:, :, h, HD + 1:HD + 2].rearrange("p i o -> p (i o)"), ALU.mult))
                link(v.tensor_tensor(den[:, s, :], den[:, s, :], l0[:, s, :], ALU.add))
                v.tensor_tensor(on[:, :, :], near[:, :, h, 0:HD], e12[:, s, :].unsqueeze(2).broadcast_to([P, 4, HD]), ALU.mult)
                link(v.reciprocal(den[:, s, :], den[:, s, :]))
                link(v.tensor_tensor(on[:, :, :], on[:, :, :], out, ALU.add))
                link(v.tensor_tensor(mem.o_nat[:, :, HD * h:HD * h + HD], on[:, :, :],
                                     den[:, s, :].unsqueeze(2).broadcast_to([P, 4, HD]), ALU.mult))
                v.sem_inc(o_moved, 1)

            for n in range(len(units)):
                if units[n] == ("near", 0):
                    finish(n - 1)
                bias(n)
                if n >= 1 and units[n] != ("near", 0):
                    finish(n - 1)
                after(n)
            finish(len(units) - 1)

        @block.scalar
        def _(act):
            for n, (kind, h) in enumerate(units):
                s = n % 2
                act.wait_ge(maxed, n + 1)
                for i in range(4):
                    acc_out = far[:, i, h, HD + 1:HD + 2] if kind == "far" else l0[:, s, i:i + 1]
                    ins = act.activation(S[s][:, i, :, :].rearrange("p g k -> p (g k)"), S[s][:, i, :, :].rearrange("p g k -> p (g k)"),
                                         ACT.Exp, bias=nmax[:, s, i:i + 1], accum_out=acc_out)
                if kind == "near":
                    ins = act.activation(e12[:, s, :], e12[:, s, :], ACT.Exp)
                ins.then_inc(exped, 1)
                act.wait_ge(t_full, n + 1)
                act.activation(PT[s][:, 0:4, :], aux[0][:, :].rearrange("p (i q) -> p i q", i=4), ACT.Copy).then_inc(t_moved, 1)


KEYS = 2 * (P + 1) + 33


def decode_attention(nc, mem, ten, dram):
    o = mem.acth_at
    rows, kT, vT = [], [], []
    for s in range(2):
        pair = []
        for which in range(2):
            t, o = mem.at(f"cache{s}{which}", [P, 2, D], o)
            pair.append(t)
        rows.append(pair)
    assert o <= mem.kvnew_at
    o = mem.kvnew_at + 2 * D * 4
    kt = []
    for which in range(2):
        t, o = mem.at(f"keysT{which}", [P, DT, P + 1], o)
        kt.append(t)
    vs = []
    for q in range(2):
        t, o = mem.at(f"v_new{q}", [1, D], o)
        vs.append(t)
    qz, o = mem.at("q_spread", [P, DT, 3, N_HEADS], o)
    drow, o = mem.at("distance_row", [N_HEADS, P + 1], o)
    slope, o = mem.at("slopes_d", [P, 3 * N_HEADS], o)
    assert o <= mem.rest
    o = mem.stat_at
    scol, o = mem.at("slope_column", [N_HEADS, 3], o)
    sc, o = mem.at("d_scores", [P, KEYS], o)
    st, o = mem.at("d_stats", [N_HEADS, 4], o)
    pt, o = mem.at("d_probsT", [P, 3, N_HEADS], o)
    mem.od, o = mem.at("d_out", [P, DT, NS], o)
    acc, aux = mem.acc, mem.aux
    with ExitStack() as ctx:
        def sem(x):
            return nc.alloc_semaphore(f"decode_{x}")

        c_in = sem("constants_in")
        r_in = [sem("rows_in0"), sem("rows_in1")]
        k_full, k_moved_a, k_moved_v, q_ready = sem("keys_transposed"), sem("keys0_moved"), sem("keys1_moved"), sem("q_ready")
        zeroed = sem("zeroed")
        s_full, maxed, exped, normed = sem("scores"), sem("maxed"), sem("exped"), sem("normed")
        p_full, p_moved, o_full, o_moved = sem("probs_transposed"), sem("probs_moved"), sem("out_full"), sem("out_moved")
        dve = sem("dve_chain")
        block = ctx.enter_context(nc.Block())

        @block.sync
        def _(sp):
            sp.dma_start(slope[:, :], ten["constants"][:, 4 * P:4 * P + 3 * N_HEADS]).then_inc(c_in, 16)
            sp.dma_start(drow[:, 0:P], ten["constants"][0:N_HEADS, 4 * P + 3 * N_HEADS:]).then_inc(c_in, 16)
            cache = ten["cache_kv"].rearrange("s t z h d -> s t z (h d)")
            v_new = ten["s_kv"][:, SEQ - 1, 1, :, :].rearrange("s h d -> s (h d)")

            def load(s, q, h):
                sp.wait_ge(o_full, s + 1)
                row = cache[bass.ds(s, 1), :, :, :].rearrange("s t z n -> (s t) z n")
                sp.dma_start(rows[q][0][:, :, :], row[SEQ - P:SEQ, :, :]).then_inc(r_in[q], 16)
                sp.dma_start(rows[q][1][:, :, :], row[0:SEQ - 3:4, :, :]).then_inc(r_in[q], 16)
                sp.dma_start(vs[q][:, :], v_new[bass.ds(s, 1), :]).then_inc(r_in[q], 16)
            paired(sp, 0, NS, load)

        @block.gpsimd
        def _(pool):
            pool.memset(qz[:, :, :, :], 0.0).then_inc(zeroed, 1)
            pool.memset(drow[:, P:P + 1], 0.0).then_inc(zeroed, 1)
            pool.memset(sc[:, :], 0.0).then_inc(zeroed, 1)

        @block.tensor
        def _(pe):
            pe.sem_inc(o_full, 2)
            pe.sem_inc(k_moved_a, 1)
            pe.sem_inc(k_moved_v, 1)
            pe.wait_ge(c_in, 32)
            for g in range(3):
                ins = nc.tensor.matmul(aux[0][0:N_HEADS, g:g + 1], slope[0:1, N_HEADS * g:N_HEADS * g + N_HEADS],
                                       mem.ones[0:1, 0:1], start=True, stop=True)
            ins.then_inc(s_full, 1)
            pe.wait_ge(maxed, 1)

            def sequence(s, q, turn):
                pe.wait_ge(r_in[q], 48 * turn + 48)
                for which, moved in ((0, k_moved_a), (1, k_moved_v)):
                    pe.wait_ge(moved, s + 1)
                    for f in range(DT):
                        ins = nc.tensor.transpose(acc[which][:, P * f:P * f + P], rows[q][which][:, 0, P * f:P * f + P],
                                                  mem.ident[:, :])
                    ins.then_inc(k_full, 1)
                pe.wait_ge(q_ready, s + 1)
                pe.wait_ge(k_moved_a, s + 2)
                pe.wait_ge(k_moved_v, s + 2)
                spans = ((0, 0, P + 1, 1), (1, P + 1, P + 1, 1), (1, 2 * (P + 1), 33, 4))
                for g, (which, at, n, step) in enumerate(spans):
                    for f in range(DT):
                        ins = nc.tensor.matmul(aux[0][0:N_HEADS, at:at + n], qz[:, f, g, :],
                                               kt[which][:, f, 0:(n - 1) * step + 1:step], start=f == 0, stop=f == DT - 1)
                ins.then_inc(s_full, 1)
                pe.wait_ge(normed, s + 1)
                nc.tensor.transpose(aux[1][:, 0:P], sc[:, 0:P], mem.ident[:, :])
                nc.tensor.transpose(aux[1][:, P:2 * P], sc[:, P + 1:2 * P + 1], mem.ident[:, :])
                nc.tensor.transpose(aux[1][0:1, 2 * P:3 * P], sc[:, P:P + 1], mem.ident[:, :]).then_inc(p_full, 1)
                pe.wait_ge(p_moved, s + 1)
                for f in range(DT):
                    out = aux[2][:, 2 * f:2 * f + 2]
                    for which in range(2):
                        nc.tensor.matmul(out, rows[q][which][:, 1, P * f:P * f + P], pt[:, which, 2 * f:2 * f + 2],
                                         start=which == 0, stop=False)
                    ins = nc.tensor.matmul(out, vs[q][0:1, P * f:P * f + P], pt[0:1, 2, 2 * f:2 * f + 2], start=False, stop=True)
                ins.then_inc(o_full, 1)
            paired(pe, 0, NS, sequence)

        @block.scalar
        def _(act):
            def sequence(s, q, turn):
                act.wait_ge(k_full, 2 * s + 1)
                act.activation(kt[0][:, :, 0:P], acc[0][:, :].rearrange("p (f n) -> p f n", f=DT), ACT.Copy)
                act.activation(kt[0][:, :, P:P + 1], mem.kv[:, 0:DT, bass.ds(SEQ + s, 1)], ACT.Copy).then_inc(k_moved_a, 1)
                act.wait_ge(maxed, s + 2)
                act.activation(sc[0:N_HEADS, :], sc[0:N_HEADS, :], ACT.Exp, bias=st[:, 1:2], accum_out=st[:, 2:3]).then_inc(exped, 1)
            paired(act, 0, NS, sequence)

        @block.vector
        def _(v):
            v.wait_ge(zeroed, 3)
            v.wait_ge(s_full, 1)
            v.tensor_copy(scol[:, 0:1], aux[0][0:N_HEADS, 0:1]).then_inc(dve, 1)
            v.tensor_scalar(scol[:, 1:3], aux[0][0:N_HEADS, 1:3], 4.0, None, ALU.mult).then_inc(dve, 1)
            v.wait_ge(dve, 2)
            v.sem_inc(maxed, 1)

            def sequence(s, q, turn):
                base = 8 * s + 2

                def link(ins, n):
                    ins.then_inc(dve, 1)
                    v.wait_ge(dve, base + n)

                flat = qz[:, :, :, :].rearrange("p f g h -> p (f g h)")
                for g in range(3):
                    for e in range(2):
                        half = slice(64 * e, 64 * e + 64)
                        first, step = N_HEADS * g + e, 3 * N_HEADS + 2
                        ins = v.tensor_copy(flat[half, first:first + (DT - 1) * step + 1:step],
                                            mem.q[half, DT * g:DT * g + DT, bass.ds(SEQ + s, 1)].rearrange("p f o -> p (f o)"))
                ins.then_inc(q_ready, 1)
                v.wait_ge(k_full, 2 * s + 2)
                v.tensor_copy(kt[1][:, :, 0:P], acc[1][:, :].rearrange("p (f n) -> p f n", f=DT))
                v.tensor_copy(kt[1][:, :, P:P + 1], mem.kv[:, 0:DT, bass.ds(SEQ + s, 1)]).then_inc(k_moved_v, 1)
                v.wait_ge(s_full, s + 2)
                for g, (at, n, step) in enumerate(((0, P + 1, 1), (P + 1, P + 1, 1), (2 * (P + 1), 33, 4))):
                    ins = v.scalar_tensor_tensor(sc[0:N_HEADS, at:at + n], drow[:, 0:(n - 1) * step + 1:step], scol[:, g:g + 1],
                                                 aux[0][0:N_HEADS, at:at + n], ALU.mult, ALU.add)
                link(ins, 1)
                link(v.tensor_reduce(st[:, 0:1], sc[0:N_HEADS, :], AX_X, ALU.max), 2)
                link(v.tensor_scalar(st[:, 1:2], st[:, 0:1], -1.0, None, ALU.mult), 3)
                v.sem_inc(maxed, 1)
                v.wait_ge(exped, s + 1)
                link(v.reciprocal(st[:, 3:4], st[:, 2:3]), 4)
                link(v.tensor_tensor(sc[0:N_HEADS, P + 1:2 * (P + 1):4], sc[0:N_HEADS, P + 1:2 * (P + 1):4], sc[0:N_HEADS, 2 * (P + 1):KEYS], ALU.add), 5)
                link(v.tensor_tensor(sc[0:N_HEADS, P:P + 1], sc[0:N_HEADS, P:P + 1], sc[0:N_HEADS, 2 * P + 1:2 * P + 2], ALU.add), 6)
                link(v.tensor_scalar(sc[0:N_HEADS, 0:2 * P + 1], sc[0:N_HEADS, 0:2 * P + 1], st[:, 3:4], None, ALU.mult), 7)
                v.sem_inc(normed, 1)
                v.wait_ge(p_full, s + 1)
                v.tensor_copy(pt[:, 0:2, :], aux[1][:, 0:2 * P].rearrange("p (a h) -> p a h", a=2)[:, :, 0:N_HEADS])
                v.tensor_copy(pt[0:1, 2, :], aux[1][0:1, 2 * P:2 * P + N_HEADS]).then_inc(p_moved, 1)
                v.wait_ge(o_full, s + 3)
                for e in range(2):
                    half = slice(64 * e, 64 * e + 64)
                    ins = v.tensor_copy(mem.od[half, :, bass.ds(s, 1)],
                                        aux[2][half, 0:16].rearrange("p (f e) -> p f e", e=2)[:, :, e:e + 1])
                link(ins, 8)
            paired(v, 0, NS, sequence)


def gate_output(nc, mem, ten, dram):
    o = mem.actl_at + DT * TOK * 4
    y = []
    for s in range(2):
        t, o = mem.at(f"gated{s}", [P, TOK], o)
        y.append(t)
    aux = mem.aux
    with ExitStack() as ctx:
        def sem(x):
            return nc.alloc_semaphore(f"gate_o_{x}")

        full, prod, hi, lo = sem("transposed"), sem("product"), sem("hi_ready"), sem("lo_ready")
        block = ctx.enter_context(nc.Block())

        @block.tensor
        def _(pe):
            for f in range(DT):
                if f >= 4:
                    pe.wait_ge(prod, f - 3)
                for b in range(4):
                    ins = nc.tensor.transpose(aux[f % 4][:, P * b:P * b + P], mem.o_nat[:, b, P * f:P * f + P], mem.ident[:, :])
                ins.then_inc(full, 1)

        @block.vector
        def _(v):
            def low(f):
                v.wait_ge(hi, f + 1)
                v.tensor_tensor(mem.actl[:, f, :], y[f % 2][:, :], mem.acth[:, f, :].bitcast(F32), ALU.subtract).then_inc(lo, 1)

            for f in range(DT):
                v.wait_ge(full, f + 1)
                if f >= 2:
                    v.wait_ge(lo, f - 1)
                v.tensor_tensor(y[f % 2][:, SEQ:TOK], mem.od[:, f, :], mem.zb[:, f, SEQ:TOK], ALU.mult)
                v.tensor_tensor(y[f % 2][:, 0:SEQ], aux[f % 4][:, :], mem.zb[:, f, 0:SEQ], ALU.mult).then_inc(prod, 1)
                if f >= 1:
                    low(f - 1)
            low(DT - 1)

        @block.scalar
        def _(act):
            for f in range(DT):
                act.wait_ge(prod, f + 1)
                act.activation(mem.acth[:, f, :], y[f % 2][:, :], ACT.Copy).then_inc(hi, 1)


def attn_out(nc, mem, ten, dram):
    residual(nc, mem, "b_out", ten["b_w_out"][0, :, :], 1, mem.acth[:, 0:DT, :], mem.actl[:, 0:DT, :], V_BPOST,
             mem.rest, mem.rest + DT * TOK * 4, natural=True)


def write_y(nc, mem, ten, dram):
    yo, o = mem.at("y_rows", [P, 4, D], mem.acth_at)
    ys, o = mem.at("y_sample_rows", [NS, D], o)
    acc = mem.acc
    with ExitStack() as ctx:
        def sem(x):
            return nc.alloc_semaphore(f"write_{x}")

        full, moved_a, moved_v, stored = sem("transposed"), sem("moved_act"), sem("moved_dve"), sem("stored")
        block = ctx.enter_context(nc.Block())

        @block.tensor
        def _(pe):
            for n in range(5):
                if n >= 2:
                    pe.wait_ge(moved_a if n % 2 == 0 else moved_v, n // 2)
                for f in range(DT):
                    if n < 4:
                        out, src = acc[n % 2][:, P * f:P * f + P], mem.xT[:, f, P * n:P * n + P]
                    else:
                        out, src = acc[0][0:NS, P * f:P * f + P], mem.xT[:, f, SEQ:TOK]
                    ins = nc.tensor.transpose(out, src, mem.ident[:, :])
                ins.then_inc(full, 1)

        @block.scalar
        def _(act):
            for n in (0, 2, 4):
                act.wait_ge(full, n + 1)
                if n < 4:
                    act.activation(yo[:, n, :], acc[0][:, :], ACT.Copy).then_inc(moved_a, 1)
                else:
                    act.activation(ys[:, :], acc[0][0:NS, :], ACT.Copy).then_inc(moved_a, 1)

        @block.vector
        def _(v):
            for n in (1, 3):
                v.wait_ge(full, n + 1)
                v.tensor_copy(yo[:, n, :], acc[1][:, :]).then_inc(moved_v, 1)

        @block.sync
        def _(sp):
            yp = ten["y_prompt"][0, :, :].rearrange("(c j) d -> j c d", j=L)
            for n in range(4):
                sp.wait_ge(moved_a if n % 2 == 0 else moved_v, n // 2 + 1)
                for i in range(2):
                    sp.dma_start(yp[2 * n + i], yo[64 * i:64 * i + 64, n, :]).then_inc(stored, 16)
            sp.wait_ge(moved_a, 3)
            sp.dma_start(ten["y_sample"][:, 0, :], ys[:, :]).then_inc(stored, 16)
            sp.wait_ge(stored, 16 * 9)


INS = ["x_prompt", "x_sample", "state_s5_re", "state_s5_im", "cache_kv", "a_norm_pre", "a_w_in", "a_lam_re",
       "a_lam_im", "a_log_dt", "a_b_re", "a_b_im", "a_c_re", "a_c_im", "a_d", "a_w_glu", "a_b_glu", "a_w_out",
       "a_norm_post", "kv_norm", "w_kv", "b_norm_pre", "b_w_in", "b_w_out", "b_norm_post"]
OUTS = [("y_prompt", (1, SEQ, D)), ("y_sample", (NS, 1, D)), ("p_re", (1, 1, G, ST)), ("p_im", (1, 1, G, ST)),
        ("p_kv", (1, SEQ, 2, N_HEADS, HD)), ("s_re", (1, NS, G, ST)), ("s_im", (1, NS, G, ST)),
        ("s_kv", (NS, SEQ, 2, N_HEADS, HD))]


def trunk(nc, ten, phases=99):
    mem = plan(nc)
    dram = {
        "u": nc.dram_tensor("scratch_u", (W2, TOK), F32, kind="Internal").ap(),
        "y": nc.dram_tensor("scratch_y", (W2, TOK), F32, kind="Internal").ap(),
        "z": nc.dram_tensor("scratch_z", (W2, TOK), F32, kind="Internal").ap(),
        "k": nc.dram_tensor("scratch_k", (CH, G, 15 * CH), F32, kind="Internal").ap(),
    }
    with ExitStack() as ctx:
        mem.acc = [ctx.enter_context(nc.psum_tensor(f"acc{a}", [P, 1024], F32)) for a in range(2)]
        mem.aux = [ctx.enter_context(nc.psum_tensor(f"aux{a}", [P, 512], F32)) for a in range(4)]
        parts = (setup, states, gate_and_scan, outputs, glu, ssm_out,
                 project, token_rows, attention, decode_attention, gate_output, attn_out, write_y)[:phases]
        for group in (parts[:6], parts[6:]):
            with nc.cleanup_on_exit():
                for f in group:
                    f(nc, mem, ten, dram)
    return mem


def constants(np):
    far = np.float32(-1e30)
    n = np.arange(P)
    own = n[None, :] - n[:, None]
    prev = own - P
    tabs = [np.where(own <= 0, own, far), np.where(prev >= -P, prev, far),
            np.where(own <= 0, 4 * own, far),
            np.where((own <= 0) & (own % 4 == 0), 4 * own, far)]
    slopes = np.broadcast_to(np.array(SLOPE, np.float64).reshape(1, 3 * N_HEADS), (P, 3 * N_HEADS))
    row = np.broadcast_to((n[None, :] - P), (P, P))
    return np.concatenate(tabs + [slopes, row], axis=1).astype(np.float32)


def kernel(**inputs):
    import numpy as np
    import concourse.bacc as bacc
    from concourse.bass_utils import run_bass_kernel_spmd

    nc = bacc.Bacc("TRN2", target_bir_lowering=False, num_devices=1)
    arrays, ten = {}, {}
    for name in INS:
        a = np.ascontiguousarray(inputs[name])
        arrays[name] = a
        ten[name] = nc.dram_tensor(name, a.shape, mybir.dt.from_np(a.dtype), kind="ExternalInput").ap()
    arrays["constants"] = constants(np)
    ten["constants"] = nc.dram_tensor("constants", arrays["constants"].shape, F32, kind="ExternalInput").ap()
    for name, shape in OUTS:
        ten[name] = nc.dram_tensor(name, shape, F32, kind="ExternalOutput").ap()
    trunk(nc, ten)
    r = run_bass_kernel_spmd(nc, [arrays], core_ids=[0])
    return tuple(r.results[0][name] for name, _ in OUTS)
```

```python
import math
from contextlib import ExitStack

import concourse.bass as bass
from concourse import mybir

F32 = mybir.dt.float32
F32R = mybir.dt.float32r
ALU = mybir.AluOpType
ACT = mybir.ActivationFunctionType
AX_X = mybir.AxisListType.X

P = 128
D = 1024
DT = D // P
W2 = 2048
WT = W2 // P
SEQ = 512
NS = 8
TOK = SEQ + NS
CUTS = ((0, 256), (256, TOK))
G = 128
NP = G // 2
CH = 16
ST = 64
L = 8
NC = SEQ // L
EPS = 1e-6

C_FIRST = NC + 1
C_LAST = C_FIRST + NS
YC = C_FIRST + NS
UC = C_LAST + NS

V_APRE, V_APOST, V_KV, V_BPRE, V_BPOST, V_D, V_BGLU = 0, 8, 16, 24, 32, 40, 56
NVEC = 88

N_HEADS = 16
HD = 64
SLOPE = [[2.0 ** (-8.0 * (g * N_HEADS + h + 1) / 48) for h in range(N_HEADS)] for g in range(3)]


class Memory:

    def __init__(self, nc):
        self.nc = nc
        self.base = (nc.sbuf_base + 63) // 64 * 64
        self.end = nc.sbuf_usable_end

    def at(self, name, shape, offset, dtype=F32):
        size = 4
        for n in shape[1:]:
            size *= n
        size = (size + 31) // 32 * 32
        assert self.base + offset + size <= self.end, (name, offset, size, self.end - self.base)
        return self.nc.alloc_sbuf_tensor_at(name, shape, dtype, offset=self.base + offset), offset + size


class Dense:

    def __init__(self, ctx, nc, mem, name, units):
        def sem(x):
            return nc.alloc_semaphore(f"{name}_{x}")

        self.nc = nc
        self.mem = mem
        self.units = units
        self.landed = [sem("weights_landed0"), sem("weights_landed1")]
        self.hi_ready = sem("hi_ready")
        self.lo_ready = sem("lo_ready")
        self.unit_read = sem("unit_read")
        self.acc_free = [sem("acc_free0"), sem("acc_free1")]

    def load(self, sp, n, s, block):
        sp.wait_ge(self.lo_ready, n + 1)
        sp.dma_start(self.mem.raw[s][:, :, :], block).then_inc(self.landed[s], 16)

    def split_hi(self, act, n, s, turn):
        act.wait_ge(self.landed[s], 16 * (turn + 1))
        act.wait_ge(self.unit_read, n + 1)
        act.activation(self.mem.wh[s][:, :, :], self.mem.raw[s][:, :, :], ACT.Copy).then_inc(self.hi_ready, 1)

    def split_lo(self, pool, n, s):
        pool.wait_ge(self.hi_ready, n + 1)
        pool.tensor_tensor(self.mem.wl[s][:, :, :], self.mem.raw[s][:, :, :],
                           self.mem.wh[s][:, :, :].bitcast(F32), ALU.subtract).then_inc(self.lo_ready, 1)

    def start(self, pe):
        pe.sem_inc(self.unit_read, 2)
        for a in range(2):
            pe.sem_inc(self.acc_free[a], 1)

    def start_raw(self, pool):
        pool.sem_inc(self.lo_ready, 2)

    def wait_tile(self, eng, t):
        eng.wait_ge(self.unit_read, (t + 1) * self.units + 2)

    def multiply(self, pe, n, s, a, xh, xl, k0, first, last):
        nc, mem = self.nc, self.mem
        pe.wait_ge(self.lo_ready, n + 3)
        for k in range(8):
            terms = ((mem.wh, xh), (mem.wh, xl), (mem.wl, xh))
            for i, (w, x) in enumerate(terms):
                for lo, hi in CUTS:
                    ins = nc.tensor.matmul(
                        mem.acc[a][:, 256 + lo:256 + hi], w[s][:, k, :], x[:, k0 + k, lo:hi],
                        start=first and k == 0 and i == 0, stop=last and k == 7 and i == 2)
        ins.then_inc(self.unit_read, 1)

    def tile(self, pe, t, a, turn, xh, xl):
        pe.wait_ge(self.acc_free[a], turn + 1)
        for u in range(self.units):
            slot = u if self.units == 2 else a
            self.multiply(pe, self.units * t + u, slot, a, xh, xl, 8 * u, u == 0, u == self.units - 1)


def columns(acc):
    return acc[:, 256:256 + TOK]


def blocks(w):
    return w.rearrange("(k p) m -> p k m", p=P)


def cols(i, n=P):
    return bass.ds(i * n, n)


def paired(eng, start, end, body):
    if start % 2:
        body(start, 1, start // 2)
        start += 1
    if end - start >= 4:
        with eng.Fori(start // 2, end // 2) as h:
            body(2 * h, 0, h)
            body(2 * h + 1, 1, h)
    else:
        for i in range(start, end // 2 * 2):
            body(i, i % 2, i // 2)
    if end % 2:
        body(end - 1, 0, end // 2)


def plan(nc):
    mem = Memory(nc)
    o = 0
    mem.ident, o = mem.at("ident", [P, P], o)
    mem.ones, o = mem.at("ones", [P, P], o)
    mem.vec, o = mem.at("vec", [P, NVEC], o)
    mem.cst, o = mem.at("cst", [P, 8], o)
    o = 2048
    mem.xT, o = mem.at("xT", [P, DT, TOK], o)
    mem.acth_at = o
    mem.acth, o = mem.at("act_hi", [P, WT, TOK], o, F32R)
    mem.actl_at = o
    mem.actl, o = mem.at("act_lo", [P, WT, TOK], o, F32R)
    mem.ring_at = o
    mem.raw, mem.wh, mem.wl = [], [], []
    for s in range(2):
        t, o = mem.at(f"raw{s}", [P, 8, P], o)
        mem.raw.append(t)
    for s in range(2):
        t, o = mem.at(f"w_hi{s}", [P, 8, P], o, F32R)
        mem.wh.append(t)
        t, o = mem.at(f"w_lo{s}", [P, 8, P], o, F32R)
        mem.wl.append(t)
    mem.rest = o
    return mem


def setup(nc, mem, ten, dram):
    R = mem.rest
    mem.XH, o = mem.at("XH", [P, C_LAST, 2, NP], R)
    mem.Ct, o = mem.at("Ct", [P, 2, NP, CH], o)
    mem.apow, o = mem.at("apow", [P, L + 1, 2, NP], o)
    mem.p3_at = o
    mem.Bt, o = mem.at("Bt", [P, 2, NP, CH], o)
    mem.cb, o = mem.at("cb", [P, L, 2, NP], o)
    mem.Xs, o = mem.at("Xs", [P, NS, 2, NP], o)
    mem.Ksb, o = mem.at("Ksb", [P, G, CH], o)
    mem.p1_at = o
    a = mem.acth_at
    xtok, a = mem.at("xtok", [P, SEQ // P, D], a)
    xsam, a = mem.at("xsam", [NS, D], a)
    crow, a = mem.at("crow", [P, 2, 8, P], a)
    h0row, a = mem.at("h0row", [NP, 2, NS, P], a)
    vrow, a = mem.at("vrow", [NVEC, P], a)
    lam, a = mem.at("lam", [NP, 2, P], a)
    ldt, a = mem.at("ldt", [NP, 2], a)
    dtr, a = mem.at("dtr", [NP, 2], a)
    lrow, a = mem.at("lrow", [NP, 4, P], a)
    ls, a = mem.at("ls", [P, 4, NP], a)
    w, a = mem.at("disc", [P, 16, NP], a)
    tm, a = mem.at("powtmp", [P, 4, 4, NP], a)
    acc = mem.acc

    with ExitStack() as ctx:
        def sem(x):
            return nc.alloc_semaphore(f"setup_{x}")

        x_in, v_in, c_in, h_in, l_in, b_in = (sem(x) for x in ("x_in", "vec_in", "c_in", "h0_in", "lam_in", "b_in"))
        masks = sem("masks")
        full, free = sem("transposed"), sem("moved")
        rows = sem("rows")
        dve = sem("dve_chain")
        a_in, a_out = sem("act_ask"), sem("act_done")
        block = ctx.enter_context(nc.Block())

        @block.sync
        def _(sp):
            xp = ten["x_prompt"][0, :, :].rearrange("(c j) d -> j c d", j=L)
            for j in range(L):
                sp.dma_start(xtok[64 * (j % 2):64 * (j % 2) + 64, j // 2, :], xp[j]).then_inc(x_in, 16)
            sp.dma_start(xsam[:, :], ten["x_sample"][:, 0, :]).then_inc(x_in, 16)
            for ri, name in enumerate(("a_lam_re", "a_lam_im")):
                sp.dma_start(lam[:, ri, :], ten[name][0, :, :].rearrange("(c e) p -> c (e p)", e=2)).then_inc(l_in, 16)
            sp.dma_start(ldt[:, :], ten["a_log_dt"][0, :].rearrange("(c e) -> c e", e=2)).then_inc(l_in, 16)
            at = 0
            for name in ("a_norm_pre", "a_norm_post", "kv_norm", "b_norm_pre", "b_norm_post", "a_d", "a_b_glu"):
                v = ten[name] if name == "kv_norm" else ten[name][0, :]
                n = v.shape[0] // P
                sp.dma_start(vrow[at:at + n, :], v.rearrange("(f p) -> f p", p=P)).then_inc(v_in, 16)
                at += n
            for ri, name in enumerate(("state_s5_re", "state_s5_im")):
                sp.dma_start(h0row[:, ri, :, :], ten[name][0, :, :, :].rearrange("s (c e) p -> c s (e p)", e=2)).then_inc(h_in, 16)

        @block.gpsimd
        def _(pool):
            pool.memset(mem.ident[:, :], 0.0).then_inc(masks, 1)
            pool.memset(mem.ones[:, :], 1.0)
            pool.memset(mem.cst[:, :], EPS)
            pool.memset(mem.XH[:, 0, :, :], 0.0).then_inc(masks, 1)
            pool.wait_ge(masks, 2)
            pool.affine_select(out=mem.ident[:, :], in_=mem.ident[:, :], compare_op=ALU.not_equal, fill=1.0,
                               base=0, pattern=[[-1, P]], channel_multiplier=1).then_inc(masks, 1)
            for ri, name in enumerate(("a_c_re", "a_c_im")):
                c = ten[name][0, :, :, :].rearrange("(c e) o p -> e c o p", e=2)
                for t in range(8):
                    for e in range(2):
                        pool.dma_start(crow[:, ri, t, 64 * e:64 * e + 64], c[e, 8 * t:8 * t + 8, :, :]).then_inc(c_in, 16)
            for ri, name in enumerate(("a_b_re", "a_b_im")):
                b = ten[name][0, :, :, :].rearrange("(c e) p i -> e p c i", e=2)
                for e in range(2):
                    pool.dma_start(mem.Bt[64 * e:64 * e + 64, ri, :, :], b[e]).then_inc(b_in, 16)
            pool.wait_ge(b_in, 64)

        @block.tensor
        def _(pe):
            pe.wait_ge(masks, 3)
            pe.wait_ge(x_in, 16 * 9)
            for f in range(DT):
                if f >= 2:
                    pe.wait_ge(free, f - 1)
                for b in range(4):
                    nc.tensor.transpose(acc[f % 2][:, P * b:P * b + P], xtok[:, b, P * f:P * f + P], mem.ident[:, :])
                nc.tensor.transpose(acc[f % 2][:, SEQ:SEQ + NS], xsam[:, P * f:P * f + P],
                                    mem.ident[0:NS, 0:NS]).then_inc(full, 1)
            pe.wait_ge(v_in, 16 * 7)
            pe.wait_ge(rows, 1)
            pe.wait_ge(free, 7)
            nc.tensor.transpose(acc[0][:, 0:NVEC], vrow[:, :], mem.ident[0:NVEC, 0:NVEC])
            for q in range(4):
                ins = nc.tensor.transpose(acc[0][:, 512 + NP * q:512 + NP * q + NP], lrow[:, q, :], mem.ident[0:NP, 0:NP])
            ins.then_inc(full, 1)
            pe.wait_ge(c_in, 16 * 32)
            for ri in range(2):
                pe.wait_ge(free, 8 + ri)
                for t in range(8):
                    ins = nc.tensor.transpose(acc[1 - ri][:, P * t:P * t + P], crow[:, ri, t, :], mem.ident[:, :])
                ins.then_inc(full, 1)
            pe.wait_ge(h_in, 32)
            pe.wait_ge(free, 10)
            for ri in range(2):
                for s in range(NS):
                    q = ri * NS + s
                    ins = nc.tensor.transpose(acc[1][:, NP * q:NP * q + NP], h0row[:, ri, s, :], mem.ident[0:NP, 0:NP])
            ins.then_inc(full, 1)

        @block.scalar
        def _(act):
            act.wait_ge(l_in, 48)
            act.activation(dtr[:, :], ldt[:, :], ACT.Exp).then_inc(a_out, 1)
            act.wait_ge(a_in, 1)
            act.activation(w[:, 0, :], ls[:, 0, :], ACT.Exp).then_inc(a_out, 1)
            act.wait_ge(a_in, 2)
            act.activation(w[:, 5:7, :], w[:, 3:5, :], ACT.Sin).then_inc(a_out, 1)

        @block.vector
        def _(v):
            count = [0]

            def link(ins):
                count[0] += 1
                ins.then_inc(dve, 1)
                v.wait_ge(dve, count[0])

            v.wait_ge(a_out, 1)
            dtb = dtr[:, :].unsqueeze(2).broadcast_to([NP, 2, ST])
            for q in range(2):
                v.tensor_tensor(lrow[:, q, :].rearrange("c (e p) -> c e p", e=2),
                                lam[:, q, :].rearrange("c (e p) -> c e p", e=2), dtb, ALU.mult)
            v.tensor_copy(lrow[:, 2:4, :], lam[:, :, :]).then_inc(rows, 1)
            for f in range(DT):
                v.wait_ge(full, f + 1)
                v.tensor_copy(mem.xT[:, f, :], acc[f % 2][:, 0:TOK]).then_inc(free, 1)
            v.wait_ge(full, 9)
            v.tensor_copy(mem.vec[:, :], acc[0][:, 0:NVEC])
            link(v.tensor_copy(ls[:, :, :], acc[0][:, 512:768].rearrange("p (q c) -> p q c", q=4)))
            v.sem_inc(free, 1)
            v.sem_inc(a_in, 1)
            for ri in range(2):
                v.wait_ge(full, 10 + ri)
                v.tensor_copy(mem.Ct[:, ri, :, :], acc[1 - ri][:, :].rearrange("p (c o) -> p c o", o=CH)).then_inc(free, 1)
            v.wait_ge(full, 12)
            for ri in range(2):
                v.tensor_copy(mem.XH[:, C_FIRST:C_LAST, ri, :],
                              acc[1][:, 512 * ri:512 * ri + 512].rearrange("p (s c) -> p s c", s=NS))
            magic = 1.5 * 2.0 ** 23
            parts = (6.28125, 0.0019340515136718750, 2 * math.pi - 6.28125 - 0.0019340515136718750)
            link(v.tensor_scalar(w[:, 1, :], ls[:, 1, :], 1.0 / (2 * math.pi), magic, ALU.mult, ALU.add))
            link(v.tensor_scalar(w[:, 1, :], w[:, 1, :], -magic, None, ALU.add))
            link(v.scalar_tensor_tensor(w[:, 2, :], w[:, 1, :], -parts[0], ls[:, 1, :], ALU.mult, ALU.add))
            link(v.scalar_tensor_tensor(w[:, 2, :], w[:, 1, :], -parts[1], w[:, 2, :], ALU.mult, ALU.add))
            link(v.scalar_tensor_tensor(w[:, 2, :], w[:, 1, :], -parts[2], w[:, 2, :], ALU.mult, ALU.add))
            top = 3.1415925
            link(v.tensor_scalar(w[:, 3, :], w[:, 2, :], top, -top, ALU.min, ALU.max))
            link(v.tensor_scalar(w[:, 7, :], w[:, 3, :], -1.0, None, ALU.mult))
            link(v.tensor_tensor(w[:, 7, :], w[:, 7, :], w[:, 3, :], ALU.max))
            link(v.tensor_scalar(w[:, 4, :], w[:, 7, :], -1.0, math.pi / 2, ALU.mult, ALU.add))
            v.sem_inc(a_in, 1)
            v.memset(mem.apow[:, 0, 0, :], 1.0)
            link(v.memset(mem.apow[:, 0, 1, :], 0.0))
            v.wait_ge(a_out, 3)
            v.tensor_tensor(mem.apow[:, 1, 0, :], w[:, 0, :], w[:, 6, :], ALU.mult)
            link(v.tensor_tensor(mem.apow[:, 1, 1, :], w[:, 0, :], w[:, 5, :], ALU.mult))
            nr, ar, ai, lr, li = w[:, 8, :], mem.apow[:, 1, 0, :], mem.apow[:, 1, 1, :], ls[:, 2, :], ls[:, 3, :]
            v.tensor_scalar(nr, ar, -1.0, None, ALU.add)
            v.tensor_tensor(w[:, 9, :], lr, lr, ALU.mult)
            link(v.tensor_tensor(w[:, 10, :], li, li, ALU.mult))
            link(v.tensor_tensor(w[:, 9, :], w[:, 9, :], w[:, 10, :], ALU.add))
            v.reciprocal(w[:, 11, :], w[:, 9, :])
            v.tensor_tensor(w[:, 12, :], nr, lr, ALU.mult)
            v.tensor_tensor(w[:, 13, :], ai, li, ALU.mult)
            v.tensor_tensor(w[:, 14, :], ai, lr, ALU.mult)
            link(v.tensor_tensor(w[:, 15, :], nr, li, ALU.mult))
            v.tensor_tensor(w[:, 12, :], w[:, 12, :], w[:, 13, :], ALU.add)
            link(v.tensor_tensor(w[:, 14, :], w[:, 14, :], w[:, 15, :], ALU.subtract))
            cr, ci = w[:, 1, :], w[:, 2, :]
            v.tensor_tensor(cr, w[:, 12, :], w[:, 11, :], ALU.mult)
            link(v.tensor_tensor(ci, w[:, 14, :], w[:, 11, :], ALU.mult))
            for n in (1, 2, 4):
                ar, ai = mem.apow[:, 1:n + 1, 0, :], mem.apow[:, 1:n + 1, 1, :]
                br = mem.apow[:, n, 0, :].unsqueeze(1).broadcast_to([P, n, NP])
                bi = mem.apow[:, n, 1, :].unsqueeze(1).broadcast_to([P, n, NP])
                v.tensor_tensor(tm[:, 0, 0:n, :], ar, br, ALU.mult)
                v.tensor_tensor(tm[:, 1, 0:n, :], ai, bi, ALU.mult)
                v.tensor_tensor(tm[:, 2, 0:n, :], ar, bi, ALU.mult)
                link(v.tensor_tensor(tm[:, 3, 0:n, :], ai, br, ALU.mult))
                v.tensor_tensor(mem.apow[:, n + 1:2 * n + 1, 0, :], tm[:, 0, 0:n, :], tm[:, 1, 0:n, :], ALU.subtract)
                link(v.tensor_tensor(mem.apow[:, n + 1:2 * n + 1, 1, :], tm[:, 2, 0:n, :], tm[:, 3, 0:n, :], ALU.add))
            for j in range(L):
                ar, ai = mem.apow[:, L - 1 - j, 0, :], mem.apow[:, L - 1 - j, 1, :]
                v.tensor_tensor(tm[:, 0, 0, :], ar, cr, ALU.mult)
                v.tensor_tensor(tm[:, 1, 0, :], ai, ci, ALU.mult)
                v.tensor_tensor(tm[:, 2, 0, :], ar, ci, ALU.mult)
                link(v.tensor_tensor(tm[:, 3, 0, :], ai, cr, ALU.mult))
                v.tensor_tensor(mem.cb[:, j, 0, :], tm[:, 0, 0, :], tm[:, 1, 0, :], ALU.subtract)
                link(v.tensor_tensor(mem.cb[:, j, 1, :], tm[:, 2, 0, :], tm[:, 3, 0, :], ALU.add))


class Norm:

    def __init__(self, ctx, nc, mem, name, at):
        def sem(x):
            return nc.alloc_semaphore(f"{name}_{x}")

        self.nc, self.mem, self.name = nc, mem, name
        self.sq = []
        self.tmp = []
        for s in range(2):
            t, at = mem.at(f"{name}_sq{s}", [P, TOK], at)
            self.sq.append(t)
        for s in range(2):
            t, at = mem.at(f"{name}_tmp{s}", [P, TOK], at)
            self.tmp.append(t)
        self.root, at = mem.at(f"{name}_root", [P, TOK], at)
        self.rstd, at = mem.at(f"{name}_rstd", [P, TOK], at)
        self.end = at
        self.squared, self.summed = sem("squared"), sem("summed")
        self.rooted, self.rstd_ready = sem("rooted"), sem("rstd_ready")
        self.scaled, self.act_hi, self.act_lo = sem("scaled"), sem("act_hi"), sem("act_lo")

    def square(self, act, f, x):
        if f >= 2:
            act.wait_ge(self.summed, f - 1)
        act.activation(self.sq[f % 2][:, :], x, ACT.Square).then_inc(self.squared, 1)

    def add(self, pe, f):
        pe.wait_ge(self.squared, f + 1)
        for h, (lo, hi) in enumerate(CUTS):
            ins = self.nc.tensor.matmul(self.mem.aux[h][:, 0:hi - lo], self.mem.ones[:, :],
                                        self.sq[f % 2][:, lo:hi], start=f == 0, stop=f == DT - 1)
        ins.then_inc(self.summed, 1)

    def take_root(self, act):
        act.wait_ge(self.summed, DT)
        for h, (lo, hi) in enumerate(CUTS):
            ins = act.activation(self.root[:, lo:hi], self.mem.aux[h][:, 0:hi - lo], ACT.Sqrt,
                                 scale=1.0 / D, bias=self.mem.cst[:, 0:1])
        ins.then_inc(self.rooted, 1)

    def invert(self, v):
        v.wait_ge(self.rooted, 1)
        v.reciprocal(self.rstd[:, :], self.root[:, :]).then_inc(self.rstd_ready, 1)
        v.wait_ge(self.rstd_ready, 1)

    def apply(self, v, gains, first, n0=0):
        mem = self.mem

        def low(f):
            v.wait_ge(self.act_hi, n0 + f + 1)
            v.tensor_tensor(mem.actl[:, first + f, :], self.tmp[f % 2][:, :],
                            mem.acth[:, first + f, :].bitcast(F32), ALU.subtract).then_inc(self.act_lo, 1)

        for f in range(DT):
            if f >= 2:
                v.wait_ge(self.act_lo, n0 + f - 1)
            v.scalar_tensor_tensor(self.tmp[f % 2][:, :], mem.xT[:, f, :], mem.vec[:, gains + f:gains + f + 1],
                                   self.rstd[:, :], ALU.mult, ALU.mult).then_inc(self.scaled, 1)
            if f >= 1:
                low(f - 1)
        low(DT - 1)
        v.wait_ge(self.act_lo, n0 + DT)

    def apply_hi(self, act, first, n0=0):
        for f in range(DT):
            act.wait_ge(self.scaled, n0 + f + 1)
            act.activation(self.mem.acth[:, first + f, :], self.tmp[f % 2][:, :], ACT.Copy).then_inc(self.act_hi, 1)


NB = 8
BG = G // NB
BP = BG // 2


def states(nc, mem, ten, dram):
    U = []
    o = mem.p1_at
    for s in range(2):
        t, o = mem.at(f"Ux{s}", [P, BG, UC], o)
        U.append(t)
    tab, o = mem.at("b_tab", [P, BP, 2, P], o)
    tabT, o = mem.at("b_tabT", [P, BP, 2, P], o)
    a = mem.acth_at + DT * TOK * 4
    cbd, a = mem.at("c_blockdiag", [P, BP, 2, 2, CH], a)
    ust = []
    for s in range(2):
        t, a = mem.at(f"u_out{s}", [P, TOK], a)
        ust.append(t)
    t1, a = mem.at("tab_t1", [P, BP, L, CH], a)
    t2, a = mem.at("tab_t2", [P, BP, L, CH], a)
    assert a <= mem.actl_at
    aux = mem.aux
    su, w = dram["u"], blocks(ten["a_w_in"][0, :, :])
    su_p = su[:, 0:SEQ].rearrange("(g i) (j c) -> j i g c", i=CH, j=L)
    su_s = su[:, SEQ:TOK].rearrange("(g i) s -> i g s", i=CH)

    with ExitStack() as ctx:
        def sem(x):
            return nc.alloc_semaphore(f"states_{x}")

        dn = Dense(ctx, nc, mem, "u_proj", 1)
        nm = Norm(ctx, nc, mem, "norm_a", mem.actl_at + DT * TOK * 4)
        zeroed = sem("zeroed")
        u_copied, u_stored = sem("u_copied"), sem("u_stored")
        U_in = [sem("U_in0"), sem("U_in1")]
        tab_ready, mul_done = sem("tab_ready"), sem("mul_done")
        tr_full, tr_free = sem("tr_full"), sem("tr_free")
        k_full, k_free = sem("k_full"), sem("k_free")
        x_full, x_free = sem("x_full"), sem("x_free")
        block = ctx.enter_context(nc.Block())

        @block.sync
        def _(sp):
            def load(b):
                for i in range(2):
                    dn.load(sp, 2 * b + i, i, w[:, :, cols(2 * b + i)])

            def store_and_gather(b, s):
                for i in range(2):
                    sp.wait_ge(u_copied, 2 * b + i + 1)
                    sp.dma_start(su[cols(2 * b + i), :], ust[i][:, :]).then_inc(u_stored, 16)
                sp.wait_ge(u_stored, 32 * b + 64)
                sp.wait_ge(x_full, 4 * b + 4)
                for j in range(L):
                    sp.dma_start(U[s][CH * j:CH * j + CH, :, 0:NC], su_p[j, :, cols(b, BG), :]).then_inc(U_in[s], 16)
                sp.dma_start(U[s][0:CH, :, C_FIRST:C_LAST], su_s[:, cols(b, BG), :]).then_inc(U_in[s], 16)
                sp.dma_start(U[s][P - CH:P, :, C_LAST:UC], su_s[:, cols(b, BG), :]).then_inc(U_in[s], 16)

            sp.sem_inc(u_stored, 32)
            load(0)
            sp.wait_ge(zeroed, 2)

            def batch(b, q, h):
                load(b)
                store_and_gather(b - 1, 1 - q)
            paired(sp, 1, NB, batch)
            store_and_gather(NB - 1, 1)

        @block.gpsimd
        def _(pool):
            dn.start_raw(pool)
            for s in range(2):
                pool.memset(U[s][:, :, :], 0.0).then_inc(zeroed, 1)
            pool.memset(cbd[:, :, :, :, :], 0.0).then_inc(zeroed, 1)
            paired(pool, 0, WT, lambda n, q, h: dn.split_lo(pool, n, q))

        @block.scalar
        def _(act):
            for f in range(DT):
                nm.square(act, f, mem.xT[:, f, :])
            nm.take_root(act)
            nm.apply_hi(act, 0)
            for n in range(2):
                dn.split_hi(act, n, n, 0)

            def copy_u(m, i, b):
                dn.wait_tile(act, m)
                act.wait_ge(u_stored, 32 * b + 32)
                act.activation(ust[i][:, :], columns(mem.acc[i]), ACT.Copy).then_inc(u_copied, 1)
                act.wait_ge(u_copied, m + 1)
                act.sem_inc(dn.acc_free[i], 1)

            def copy_tab(b):
                for r in range(4):
                    act.wait_ge(tr_full, 4 * b + r + 1)
                    act.activation(tabT[:, 2 * r:2 * r + 2, :, :],
                                   aux[r % 2][:, :].rearrange("p (c z m) -> p c z m", c=2, z=2),
                                   ACT.Copy).then_inc(tr_free, 1)

            def batch(b, q, h):
                for i in range(2):
                    copy_u(2 * b - 2 + i, i, b - 1)
                    dn.split_hi(act, 2 * b + i, i, b)
                copy_tab(b - 1)
            paired(act, 1, NB, batch)
            for i in range(2):
                copy_u(WT - 2 + i, i, NB - 1)
            copy_tab(NB - 1)

        @block.vector
        def _(v):
            v.sem_inc(mul_done, 1)
            nm.invert(v)
            nm.apply(v, V_APRE, 0)
            v.wait_ge(zeroed, 3)

            def pairs(x, b):
                return x[:, cols(b, BP)]

            def build(b):
                def coef(z):
                    return mem.cb[:, :, z, cols(b, BP)].rearrange("p j c -> p c j").unsqueeze(3).broadcast_to([P, BP, L, CH])

                def inp(z):
                    return mem.Bt[:, z, cols(b, BP), :].unsqueeze(2).broadcast_to([P, BP, L, CH])

                for z in range(2):
                    v.wait_ge(mul_done, 6 * b + 3 * z + 1)
                    v.tensor_tensor(t1[:, :, :, :], coef(0), inp(z), ALU.mult).then_inc(mul_done, 1)
                    v.tensor_tensor(t2[:, :, :, :], coef(1), inp(1 - z), ALU.mult).then_inc(mul_done, 1)
                    v.wait_ge(mul_done, 6 * b + 3 * z + 3)
                    v.tensor_tensor(tab[:, :, z, :], t1[:, :, :, :].rearrange("p c j i -> p c (j i)"),
                                    t2[:, :, :, :].rearrange("p c j i -> p c (j i)"),
                                    ALU.subtract if z == 0 else ALU.add).then_inc(mul_done, 1)
                v.wait_ge(mul_done, 6 * b + 7)
                for e in range(2):
                    q = slice(64 * e, 64 * e + 64)
                    v.tensor_copy(cbd[q, :, 0, e, :], mem.Ct[q, 0, cols(b, BP), :])
                    ins = v.tensor_scalar(cbd[q, :, 1, e, :], mem.Ct[q, 1, cols(b, BP), :], -1.0, None, ALU.mult)
                ins.then_inc(tab_ready, 1)

            def copy_k(b):
                v.wait_ge(k_full, b + 1)
                v.tensor_copy(mem.Ksb[:, cols(b, BG), :], aux[2][:, 0:BG * CH].rearrange("p (g o) -> p g o", o=CH)).then_inc(k_free, 1)

            def copy_x(b):
                for r in range(4):
                    v.wait_ge(x_full, 4 * (b + 2) + r + 1)
                    x = aux[2 + r % 2][:, 0:4 * UC].rearrange("p (c z n) -> p c z n", c=2, z=2)
                    for z in range(2):
                        pair = bass.ds(b * BP + 2 * r, 2)
                        v.tensor_copy(mem.XH[:, 1:NC + 1, z, pair].rearrange("p n c -> p c n"), x[:, :, z, 0:NC])
                        ins = v.tensor_copy(mem.Xs[:, :, z, pair].rearrange("p n c -> p c n"), x[:, :, z, C_LAST:UC])
                    ins.then_inc(x_free, 1)

            build(0)
            copy_k(0)

            def batch(b, q, h):
                build(b)
                copy_x(b - 1)
                copy_k(b)
            paired(v, 1, NB, batch)
            copy_x(NB - 1)

        @block.tensor
        def _(pe):
            dn.start(pe)
            pe.sem_inc(x_full, 8)
            pe.sem_inc(x_free, 2)
            pe.sem_inc(tr_free, 2)
            for f in range(DT):
                nm.add(pe, f)
            pe.wait_ge(nm.act_lo, DT)

            def tables(b):
                pe.wait_ge(tab_ready, b + 1)
                for r in range(4):
                    pe.wait_ge(tr_free, 4 * b + r + 1)
                    for c in range(2):
                        for z in range(2):
                            ins = nc.tensor.transpose(aux[r % 2][:, 256 * c + P * z:256 * c + P * z + P],
                                                      tab[:, 2 * r + c, z, :], mem.ident[:, :])
                    ins.then_inc(tr_full, 1)
                pe.wait_ge(x_free, 4 * b + 2)
                for c in range(BP):
                    for z in range(2):
                        ins = nc.tensor.matmul(aux[2][:, 32 * c:32 * c + 32], tab[:, c, z, :],
                                               cbd[:, c, z, :, :].rearrange("p e o -> p (e o)"), start=z == 0, stop=z == 1)
                ins.then_inc(k_full, 1)

            def inputs(b, s, turn):
                pe.wait_ge(U_in[s], 160 * turn + 160)
                pe.wait_ge(tr_free, 4 * b + 6)
                pe.wait_ge(k_free, b + 1)
                for r in range(4):
                    pe.wait_ge(x_free, 4 * b + r + 1)
                    for c in range(2 * r, 2 * r + 2):
                        for z in range(2):
                            for e in range(2):
                                at = UC * (2 * (c % 2) + z)
                                ins = nc.tensor.matmul(aux[2 + r % 2][64 * e:64 * e + 64, at:at + UC],
                                                       tabT[:, c, z, 64 * e:64 * e + 64], U[s][:, 2 * c + e, :],
                                                       start=True, stop=True)
                    ins.then_inc(x_full, 1)

            for i in range(2):
                dn.tile(pe, i, i, 0, mem.acth, mem.actl)
            tables(0)

            def batch(b, q, h):
                for i in range(2):
                    dn.tile(pe, 2 * b + i, i, b, mem.acth, mem.actl)
                inputs(b - 1, 1 - q, h if q == 1 else h - 1)
                tables(b)
            paired(pe, 1, NB, batch)
            inputs(NB - 1, 1, NB // 2 - 1)


def gate_and_scan(nc, mem, ten, dram):
    o = mem.p1_at
    zst = []
    for s in range(2):
        t, o = mem.at(f"z_out{s}", [P, TOK], o)
        zst.append(t)
    a8i, o = mem.at("a8_im_signed", [P, 2, NP], o)
    m1, o = mem.at("scan_m1", [P, 2, NP], o)
    m2, o = mem.at("scan_m2", [P, 2, NP], o)
    so, o = mem.at("state_out", [P, 2, NS + 1, NP], o)
    s1, o = mem.at("state_t1", [P, NS, NP], o)
    s2, o = mem.at("state_t2", [P, NS, NP], o)
    srow, o = mem.at("state_rows", [NP, 2, NS + 1, P], o)
    zer = mem.Bt
    aux = mem.aux
    w = blocks(ten["a_w_in"][0, :, :])
    kk = dram["k"].rearrange("i g (t o) -> i g t o", o=CH)
    with ExitStack() as ctx:
        def sem(x):
            return nc.alloc_semaphore(f"scan_{x}")

        dn = Dense(ctx, nc, mem, "z_proj", 1)
        z_copied, k_stored = sem("z_copied"), sem("k_stored")
        z_stored = [sem("z_stored0"), sem("z_stored1")]
        zeroed, step, fin, ended = sem("zeroed"), sem("step"), sem("final"), sem("states_ready")
        s_full, s_free, s_out = sem("rows_full"), sem("rows_moved"), sem("rows_stored")
        block = ctx.enter_context(nc.Block())

        @block.sync
        def _(sp):
            for s in range(2):
                sp.sem_inc(z_stored[s], 16)
            for n in range(2):
                dn.load(sp, n, n, w[:, :, W2 + P * n:W2 + P * n + P])
            for j in range(L):
                sp.dma_start(kk[:, :, 14 - j, :], mem.Ksb[CH * j:CH * j + CH, :, :]).then_inc(k_stored, 16)
            sp.wait_ge(zeroed, 1)
            for t in range(7):
                sp.dma_start(kk[:, :, t, :], zer[0:CH, :, :, :].rearrange("p z c o -> p (z c) o")).then_inc(k_stored, 16)

            def store(m, i):
                sp.wait_ge(z_copied, m + 1)
                sp.dma_start(dram["z"][cols(m), :], zst[i][:, :]).then_inc(z_stored[i], 16)

            def tile(m, i, h):
                dn.load(sp, m, i, w[:, :, bass.ds(W2 + m * P, P)])
                store(m - 2, i)
            paired(sp, 2, WT, tile)
            for i in range(2):
                store(WT - 2 + i, i)
            sp.wait_ge(s_free, 5)
            for z, (pn, sn) in enumerate((("p_re", "s_re"), ("p_im", "s_im"))):
                sp.dma_start(ten[pn][0, 0, :, :].rearrange("(c e) p -> c (e p)", e=2), srow[:, z, 0, :]).then_inc(s_out, 16)
                sp.dma_start(ten[sn][0, :, :, :].rearrange("s (c e) p -> c s (e p)", e=2), srow[:, z, 1:NS + 1, :]).then_inc(s_out, 16)
            sp.wait_ge(s_out, 64)
            sp.wait_ge(k_stored, 16 * 15)
            for s in range(2):
                sp.wait_ge(z_stored[s], 16 * (WT // 2) + 16)

        @block.gpsimd
        def _(pool):
            dn.start_raw(pool)
            pool.memset(zer[0:CH, :, :, :], 0.0).then_inc(zeroed, 1)
            paired(pool, 0, WT, lambda n, q, h: dn.split_lo(pool, n, q))

        @block.scalar
        def _(act):
            for n in range(2):
                dn.split_hi(act, n, n, 0)

            def silu(m, i, h):
                dn.wait_tile(act, m)
                act.wait_ge(z_stored[i], 16 * h + 16)
                act.activation(zst[i][:, :], columns(mem.acc[i]), ACT.Silu).then_inc(z_copied, 1)
                act.wait_ge(z_copied, m + 1)
                act.sem_inc(dn.acc_free[i], 1)

            def tile(m, i, h):
                silu(m - 2, i, h - 1)
                dn.split_hi(act, m, i, h)
            paired(act, 2, WT, tile)
            for i in range(2):
                silu(WT - 2 + i, i, WT // 2 - 1)

        @block.vector
        def _(v):
            a8 = mem.apow[:, L, 0, :].unsqueeze(1).broadcast_to([P, 2, NP])
            v.tensor_scalar(a8i[:, 0, :], mem.apow[:, L, 1, :], -1.0, None, ALU.mult)
            v.tensor_copy(a8i[:, 1, :], mem.apow[:, L, 1, :]).then_inc(step, 1)
            v.wait_ge(step, 1)
            with v.Fori(0, NC // 4) as h:
                for q in range(4):
                    c = 4 * h + q
                    was = mem.XH[:, bass.ds(c, 1), :, :].rearrange("p n z c -> p (n z) c")
                    now = mem.XH[:, bass.ds(c + 1, 1), :, :].rearrange("p n z c -> p (n z) c")
                    v.tensor_tensor(m1[:, :, :], was, a8, ALU.mult)
                    v.tensor_tensor(m2[:, 0, :], was[:, 1, :], a8i[:, 0, :], ALU.mult)
                    v.tensor_tensor(m2[:, 1, :], was[:, 0, :], a8i[:, 1, :], ALU.mult).then_inc(step, 1)
                    v.wait_ge(step, 3 * c + 2)
                    v.tensor_tensor(m1[:, :, :], m1[:, :, :], m2[:, :, :], ALU.add).then_inc(step, 1)
                    v.wait_ge(step, 3 * c + 3)
                    v.tensor_tensor(now, now, m1[:, :, :], ALU.add).then_inc(step, 1)
                    v.wait_ge(step, 3 * c + 4)
            count = [0]

            def link(ins):
                count[0] += 1
                ins.then_inc(fin, 1)
                v.wait_ge(fin, count[0])

            hr = mem.XH[:, C_FIRST:C_LAST, 0, :]
            hi = mem.XH[:, C_FIRST:C_LAST, 1, :]
            ar = mem.apow[:, 1, 0, :].unsqueeze(1).broadcast_to([P, NS, NP])
            ai = mem.apow[:, 1, 1, :].unsqueeze(1).broadcast_to([P, NS, NP])
            for z, (x, y, op) in enumerate(((hr, hi, ALU.subtract), (hi, hr, ALU.add))):
                v.tensor_copy(so[:, z, 0, :], mem.XH[:, NC, z, :])
                v.tensor_tensor(s1[:, :, :], x, ar, ALU.mult)
                link(v.tensor_tensor(s2[:, :, :], y, ai, ALU.mult))
                link(v.tensor_tensor(s1[:, :, :], s1[:, :, :], s2[:, :, :], op))
                link(v.tensor_tensor(so[:, z, 1:NS + 1, :], s1[:, :, :], mem.Xs[:, :, z, :], ALU.add))
            v.sem_inc(ended, 1)
            rows = srow[:, :, :, :].rearrange("p z s m -> p (z s) m")
            for r in range(5):
                n = min(4, 18 - 4 * r)
                v.wait_ge(s_full, r + 1)
                v.tensor_copy(rows[:, 4 * r:4 * r + n, :],
                              aux[r % 4][0:NP, 0:P * n].rearrange("p (s m) -> p s m", m=P)).then_inc(s_free, 1)

        @block.tensor
        def _(pe):
            dn.start(pe)
            paired(pe, 0, WT, lambda m, a, h: dn.tile(pe, m, a, h, mem.acth, mem.actl))
            pe.wait_ge(ended, 1)
            flat = so[:, :, :, :].rearrange("p z s c -> p (z s) c")
            for r in range(5):
                if r == 4:
                    pe.wait_ge(s_free, 1)
                for q in range(4 * r, min(4 * r + 4, 18)):
                    ins = nc.tensor.transpose(aux[r % 4][0:NP, P * (q % 4):P * (q % 4) + P], flat[:, q, :], mem.ident[:, :])
                ins.then_inc(s_full, 1)


def outputs(nc, mem, ten, dram):
    o = mem.p3_at
    T, U, C8, Y, hb, yt, ut = [], [], [], [], [], [], []
    for s in range(2):
        for name, shape, l in (("toeplitz", [P, BG, P], T), ("Uy", [P, BG, YC], U), ("Y", [P, BG, YC], Y),
                               ("h_dense", [P, 2, BP, YC], hb), ("y_in", [P, TOK], yt), ("u_in", [P, TOK], ut)):
            t, o = mem.at(f"{name}{s}", shape, o)
            l.append(t)
    o = mem.ring_at
    for s in range(2):
        t, o = mem.at(f"c_tab{s}", [P, BP, 2, P], o)
        C8.append(t)
    t1, o = mem.at("c_t1", [P, BP, L, CH], o)
    t2, o = mem.at("c_t2", [P, BP, L, CH], o)
    assert o <= mem.rest
    aux = mem.aux
    kk, su, sy = dram["k"], dram["u"], dram["y"]
    su_p = su[:, 0:SEQ].rearrange("(g i) (j c) -> j i g c", i=CH, j=L)
    su_s = su[:, SEQ:TOK].rearrange("(g i) s -> i g s", i=CH)
    sy_p = sy[:, 0:SEQ].rearrange("(g i) (j c) -> j i g c", i=CH, j=L)
    sy_s = sy[:, SEQ:TOK].rearrange("(g i) s -> i g s", i=CH)
    with ExitStack() as ctx:
        def sem(x):
            return nc.alloc_semaphore(f"outputs_{x}")

        zeroed = sem("zeroed")
        T_in = [sem("T_in0"), sem("T_in1")]
        U_in = [sem("U_in0"), sem("U_in1")]
        y_full, y_copied = sem("y_full"), sem("y_copied")
        y_stored = [sem("y_stored0"), sem("y_stored1")]
        y_in, u_in = [sem("y_in0"), sem("y_in1")], [sem("u_in0"), sem("u_in1")]
        mul, tab, dense = sem("mul_done"), sem("tab_ready"), sem("h_dense")
        skip, gel, hi_r, lo_r = sem("skip_added"), sem("gelu_done"), sem("hi_ready"), sem("lo_ready")
        block = ctx.enter_context(nc.Block())

        @block.sync
        def _(sp):
            for s in range(2):
                sp.sem_inc(y_stored[s], 16)
            sp.wait_ge(zeroed, 2)

            def load(b, s):
                sp.wait_ge(y_full, 2 * b + 2)
                for j in range(L):
                    sp.dma_start(T[s][CH * j:CH * j + CH, :, :], kk[:, cols(b, BG), CH * (7 - j):CH * (15 - j)]).then_inc(T_in[s], 16)
                    sp.dma_start(U[s][CH * j:CH * j + CH, :, 0:NC], su_p[j, :, cols(b, BG), :]).then_inc(U_in[s], 16)
                sp.dma_start(U[s][0:CH, :, C_FIRST:C_LAST], su_s[:, cols(b, BG), :]).then_inc(U_in[s], 16)

            def fetch(b, s, turn):
                sp.wait_ge(y_stored[s], 144 * turn + 160)
                for i in range(2):
                    m = 2 * b + i
                    sp.wait_ge(lo_r, m + 1)
                    sp.dma_start(yt[i][:, :], sy[cols(m), :]).then_inc(y_in[i], 16)
                    sp.dma_start(ut[i][:, :], su[cols(m), :]).then_inc(u_in[i], 16)

            load(0, 0)
            load(1, 1)

            def batch(b, q, h):
                load(b, q)
                fetch(b - 2, q, h - 1)
            paired(sp, 2, NB, batch)
            fetch(NB - 2, 0, NB // 2 - 1)
            fetch(NB - 1, 1, NB // 2 - 1)

        @block.gpsimd
        def _(pool):
            for s in range(2):
                pool.memset(U[s][:, :, :], 0.0).then_inc(zeroed, 1)

        @block.tensor
        def _(pe):
            pe.sem_inc(y_full, 4)

            def batch(b, s, turn):
                pe.wait_ge(T_in[s], 128 * turn + 128)
                pe.wait_ge(U_in[s], 144 * turn + 144)
                pe.wait_ge(tab, b + 1)
                pe.wait_ge(dense, b + 1)
                for r in range(2):
                    pe.wait_ge(y_copied, 4 * b + 2 * r + 2)
                    for c in range(4 * r, 4 * r + 4):
                        y = [aux[2 * r + e][:, P * (c % 4):P * (c % 4) + YC] for e in range(2)]
                        for e in range(2):
                            nc.tensor.matmul(y[e], T[s][:, 2 * c + e, :], U[s][:, 2 * c + e, 0:YC], start=True, stop=False)
                        for z in range(2):
                            for e in range(2):
                                rows = slice(64 * e, 64 * e + 64)
                                ins = nc.tensor.matmul(y[e], C8[s][rows, c, z, :], hb[s][rows, z, c, :],
                                                       start=False, stop=z == 1)
                    ins.then_inc(y_full, 1)
            paired(pe, 0, NB, batch)

        @block.scalar
        def _(act):
            def copy_y(b, s, turn):
                act.wait_ge(y_stored[s], 144 * turn + 16)
                for r in range(2):
                    act.wait_ge(y_full, 2 * b + 5 + r)
                    for e in range(2):
                        act.activation(Y[s][:, 8 * r:8 * r + 8, :].rearrange("p (c e) n -> p e c n", e=2)[:, e, :, :],
                                       aux[2 * r + e][:, :].rearrange("p (g n) -> p g n", g=4)[:, :, 0:YC],
                                       ACT.Copy).then_inc(y_copied, 1)

            def store_y(b, s):
                act.wait_ge(y_copied, 4 * b + 8)
                for j in range(L):
                    act.dma_start(sy_p[j, :, cols(b, BG), :], Y[s][CH * j:CH * j + CH, :, 0:NC]).then_inc(y_stored[s], 16)
                act.dma_start(sy_s[:, cols(b, BG), :], Y[s][0:CH, :, C_FIRST:C_LAST]).then_inc(y_stored[s], 16)

            def gelu(m, i):
                act.wait_ge(skip, m + 2)
                act.activation(yt[i][:, :], yt[i][:, :], ACT.Gelu_apprx_tanh).then_inc(gel, 1)
                act.wait_ge(gel, m + 1)
                act.activation(mem.acth[:, bass.ds(m, 1), :].rearrange("p o n -> p (o n)"), yt[i][:, :], ACT.Copy).then_inc(hi_r, 1)

            act.sem_inc(y_copied, 4)
            for b in range(2):
                copy_y(b, b, 0)
                store_y(b, b)

            def batch(b, q, h):
                for i in range(2):
                    gelu(2 * b - 4 + i, i)
                copy_y(b, q, h)
                store_y(b, q)
            paired(act, 2, NB, batch)
            for m in range(WT - 4, WT):
                gelu(m, m % 2)

        @block.vector
        def _(v):
            v.sem_inc(lo_r, 2)
            v.sem_inc(skip, 1)
            v.sem_inc(mul, 1)

            def build(b, s):
                def power(z):
                    return mem.apow[:, 1:L + 1, z, cols(b, BP)].rearrange("p j c -> p c j").unsqueeze(3).broadcast_to([P, BP, L, CH])

                def c(z):
                    return mem.Ct[:, z, cols(b, BP), :].unsqueeze(2).broadcast_to([P, BP, L, CH])

                v.wait_ge(y_full, 2 * b + 2)
                for z in range(2):
                    v.wait_ge(mul, 6 * b + 3 * z + 1)
                    v.tensor_tensor(t1[:, :, :, :], c(z), power(0), ALU.mult).then_inc(mul, 1)
                    v.tensor_tensor(t2[:, :, :, :], c(1 - z), power(1), ALU.mult).then_inc(mul, 1)
                    v.wait_ge(mul, 6 * b + 3 * z + 3)
                    a, d = (x[:, :, :, :].rearrange("p c j i -> p c (j i)") for x in (t1, t2))
                    if z == 0:
                        v.tensor_tensor(C8[s][:, :, 0, :], a, d, ALU.subtract).then_inc(mul, 1)
                    else:
                        v.scalar_tensor_tensor(C8[s][:, :, 1, :], a, -1.0, d, ALU.mult, ALU.subtract).then_inc(mul, 1)
                v.wait_ge(mul, 6 * b + 7)
                for z in range(2):
                    ins = v.tensor_copy(hb[s][:, z, :, :], mem.XH[:, 0:YC, z, cols(b, BP)].rearrange("p n c -> p c n"))
                ins.then_inc(dense, 1)
                v.wait_ge(dense, b + 1)
                v.sem_inc(tab, 1)

            def add_skip(m, i, turn):
                v.wait_ge(y_in[i], 16 * turn + 16)
                v.wait_ge(u_in[i], 16 * turn + 16)
                v.scalar_tensor_tensor(yt[i][:, :], ut[i][:, :], mem.vec[:, bass.ds(V_D + m, 1)], yt[i][:, :],
                                       ALU.mult, ALU.add).then_inc(skip, 1)

            def low(m, i):
                v.wait_ge(hi_r, m + 1)
                at = bass.ds(m, 1)
                v.tensor_tensor(mem.actl[:, at, :].rearrange("p o n -> p (o n)"), yt[i][:, :],
                                mem.acth[:, at, :].rearrange("p o n -> p (o n)").bitcast(F32), ALU.subtract).then_inc(lo_r, 1)

            build(0, 0)
            build(1, 1)

            def batch(b, q, h):
                build(b, q)
                for i in range(2):
                    add_skip(2 * b - 4 + i, i, b - 2)
                for i in range(2):
                    low(2 * b - 4 + i, i)
            paired(v, 2, NB, batch)
            for m in range(WT - 4, WT, 2):
                for i in range(2):
                    add_skip(m + i, i, m // 2)
                for i in range(2):
                    low(m + i, i)


def glu(nc, mem, ten, dram):
    o = mem.rest
    mem.yh, o = mem.at("y_hi", [P, WT, TOK], o, F32R)
    mem.yl, o = mem.at("y_lo", [P, WT, TOK], o, F32R)
    mem.glu_end = o
    sg, zt, yt = [], [], []
    for s in range(2):
        for name, l in (("sig", sg), ("z_in", zt), ("y_f32", yt)):
            t, o = mem.at(f"{name}{s}", [P, TOK], o)
            l.append(t)
    w = blocks(ten["a_w_glu"][0, :, :])
    with ExitStack() as ctx:
        def sem(x):
            return nc.alloc_semaphore(f"gate_{x}")

        dn = Dense(ctx, nc, mem, "glu", 2)
        z_in = [sem("z_in0"), sem("z_in1")]
        sig, gated, prod = sem("sigmoid"), sem("gated"), sem("product")
        hi_r, lo_r = sem("hi_ready"), sem("lo_ready")
        block = ctx.enter_context(nc.Block())

        @block.sync
        def _(sp):
            def tile(i, s, h):
                for a in range(2):
                    for u in range(2):
                        at = bass.ds((i + WT) * P - a * W2, P)
                        dn.load(sp, 4 * i + 2 * a + u, u, w[:, 8 * u:8 * u + 8, at])
                sp.wait_ge(prod, i + 1)
                sp.dma_start(zt[s][:, :], dram["z"][cols(i), :]).then_inc(z_in[s], 16)
            sp.sem_inc(prod, 2)
            paired(sp, 0, WT, tile)

        @block.gpsimd
        def _(pool):
            dn.start_raw(pool)
            paired(pool, 0, 4 * WT, lambda n, q, h: dn.split_lo(pool, n, q))

        @block.tensor
        def _(pe):
            dn.start(pe)
            paired(pe, 0, 2 * WT, lambda m, a, h: dn.tile(pe, m, a, h, mem.acth, mem.actl))

        @block.scalar
        def _(act):
            def high(i, s):
                act.wait_ge(prod, i + 3)
                act.activation(mem.yh[:, bass.ds(i, 1), :].rearrange("p o n -> p (o n)"), yt[s][:, :], ACT.Copy).then_inc(hi_r, 1)

            def tile(i, s, h, first=False):
                dn.split_hi(act, 4 * i, 0, 2 * i)
                dn.split_hi(act, 4 * i + 1, 1, 2 * i)
                if not first:
                    high(i - 1, 1 - s)
                dn.split_hi(act, 4 * i + 2, 0, 2 * i + 1)
                dn.wait_tile(act, 2 * i)
                act.wait_ge(gated, i)
                act.activation(sg[s][:, :], columns(mem.acc[0]), ACT.Sigmoid,
                               bias=mem.vec[:, bass.ds(V_BGLU + WT + i, 1)]).then_inc(dn.acc_free[0], 1)
                dn.split_hi(act, 4 * i + 3, 1, 2 * i + 1)
            act.sem_inc(gated, 1)
            tile(0, 0, 0, True)
            paired(act, 1, WT, tile)
            high(WT - 1, 1)

        @block.vector
        def _(v):
            def tile(i, s, h):
                dn.wait_tile(v, 2 * i + 1)
                v.wait_ge(dn.acc_free[0], i + 2)
                v.scalar_tensor_tensor(sg[s][:, :], columns(mem.acc[1]), mem.vec[:, bass.ds(V_BGLU + i, 1)],
                                       sg[s][:, :], ALU.add, ALU.mult).then_inc(dn.acc_free[1], 1)
                v.wait_ge(dn.acc_free[1], i + 2)
                v.sem_inc(gated, 1)
                v.wait_ge(z_in[s], 16 * h + 16)
                v.wait_ge(lo_r, i + 1)
                v.tensor_tensor(yt[s][:, :], sg[s][:, :], zt[s][:, :], ALU.mult).then_inc(prod, 1)
                v.wait_ge(hi_r, i + 1)
                at = bass.ds(i, 1)
                v.tensor_tensor(mem.yl[:, at, :].rearrange("p o n -> p (o n)"), yt[s][:, :],
                                mem.yh[:, at, :].rearrange("p o n -> p (o n)").bitcast(F32), ALU.subtract).then_inc(lo_r, 1)
            v.sem_inc(lo_r, 2)
            paired(v, 0, WT, tile)


def residual(nc, mem, name, ten_w, units, xh, xl, gains, o_at, norm_at, natural=False):
    ot, o = mem.at(f"{name}_o", [P, DT, TOK], o_at)
    w = blocks(ten_w)
    with ExitStack() as ctx:
        def sem(x):
            return nc.alloc_semaphore(f"{name}_{x}")

        dn = Dense(ctx, nc, mem, name, units)
        nm = Norm(ctx, nc, mem, name + "_post", norm_at)
        added = sem("added")
        block = ctx.enter_context(nc.Block())

        @block.sync
        def _(sp):
            def tile(m, a, h):
                for u in range(units):
                    s = u if units == 2 else a
                    dn.load(sp, units * m + u, s, w[:, 8 * u:8 * u + 8, cols(m)])
            paired(sp, 0, DT, tile)

        @block.gpsimd
        def _(pool):
            dn.start_raw(pool)
            paired(pool, 0, units * DT, lambda n, q, h: dn.split_lo(pool, n, q))

        @block.scalar
        def _(act):
            paired(act, 0, units * DT, lambda n, q, h: dn.split_hi(act, n, q, h))
            for f in range(DT):
                act.wait_ge(dn.acc_free[f % 2], f // 2 + 2)
                nm.square(act, f, ot[:, f, :])
            nm.take_root(act)

        @block.tensor
        def _(pe):
            dn.start(pe)
            paired(pe, 0, DT, lambda m, a, h: dn.tile(pe, m, a, h, xh, xl))
            for f in range(DT):
                nm.add(pe, f)

        @block.vector
        def _(v):
            def tile(m, a, h):
                dn.wait_tile(v, m)
                x = ot[:, bass.ds(m, 1), :].rearrange("p o n -> p (o n)")
                if natural:
                    v.tensor_copy(x[:, 0:SEQ].rearrange("p (j c) -> p j c", j=L),
                                  columns(mem.acc[a])[:, 0:SEQ].rearrange("p (c j) -> p j c", j=L))
                    v.tensor_copy(x[:, SEQ:TOK], columns(mem.acc[a])[:, SEQ:TOK]).then_inc(dn.acc_free[a], 1)
                else:
                    v.tensor_copy(x, columns(mem.acc[a])).then_inc(dn.acc_free[a], 1)
            paired(v, 0, DT, tile)
            nm.invert(v)
            for f in range(DT):
                if f >= 2:
                    v.wait_ge(added, 2 * f - 2)
                v.scalar_tensor_tensor(nm.tmp[f % 2][:, :], ot[:, f, :], mem.vec[:, gains + f:gains + f + 1],
                                       nm.rstd[:, :], ALU.mult, ALU.mult).then_inc(added, 1)
                v.wait_ge(added, 2 * f + 1)
                v.tensor_tensor(mem.xT[:, f, :], mem.xT[:, f, :], nm.tmp[f % 2][:, :], ALU.add).then_inc(added, 1)
            v.wait_ge(added, 2 * DT)


def ssm_out(nc, mem, ten, dram):
    residual(nc, mem, "a_out", ten["a_w_out"][0, :, :], 2, mem.yh, mem.yl, V_APOST, mem.acth_at, mem.glu_end)


def project(nc, mem, ten, dram):
    o = mem.rest
    mem.kv, o = mem.at("kvT", [P, 2 * DT, TOK], o)
    mem.v_at = mem.rest + DT * TOK * 4
    mem.q, o = mem.at("qT", [P, 3 * DT, TOK], o)
    mem.zb, o = mem.at("zb", [P, DT, TOK], o)
    mem.stat_at = o
    wk, wb = blocks(ten["w_kv"]), blocks(ten["b_w_in"][0, :, :])

    def in_token_order(op, out, tile, a, dn, *func, **scale):
        x = out[:, bass.ds(tile, 1), :].rearrange("p o n -> p (o n)")
        y = columns(mem.acc[a])
        op(x[:, 0:SEQ].rearrange("p (c j) -> p j c", j=L), y[:, 0:SEQ].rearrange("p (j c) -> p j c", j=L), *func, **scale)
        op(x[:, SEQ:TOK], y[:, SEQ:TOK], *func, **scale).then_inc(dn.acc_free[a], 1)

    with ExitStack() as ctx:
        def sem(x):
            return nc.alloc_semaphore(f"proj_{x}")

        dn = Dense(ctx, nc, mem, "proj", 1)
        nm = Norm(ctx, nc, mem, "norm_kv", mem.rest)
        block = ctx.enter_context(nc.Block())

        @block.sync
        def _(sp):
            paired(sp, 0, 2 * DT, lambda m, s, h: dn.load(sp, m, s, wk[:, :, cols(m)]))
            paired(sp, 2 * DT, 6 * DT, lambda m, s, h: dn.load(sp, m, s, wb[:, :, bass.ds(m * P - 2 * D, P)]))

        @block.gpsimd
        def _(pool):
            dn.start_raw(pool)
            paired(pool, 0, 6 * DT, lambda n, q, h: dn.split_lo(pool, n, q))

        @block.tensor
        def _(pe):
            dn.start(pe)
            for f in range(DT):
                nm.add(pe, f)
            pe.wait_ge(nm.act_lo, 2 * DT)
            paired(pe, 0, 2 * DT, lambda m, a, h: dn.tile(pe, m, a, h, mem.acth[:, 0:DT, :], mem.actl[:, 0:DT, :]))
            paired(pe, 2 * DT, 6 * DT, lambda m, a, h: dn.tile(pe, m, a, h, mem.acth[:, DT:, :], mem.actl[:, DT:, :]))

        @block.scalar
        def _(act):
            for f in range(DT):
                nm.square(act, f, mem.xT[:, f, :])
            nm.take_root(act)
            nm.apply_hi(act, 0)
            nm.apply_hi(act, DT, DT)
            paired(act, 0, 2 * DT + 2, lambda n, q, h: dn.split_hi(act, n, q, h))

            def q_tile(m, a, h):
                dn.wait_tile(act, m - 2)
                in_token_order(act.activation, mem.q, m - 2 - 2 * DT, a, dn, ACT.Copy, scale=HD ** -0.5)
                dn.split_hi(act, m, a, h)

            def z_tile(m, a):
                dn.wait_tile(act, m)
                in_token_order(act.activation, mem.zb, m - 5 * DT, a, dn, ACT.Silu)

            def z_next(m, a, h):
                z_tile(m - 2, a)
                dn.split_hi(act, m, a, h)
            paired(act, 2 * DT + 2, 5 * DT + 2, q_tile)
            paired(act, 5 * DT + 2, 6 * DT, z_next)
            z_tile(6 * DT - 2, 0)
            z_tile(6 * DT - 1, 1)

        @block.vector
        def _(v):
            nm.invert(v)
            nm.apply(v, V_KV, 0)
            nm.apply(v, V_BPRE, DT, DT)

            def kv_tile(m, a, h):
                dn.wait_tile(v, m)
                in_token_order(v.tensor_copy, mem.kv, m, a, dn)
            paired(v, 0, 2 * DT, kv_tile)


def block_tokens(x, b):
    return x[:, P * b:P * b + P]


def residue_tokens(x, r):
    return x[:, r:r + 4 * (P - 1) + 1:4]


def token_rows(nc, mem, ten, dram):
    o = mem.acth_at
    mem.vnat, o = mem.at("v_block", [P, 4, D], o)
    mem.vres, o = mem.at("v_residue", [P, 4, D], o)
    mem.attn_at = o
    knat, o = mem.at("k_block", [P, 4, D], o)
    kvnew, o = mem.at("kv_new", [NS, 2, D], o)
    qnew, o = mem.at("q_new", [NS, 3, D], o)
    assert o <= mem.rest
    acc = mem.acc
    with ExitStack() as ctx:
        def sem(x):
            return nc.alloc_semaphore(f"rows_{x}")

        full, moved_a, moved_v, stored = sem("full"), sem("moved_act"), sem("moved_dve"), sem("stored")
        block = ctx.enter_context(nc.Block())

        rounds = [("kb", b) for b in range(4)] + [("vb", b) for b in range(4)] + [("vr", r) for r in range(4)] + \
                 [("new", z) for z in range(2)] + [("q", g) for g in range(3)]

        def target(kind, i):
            return {"kb": knat, "vb": mem.vnat, "vr": mem.vres, "new": kvnew, "q": qnew}[kind][:, i, :]

        @block.tensor
        def _(pe):
            for n, (kind, i) in enumerate(rounds):
                if n >= 2:
                    pe.wait_ge(moved_a if n % 2 == 0 else moved_v, n // 2)
                for f in range(DT):
                    if kind == "q":
                        src = mem.q[:, DT * i + f, :]
                    else:
                        src = mem.kv[:, f + (DT if kind[0] == "v" or (kind, i) == ("new", 1) else 0), :]
                    if kind in ("new", "q"):
                        out, src = acc[n % 2][0:NS, P * f:P * f + P], src[:, SEQ:TOK]
                    else:
                        out = acc[n % 2][:, P * f:P * f + P]
                        src = residue_tokens(src[:, 0:SEQ], i) if kind == "vr" else block_tokens(src[:, 0:SEQ], i)
                    ins = nc.tensor.transpose(out, src, mem.ident[:, :])
                ins.then_inc(full, 1)

        @block.scalar
        def _(act):
            for n in range(0, len(rounds), 2):
                rows = NS if rounds[n][0] in ("new", "q") else P
                act.wait_ge(full, n + 1)
                act.activation(target(*rounds[n]), acc[0][0:rows, :], ACT.Copy).then_inc(moved_a, 1)

        @block.vector
        def _(v):
            for n in range(1, len(rounds), 2):
                rows = NS if rounds[n][0] in ("new", "q") else P
                v.wait_ge(full, n + 1)
                v.tensor_copy(target(*rounds[n]), acc[1][0:rows, :]).then_inc(moved_v, 1)

        @block.sync
        def _(sp):
            out = ten["p_kv"][0, :, :, :, :].rearrange("t z h d -> z t (h d)")
            for z, x in enumerate((knat, mem.vnat)):
                sp.wait_ge(moved_a, 2 * z + 2)
                sp.wait_ge(moved_v, 2 * z + 2)
                for b in range(4):
                    sp.dma_start(out[z, P * b:P * b + P, :], x[:, b, :]).then_inc(stored, 16)
            sp.wait_ge(moved_a, 7)
            sp.wait_ge(moved_v, 7)
            sp.dma_start(ten["s_kv"][:, SEQ - 1, :, :, :].rearrange("s z h d -> s z (h d)"), kvnew[:, :, :]).then_inc(stored, 16)
            sp.wait_ge(moved_a, 9)
            sp.wait_ge(moved_v, 8)
            sp.dma_start(dram["q"], qnew[:, :, :]).then_inc(stored, 16)
            sp.wait_ge(stored, 16 * 10)


HALVES = ((0, 12), (12, N_HEADS))


def attention(nc, mem, ten, dram):
    o = mem.attn_at
    far, o = mem.at("far_res", [P, 4, N_HEADS, HD + 2], o)
    near, o = mem.at("far_nat", [P, 4, N_HEADS, HD + 2], o)
    S, PT = [], []
    for s in range(2):
        t, o = mem.at(f"scores{s}", [P, 4, 2, P], o)
        S.append(t)
    for s in range(2):
        t, o = mem.at(f"probsT{s}", [P, 8, P], o)
        PT.append(t)
    dist, o = mem.at("distances", [P, 4, P], o)
    slope, o = mem.at("slopes", [P, 3 * N_HEADS], o)
    assert o <= mem.rest
    mem.o_nat, _ = mem.at("o_nat", [P, 4, D], mem.v_at)
    o = mem.stat_at
    nmax, o = mem.at("neg_max", [P, 4, 4], o)
    e12, o = mem.at("far_scale", [P, 4, 4], o)
    l0, o = mem.at("near_sum", [P, 4, 4], o)
    den, o = mem.at("denominator", [P, 2, 4], o)
    on, o = mem.at("joined", [P, 4, HD], o)
    aux, acc = mem.aux, mem.acc
    const = ten["constants"]

    with ExitStack() as ctx:
        def sem(x):
            return nc.alloc_semaphore(f"attn_{x}")

        c_in = sem("constants_in")
        s_full, biased, maxed, exped, summed = sem("scores"), sem("biased"), sem("maxed"), sem("exped"), sem("summed")
        t_full, t_moved, o_full, o_moved = sem("transposed"), sem("t_moved"), sem("out_full"), sem("out_moved")
        moved = [sem("far_moved0"), sem("far_moved1")]
        dve = sem("dve_chain")
        block = ctx.enter_context(nc.Block())
        units = [("far", h) for h in range(N_HEADS)] + [("near", h) for h in range(N_HEADS)]

        @block.sync
        def _(sp):
            sp.dma_start(dist[:, :, :], const[:, 0:4 * P].rearrange("p (a k) -> p a k", a=4)).then_inc(c_in, 16)
            sp.dma_start(slope[:, :], const[:, 4 * P:4 * P + 3 * N_HEADS]).then_inc(c_in, 16)
            for part, (h0, h1) in enumerate(HALVES):
                sp.wait_ge(o_moved, h1)
                for r in range(4):
                    for b in range(4):
                        sp.dma_start(near[r:r + 4 * 31 + 1:4, b, h0:h1, :],
                                     far[32 * b:32 * b + 32, r, h0:h1, :]).then_inc(moved[part], 16)

        @block.tensor
        def _(pe):
            def rows(h):
                return slice(HD * (h % 2), HD * (h % 2) + HD)

            def scores(n):
                kind, h = units[n]
                if n >= 2:
                    pe.wait_ge(biased, n - 1)
                q, k = mem.q[rows(h), :, 0:SEQ], mem.kv[rows(h), h // 2, 0:SEQ]
                out = acc[n % 2][:, :].rearrange("p (i g k) -> p i g k", i=4, g=2)
                for i in range(4):
                    if kind == "far":
                        for g in range(2):
                            ins = nc.tensor.matmul(out[:, i, g, :], residue_tokens(q[:, DT * (1 + g) + h // 2, :], i),
                                                   residue_tokens(k, i), start=True, stop=True)
                    else:
                        for g in range(2 if i else 1):
                            ins = nc.tensor.matmul(out[:, i, g, :], block_tokens(q[:, h // 2, :], i),
                                                   block_tokens(k, i - g), start=True, stop=True)
                ins.then_inc(s_full, 1)

            def transposes(n):
                kind, h = units[n]
                s = n % 2
                probs = S[s]
                far_unit = kind == "far"
                pe.wait_ge(summed, n + 1)
                if n >= 1:
                    pe.wait_ge(t_moved, 2 * n)
                for i in range(4):
                    nc.tensor.transpose(aux[0][:, P * i:P * i + P], probs[:, i, 0, :], mem.ident[:, :])
                ins = None
                if not far_unit:
                    for i in range(1, 4):
                        ins = nc.tensor.transpose(aux[1][:, P * i:P * i + P], probs[:, i, 1, :], mem.ident[:, :])
                else:
                    ins = nc.tensor.transpose(aux[1][:, 0:P], probs[:, 0, 0, :], mem.ident[:, :])
                ins.then_inc(t_full, 1)

            def products(n):
                kind, h = units[n]
                s = n % 2
                far_unit = kind == "far"
                pe.wait_ge(t_moved, 2 * n + 2)
                if n >= 2:
                    pe.wait_ge(o_moved, n - 1)
                v = mem.vres if far_unit else mem.vnat
                for i in range(4):
                    out = aux[2 + s][:, HD * i:HD * i + HD]
                    two_blocks = not far_unit and i > 0
                    ins = nc.tensor.matmul(out, PT[s][:, i, :], v[:, i, HD * h:HD * h + HD], start=True, stop=not two_blocks)
                    if two_blocks:
                        ins = nc.tensor.matmul(out, PT[s][:, 4 + i, :], v[:, i - 1, HD * h:HD * h + HD], start=False, stop=True)
                ins.then_inc(o_full, 1)

            scores(0)
            scores(1)
            for n in range(len(units)):
                transposes(n)
                if n + 2 < len(units):
                    scores(n + 2)
                products(n)

        @block.vector
        def _(v):
            count = [0]

            def link(ins):
                count[0] += 1
                ins.then_inc(dve, 1)
                v.wait_ge(dve, count[0])

            v.wait_ge(c_in, 32)

            def bias(n):
                kind, h = units[n]
                s = n % 2
                src = acc[s][:, :].rearrange("p (i g k) -> p i g k", i=4, g=2)
                v.wait_ge(s_full, n + 1)
                if n >= 2:
                    v.wait_ge(t_full, n - 1)
                if kind == "near":
                    link(v.memset(S[s][:, 0, 1, :], -1e30))
                for g in range(2):
                    if kind == "far":
                        d, sl, i0 = dist[:, 2 + g, :], slope[:, N_HEADS * (1 + g) + h:N_HEADS * (1 + g) + h + 1], 0
                    else:
                        d, sl, i0 = dist[:, g, :], slope[:, h:h + 1], g
                    ins = v.scalar_tensor_tensor(S[s][:, i0:4, g, :], d.unsqueeze(1).broadcast_to([P, 4 - i0, P]), sl,
                                                 src[:, i0:4, g, :], ALU.mult, ALU.add)
                ins.then_inc(biased, 1)
                v.wait_ge(biased, n + 1)
                flat = S[s][:, :, :, :].rearrange("p i g k -> p i (g k)")
                if kind == "far":
                    m = far[:, :, h, HD:HD + 1].rearrange("p i o -> p (i o)")
                    link(v.tensor_reduce(m, flat, AX_X, ALU.max))
                else:
                    if h in HALVES[0][:1] + HALVES[1][:1]:
                        v.wait_ge(moved[h > 0], 16 * 16)
                    m = nmax[:, n % 4, :]
                    link(v.tensor_reduce(m, flat, AX_X, ALU.max))
                    link(v.tensor_tensor(m, m, near[:, :, h, HD:HD + 1].rearrange("p i o -> p (i o)"), ALU.max))
                    link(v.tensor_tensor(e12[:, n % 4, :], near[:, :, h, HD:HD + 1].rearrange("p i o -> p (i o)"), m, ALU.subtract))
                link(v.tensor_scalar(nmax[:, n % 4, :], m, -1.0, None, ALU.mult))
                v.sem_inc(maxed, 1)

            def add_far(n):
                kind, h = units[n]
                s = n % 2
                v.wait_ge(exped, n + 1)
                if kind == "far":
                    link(v.tensor_tensor(S[s][:, :, 0, :], S[s][:, :, 0, :], S[s][:, :, 1, :], ALU.add))
                v.sem_inc(summed, 1)

            def move(n):
                kind, h = units[n]
                s = n % 2
                v.wait_ge(t_full, n + 1)
                if kind == "near":
                    v.tensor_copy(PT[s][:, 5:8, :], aux[1][:, P:4 * P].rearrange("p (i q) -> p i q", i=3)).then_inc(t_moved, 1)
                else:
                    v.sem_inc(t_moved, 1)

            def finish(n):
                kind, h = units[n]
                s = n % 2
                v.wait_ge(o_full, n + 1)
                out = aux[2 + s][:, 0:4 * HD].rearrange("p (i d) -> p i d", i=4)
                if kind == "far":
                    v.tensor_copy(far[:, :, h, 0:HD], out).then_inc(o_moved, 1)
                    return
                link(v.tensor_tensor(den[:, s, :], e12[:, n % 4, :], near[:, :, h, HD + 1:HD + 2].rearrange("p i o -> p (i o)"), ALU.mult))
                link(v.tensor_tensor(den[:, s, :], den[:, s, :], l0[:, n % 4, :], ALU.add))
                v.tensor_tensor(on[:, :, :], near[:, :, h, 0:HD], e12[:, n % 4, :].unsqueeze(2).broadcast_to([P, 4, HD]), ALU.mult)
                link(v.reciprocal(den[:, s, :], den[:, s, :]))
                link(v.tensor_tensor(on[:, :, :], on[:, :, :], out, ALU.add))
                link(v.tensor_tensor(mem.o_nat[:, :, HD * h:HD * h + HD], on[:, :, :],
                                     den[:, s, :].unsqueeze(2).broadcast_to([P, 4, HD]), ALU.mult))
                v.sem_inc(o_moved, 1)

            bias(0)
            for n in range(len(units)):
                add_far(n)
                if n + 1 < len(units):
                    bias(n + 1)
                move(n)
                if n >= 1:
                    finish(n - 1)
            finish(len(units) - 1)

        @block.scalar
        def _(act):
            for q in range(NS):
                act.dma_start(ten["s_kv"][q, 0:SEQ - 1, :, :, :], ten["cache_kv"][q, 1:SEQ, :, :, :]).then_inc(mem.cache_moved, 16)
            for n, (kind, h) in enumerate(units):
                s = n % 2
                act.wait_ge(maxed, n + 1)
                for i in range(4):
                    acc_out = far[:, i, h, HD + 1:HD + 2] if kind == "far" else l0[:, n % 4, i:i + 1]
                    ins = act.activation(S[s][:, i, :, :].rearrange("p g k -> p (g k)"), S[s][:, i, :, :].rearrange("p g k -> p (g k)"),
                                         ACT.Exp, bias=nmax[:, n % 4, i:i + 1], accum_out=acc_out)
                if kind == "near":
                    ins = act.activation(e12[:, n % 4, :], e12[:, n % 4, :], ACT.Exp)
                ins.then_inc(exped, 1)
                act.wait_ge(t_full, n + 1)
                act.activation(PT[s][:, 0:4, :], aux[0][:, :].rearrange("p (i q) -> p i q", i=4), ACT.Copy).then_inc(t_moved, 1)


KEYS = 2 * (P + 1) + 33


def decode_attention(nc, mem, ten, dram):
    o = mem.acth_at
    krow, qrow, vrow, prod = [], [], [], []
    for s in range(2):
        t, o = mem.at(f"k_rows{s}", [P, 2, D], o)
        krow.append(t)
        t, o = mem.at(f"v_rows{s}", [P, 2, D], o)
        vrow.append(t)
        t, o = mem.at(f"q_rows{s}", [P, 3, D], o)
        qrow.append(t)
    for s in range(3):
        t, o = mem.at(f"qk{s}", [P, D], o)
        prod.append(t)
    vring = vrow + krow
    pv = prod[2]
    vnew, o = mem.at("v_new", [NS, D], o)
    scT, o = mem.at("d_scoresT", [P, 3, NS, N_HEADS], o)
    ptz, o = mem.at("d_probsT", [P, 2, NS, P], o)
    qkz, o = mem.at("qk_new", [P, 3, P], o)
    drow, o = mem.at("distance_row", [P, P + 1], o)
    scol, o = mem.at("slope_column", [P, 3], o)
    pick, o = mem.at("sequence_of_row", [P, NS], o)
    sc, o = mem.at("d_scores", [P, KEYS], o)
    st, o = mem.at("d_stats", [P, 4], o)
    diag, o = mem.at("p_new_diagonal", [P, P], o)
    pnew, o = mem.at("p_new", [NS, P], o)
    assert o <= mem.rest
    mem.od, _ = mem.at("d_out", [P, DT, NS], mem.stat_at)
    acc, aux = mem.acc, mem.aux
    spans = ((0, P + 1, 1), (P + 1, P + 1, 1), (2 * (P + 1), 33, 4))
    with ExitStack() as ctx:
        def sem(x):
            return nc.alloc_semaphore(f"decode_{x}")

        c_in, zeroed = sem("constants_in"), sem("zeroed")
        v_in = [sem(f"v_rows_in{s}") for s in range(4)]
        d_in, new_in = [sem("k_rows_in0"), sem("k_rows_in1")], sem("v_new_in")
        by_pool, by_dve, summed = sem("qk_by_pool"), sem("qk_by_dve"), sem("qk_summed")
        qk, s_full, maxed, exped, normed = sem("qk_new"), sem("scores"), sem("maxed"), sem("exped"), sem("normed")
        p_full, p_moved, v_used = sem("probs_transposed"), sem("probs_moved"), sem("v_used")
        o_full, o_moved, t_full = sem("out_full"), sem("out_moved"), sem("out_transposed")
        dve = sem("dve_chain")
        block = ctx.enter_context(nc.Block())

        @block.sync
        def _(sp):
            const, at = ten["constants"], 4 * P + 3 * N_HEADS
            sp.dma_start(drow[:, 0:P], const[:, at:at + P]).then_inc(c_in, 16)
            sp.dma_start(scol[:, :], const[:, at + P:at + P + 3]).then_inc(c_in, 16)
            sp.dma_start(pick[:, :], const[:, at + P + 3:at + P + 3 + NS]).then_inc(c_in, 16)
            cache = ten["cache_kv"].rearrange("s t z h d -> s t z (h d)")

            def load_v(s):
                sp.dma_start(vring[s % 4][:, 0, :], cache[s, SEQ - P:SEQ, 1, :]).then_inc(v_in[s % 4], 16)
                sp.dma_start(vring[s % 4][:, 1, :], cache[s, 0:SEQ - 3:4, 1, :]).then_inc(v_in[s % 4], 16)

            for s in range(NS):
                if s >= 2:
                    sp.wait_ge(by_pool, 2 * s - 2)
                    sp.wait_ge(by_dve, s - 1)
                sp.dma_start(krow[s % 2][:, 0, :], cache[s, SEQ - P:SEQ, 0, :]).then_inc(d_in[s % 2], 16)
                sp.dma_start(krow[s % 2][:, 1, :], cache[s, 0:SEQ - 3:4, 0, :]).then_inc(d_in[s % 2], 16)
                sp.dma_start(qrow[s % 2][:, :, :], dram["q"][s:s + 1, :, :].broadcast_to([P, 3, D])).then_inc(d_in[s % 2], 16)
            sp.dma_start(vnew[:, :], ten["s_kv"][:, SEQ - 1, 1, :, :].rearrange("s h d -> s (h d)")).then_inc(new_in, 16)
            load_v(0)
            load_v(1)
            sp.wait_ge(by_pool, 2 * NS)
            sp.wait_ge(by_dve, NS)
            for s in range(2, NS):
                if s >= 4:
                    sp.wait_ge(v_used, s - 3)
                load_v(s)

        @block.gpsimd
        def _(pool):
            pool.memset(qkz[:, :, :], 0.0).then_inc(zeroed, 1)
            pool.memset(drow[:, P:P + 1], 0.0).then_inc(zeroed, 1)
            pool.memset(ptz[:, :, :, :], 0.0).then_inc(zeroed, 1)
            for s in range(NS):
                pool.wait_ge(d_in[s % 2], 48 * (s // 2) + 48)
                for g in range(2):
                    if s >= 1:
                        pool.wait_ge(summed, 3 * s - 2 + g)
                    pool.tensor_tensor(prod[g][:, :], krow[s % 2][:, g, :], qrow[s % 2][:, g, :], ALU.mult).then_inc(by_pool, 1)

        @block.tensor
        def _(pe):
            pe.wait_ge(qk, 1)
            pe.wait_ge(summed, 3 * NS)
            for g in range(3):
                at = g * (P + 1)
                nc.tensor.transpose(aux[0][:, at:at + P], scT[:, g, :, :].rearrange("p s h -> p (s h)"), mem.ident[:, :])
                ins = nc.tensor.matmul(aux[0][:, at + P:at + P + 1], qkz[:, g, :], mem.ones[:, 0:1], start=True, stop=True)
            ins.then_inc(s_full, 1)
            pe.wait_ge(normed, 1)
            nc.tensor.transpose(aux[1][:, 0:P], sc[:, 0:P], mem.ident[:, :])
            nc.tensor.transpose(aux[1][:, P:2 * P], sc[:, P + 1:2 * P + 1], mem.ident[:, :])
            nc.tensor.matmul(aux[1][0:NS, 2 * P:3 * P], pick[:, :], diag[:, :], start=True, stop=True).then_inc(p_full, 1)
            pe.wait_ge(p_moved, 3)
            pe.wait_ge(new_in, 16)
            halves = (slice(0, 512), slice(512, 1024))
            for c in halves:
                nc.tensor.matmul(acc[0][:, c], pnew[:, :], vnew[:, c], start=True, stop=False)
            for s in range(NS):
                pe.wait_ge(v_in[s % 4], 32 * (s // 4) + 32)
                for which in range(2):
                    for c in halves:
                        ins = nc.tensor.matmul(acc[0][:, c], ptz[:, which, s, :], vring[s % 4][:, which, c],
                                               start=False, stop=s == NS - 1 and which == 1)
                ins.then_inc(v_used, 1)
            pe.wait_ge(o_moved, 2)
            for f in range(DT):
                ins = nc.tensor.transpose(aux[2 + f // 4][:, P * (f % 4):P * (f % 4) + P], pv[:, P * f:P * f + P], mem.ident[:, :])
            ins.then_inc(t_full, 1)

        @block.scalar
        def _(act):
            act.wait_ge(maxed, 1)
            act.activation(sc[:, :], sc[:, :], ACT.Exp, bias=st[:, 1:2], accum_out=st[:, 2:3]).then_inc(exped, 1)
            act.wait_ge(v_used, NS)
            act.activation(pv[:, 0:512], acc[0][:, 0:512], ACT.Copy).then_inc(o_moved, 1)

        @block.vector
        def _(v):
            count = [0]

            def link(ins):
                count[0] += 1
                ins.then_inc(dve, 1)
                v.wait_ge(dve, count[0])

            v.wait_ge(zeroed, 3)
            for g in range(3):
                for e in range(2):
                    half = slice(64 * e, 64 * e + 64)
                    ins = v.tensor_tensor(qkz[half, g, :].rearrange("p (s f e) -> p e f s", e=2, f=DT)[:, e, :, :],
                                          mem.q[half, DT * g:DT * g + DT, SEQ:TOK], mem.kv[half, 0:DT, SEQ:TOK], ALU.mult)
            ins.then_inc(qk, 1)

            def total(s, g):
                v.tensor_reduce(scT[:, g, s, :], prod[g][:, :].rearrange("p (h d) -> p h d", d=HD),
                                AX_X, ALU.add).then_inc(summed, 1)

            for s in range(NS):
                v.wait_ge(d_in[s % 2], 48 * (s // 2) + 48)
                if s >= 1:
                    v.wait_ge(summed, 3 * s)
                v.tensor_tensor(prod[2][:, :], krow[s % 2][:, 1, :], qrow[s % 2][:, 2, :], ALU.mult).then_inc(by_dve, 1)
                for g in range(2):
                    v.wait_ge(by_pool, 2 * s + g + 1)
                    total(s, g)
                v.wait_ge(by_dve, s + 1)
                total(s, 2)
            v.wait_ge(c_in, 48)
            v.wait_ge(s_full, 1)
            for g, (at, n, step) in enumerate(spans):
                x = aux[0][:, g * (P + 1):g * (P + 1) + (n - 1) * step + 1:step]
                ins = v.scalar_tensor_tensor(sc[:, at:at + n], drow[:, 0:(n - 1) * step + 1:step], scol[:, g:g + 1], x,
                                             ALU.mult, ALU.add)
            link(ins)
            link(v.tensor_reduce(st[:, 0:1], sc[:, :], AX_X, ALU.max))
            link(v.tensor_scalar(st[:, 1:2], st[:, 0:1], -1.0, None, ALU.mult))
            v.sem_inc(maxed, 1)
            v.wait_ge(exped, 1)
            link(v.reciprocal(st[:, 3:4], st[:, 2:3]))
            link(v.tensor_tensor(sc[:, P + 1:2 * (P + 1):4], sc[:, P + 1:2 * (P + 1):4], sc[:, 2 * (P + 1):KEYS], ALU.add))
            link(v.tensor_tensor(sc[:, P:P + 1], sc[:, P:P + 1], sc[:, 2 * P + 1:2 * P + 2], ALU.add))
            link(v.tensor_scalar(sc[:, 0:2 * P + 1], sc[:, 0:2 * P + 1], st[:, 3:4], None, ALU.mult))
            link(v.tensor_scalar(diag[:, :], mem.ident[:, :], sc[:, P:P + 1], None, ALU.mult))
            v.sem_inc(normed, 1)
            v.wait_ge(p_full, 1)
            v.tensor_copy(pnew[:, :], aux[1][0:NS, 2 * P:3 * P]).then_inc(p_moved, 1)
            for which in range(2):
                for s in range(NS):
                    ins = v.tensor_copy(ptz[:, which, s, N_HEADS * s:N_HEADS * s + N_HEADS],
                                        aux[1][:, P * which + N_HEADS * s:P * which + N_HEADS * s + N_HEADS])
                ins.then_inc(p_moved, 1)
            v.wait_ge(v_used, NS)
            v.tensor_copy(pv[:, 512:1024], acc[0][:, 512:1024]).then_inc(o_moved, 1)
            v.wait_ge(t_full, 1)
            for part in range(2):
                for e in range(2):
                    half = slice(64 * e, 64 * e + 64)
                    for f in range(4 * part, 4 * part + 4):
                        ins = v.tensor_copy(mem.od[half, f, :], aux[2 + part][half, P * (f % 4) + 2 * f + e:P * (f % 4) + P:N_HEADS])
            link(ins)


def gate_output(nc, mem, ten, dram):
    o = mem.actl_at + DT * TOK * 4
    y = []
    for s in range(2):
        t, o = mem.at(f"gated{s}", [P, TOK], o)
        y.append(t)
    aux = mem.aux
    with ExitStack() as ctx:
        def sem(x):
            return nc.alloc_semaphore(f"gate_o_{x}")

        full, prod, hi, lo = sem("transposed"), sem("product"), sem("hi_ready"), sem("lo_ready")
        block = ctx.enter_context(nc.Block())

        @block.tensor
        def _(pe):
            for f in range(DT):
                if f >= 4:
                    pe.wait_ge(prod, f - 3)
                for b in range(4):
                    ins = nc.tensor.transpose(aux[f % 4][:, P * b:P * b + P], mem.o_nat[:, b, P * f:P * f + P], mem.ident[:, :])
                ins.then_inc(full, 1)

        @block.vector
        def _(v):
            def low(f):
                v.wait_ge(hi, f + 1)
                v.tensor_tensor(mem.actl[:, f, :], y[f % 2][:, :], mem.acth[:, f, :].bitcast(F32), ALU.subtract).then_inc(lo, 1)

            for f in range(DT):
                v.wait_ge(full, f + 1)
                if f >= 2:
                    v.wait_ge(lo, f - 1)
                v.tensor_tensor(y[f % 2][:, SEQ:TOK], mem.od[:, f, :], mem.zb[:, f, SEQ:TOK], ALU.mult)
                v.tensor_tensor(y[f % 2][:, 0:SEQ], aux[f % 4][:, :], mem.zb[:, f, 0:SEQ], ALU.mult).then_inc(prod, 1)
                if f >= 1:
                    low(f - 1)
            low(DT - 1)

        @block.scalar
        def _(act):
            for f in range(DT):
                act.wait_ge(prod, f + 1)
                act.activation(mem.acth[:, f, :], y[f % 2][:, :], ACT.Copy).then_inc(hi, 1)


def attn_out(nc, mem, ten, dram):
    residual(nc, mem, "b_out", ten["b_w_out"][0, :, :], 1, mem.acth[:, 0:DT, :], mem.actl[:, 0:DT, :], V_BPOST,
             mem.rest, mem.rest + DT * TOK * 4, natural=True)


def write_y(nc, mem, ten, dram):
    yo, o = mem.at("y_rows", [P, 4, D], mem.acth_at)
    ys, o = mem.at("y_sample_rows", [NS, D], o)
    acc = mem.acc
    with ExitStack() as ctx:
        def sem(x):
            return nc.alloc_semaphore(f"write_{x}")

        full, moved_a, moved_v, stored = sem("transposed"), sem("moved_act"), sem("moved_dve"), sem("stored")
        block = ctx.enter_context(nc.Block())

        @block.tensor
        def _(pe):
            for n in range(5):
                if n >= 2:
                    pe.wait_ge(moved_a if n % 2 == 0 else moved_v, n // 2)
                for f in range(DT):
                    if n < 4:
                        out, src = acc[n % 2][:, P * f:P * f + P], mem.xT[:, f, P * n:P * n + P]
                    else:
                        out, src = acc[0][0:NS, P * f:P * f + P], mem.xT[:, f, SEQ:TOK]
                    ins = nc.tensor.transpose(out, src, mem.ident[:, :])
                ins.then_inc(full, 1)

        @block.scalar
        def _(act):
            for n in (0, 2, 4):
                act.wait_ge(full, n + 1)
                if n < 4:
                    act.activation(yo[:, n, :], acc[0][:, :], ACT.Copy).then_inc(moved_a, 1)
                else:
                    act.activation(ys[:, :], acc[0][0:NS, :], ACT.Copy).then_inc(moved_a, 1)

        @block.vector
        def _(v):
            for n in (1, 3):
                v.wait_ge(full, n + 1)
                v.tensor_copy(yo[:, n, :], acc[1][:, :]).then_inc(moved_v, 1)

        @block.sync
        def _(sp):
            yp = ten["y_prompt"][0, :, :].rearrange("(c j) d -> j c d", j=L)
            for n in range(4):
                sp.wait_ge(moved_a if n % 2 == 0 else moved_v, n // 2 + 1)
                for i in range(2):
                    sp.dma_start(yp[2 * n + i], yo[64 * i:64 * i + 64, n, :]).then_inc(stored, 16)
            sp.wait_ge(moved_a, 3)
            sp.dma_start(ten["y_sample"][:, 0, :], ys[:, :]).then_inc(stored, 16)
            sp.wait_ge(stored, 16 * 9)
            sp.wait_ge(mem.cache_moved, 16 * NS)


INS = ["x_prompt", "x_sample", "state_s5_re", "state_s5_im", "cache_kv", "a_norm_pre", "a_w_in", "a_lam_re",
       "a_lam_im", "a_log_dt", "a_b_re", "a_b_im", "a_c_re", "a_c_im", "a_d", "a_w_glu", "a_b_glu", "a_w_out",
       "a_norm_post", "kv_norm", "w_kv", "b_norm_pre", "b_w_in", "b_w_out", "b_norm_post"]
OUTS = [("y_prompt", (1, SEQ, D)), ("y_sample", (NS, 1, D)), ("p_re", (1, 1, G, ST)), ("p_im", (1, 1, G, ST)),
        ("p_kv", (1, SEQ, 2, N_HEADS, HD)), ("s_re", (1, NS, G, ST)), ("s_im", (1, NS, G, ST)),
        ("s_kv", (NS, SEQ, 2, N_HEADS, HD))]


def trunk(nc, ten, phases=99):
    mem = plan(nc)
    dram = {
        "u": nc.dram_tensor("scratch_u", (W2, TOK), F32, kind="Internal").ap(),
        "y": nc.dram_tensor("scratch_y", (W2, TOK), F32, kind="Internal").ap(),
        "z": nc.dram_tensor("scratch_z", (W2, TOK), F32, kind="Internal").ap(),
        "q": nc.dram_tensor("scratch_q", (NS, 3, D), F32, kind="Internal").ap(),
        "k": nc.dram_tensor("scratch_k", (CH, G, 15 * CH), F32, kind="Internal").ap(),
    }
    with ExitStack() as ctx:
        mem.acc = [ctx.enter_context(nc.psum_tensor(f"acc{a}", [P, 1024], F32)) for a in range(2)]
        mem.aux = [ctx.enter_context(nc.psum_tensor(f"aux{a}", [P, 512], F32)) for a in range(4)]
        mem.cache_moved = nc.alloc_semaphore("cache_moved")
        parts = (setup, states, gate_and_scan, outputs, glu, ssm_out,
                 project, token_rows, attention, decode_attention, gate_output, attn_out, write_y)[:phases]
        for group in (parts[:6], parts[6:]):
            with nc.cleanup_on_exit():
                for f in group:
                    f(nc, mem, ten, dram)
    return mem


def constants(np):
    far = np.float32(-1e30)
    n = np.arange(P)
    own = n[None, :] - n[:, None]
    prev = own - P
    tabs = [np.where(own <= 0, own, far), np.where(prev >= -P, prev, far),
            np.where(own <= 0, 4 * own, far),
            np.where((own <= 0) & (own % 4 == 0), 4 * own, far)]
    slopes = np.broadcast_to(np.array(SLOPE, np.float64).reshape(1, 3 * N_HEADS), (P, 3 * N_HEADS))
    row = np.broadcast_to((n[None, :] - P), (P, P))
    steps = np.array([1.0, 4.0, 4.0]).reshape(3, 1)
    d_slopes = np.tile((np.array(SLOPE, np.float64) * steps).T, (NS, 1))
    pick = (n[:, None] // N_HEADS == np.arange(NS)[None, :]).astype(np.float32)
    return np.concatenate(tabs + [slopes, row, d_slopes, pick], axis=1).astype(np.float32)


def kernel(**inputs):
    import numpy as np
    import concourse.bacc as bacc
    from concourse.bass_utils import run_bass_kernel_spmd

    nc = bacc.Bacc("TRN2", target_bir_lowering=False, num_devices=1)
    arrays, ten = {}, {}
    for name in INS:
        a = np.ascontiguousarray(inputs[name])
        arrays[name] = a
        ten[name] = nc.dram_tensor(name, a.shape, mybir.dt.from_np(a.dtype), kind="ExternalInput").ap()
    arrays["constants"] = constants(np)
    ten["constants"] = nc.dram_tensor("constants", arrays["constants"].shape, F32, kind="ExternalInput").ap()
    for name, shape in OUTS:
        ten[name] = nc.dram_tensor(name, shape, F32, kind="ExternalOutput").ap()
    trunk(nc, ten)
    r = run_bass_kernel_spmd(nc, [arrays], core_ids=[0])
    return tuple(r.results[0][name] for name, _ in OUTS)
```

```python
import math
from contextlib import ExitStack

import concourse.bass as bass
from concourse import mybir

F32 = mybir.dt.float32
F32R = mybir.dt.float32r
ALU = mybir.AluOpType
ACT = mybir.ActivationFunctionType
AX_X = mybir.AxisListType.X

P = 128
D = 1024
DT = D // P
W2 = 2048
WT = W2 // P
SEQ = 512
NS = 8
TOK = SEQ + NS
CUTS = ((0, 256), (256, TOK))
G = 128
NP = G // 2
CH = 16
ST = 64
L = 8
NC = SEQ // L
EPS = 1e-6

C_FIRST = NC + 1
C_LAST = C_FIRST + NS
YC = C_FIRST + NS
UC = C_LAST + NS

V_APRE, V_APOST, V_KV, V_BPRE, V_BPOST, V_D, V_BGLU = 0, 8, 16, 24, 32, 40, 56
NVEC = 88

N_HEADS = 16
HD = 64
SLOPE = [[2.0 ** (-8.0 * (g * N_HEADS + h + 1) / 48) for h in range(N_HEADS)] for g in range(3)]


class Memory:

    def __init__(self, nc):
        self.nc = nc
        self.base = (nc.sbuf_base + 63) // 64 * 64
        self.end = nc.sbuf_usable_end

    def at(self, name, shape, offset, dtype=F32):
        size = 4
        for n in shape[1:]:
            size *= n
        size = (size + 31) // 32 * 32
        assert self.base + offset + size <= self.end, (name, offset, size, self.end - self.base)
        return self.nc.alloc_sbuf_tensor_at(name, shape, dtype, offset=self.base + offset), offset + size


class Dense:

    def __init__(self, nc, mem, name, units, first):
        def sem(x):
            return nc.alloc_semaphore(f"{name}_{x}")

        self.nc = nc
        self.mem = mem
        self.units = units
        self.first = first
        self.landed = [sem("weights_landed0"), sem("weights_landed1")]
        self.hi_ready = sem("hi_ready")
        self.lo_ready = sem("lo_ready")
        self.unit_read = sem("unit_read")
        self.acc_free = [sem("acc_free0"), sem("acc_free1")]

    def load(self, sp, n, s, block):
        sp.wait_ge(self.lo_ready, n + 1)
        sp.dma_start(self.mem.raw[s][:, :, :], block).then_inc(self.landed[s], 16)

    def split_hi(self, act, n, s, turn):
        act.wait_ge(self.landed[s], 16 * (turn + 1))
        act.wait_ge(self.unit_read, n + 1)
        act.activation(self.mem.wh[s][:, :, :], self.mem.raw[s][:, :, :], ACT.Copy).then_inc(self.hi_ready, 1)

    def split_lo(self, pool, n, s):
        pool.wait_ge(self.hi_ready, n + 1)
        pool.tensor_tensor(self.mem.wl[s][:, :, :], self.mem.raw[s][:, :, :],
                           self.mem.wh[s][:, :, :].bitcast(F32), ALU.subtract).then_inc(self.lo_ready, 1)

    def start(self, pe):
        pe.sem_inc(self.unit_read, 2)
        for a in range(2):
            pe.sem_inc(self.acc_free[a], 1)

    def load_first(self, sp, before=None, total=0):
        for n in range(2):
            if before:
                sp.wait_ge(before.lo_ready, total + n + 1)
            sp.dma_start(self.mem.raw[n][:, :, :], self.first[n]).then_inc(self.landed[n], 16)

    def load_second(self, sp, second):
        for n in range(2):
            self.load(sp, n + 2, n, second[n])

    def split_hi_first(self, act, before=None, total=0):
        for n in range(2):
            act.wait_ge(self.landed[n], 16)
            if before:
                act.wait_ge(before.unit_read, total + n + 1)
            act.activation(self.mem.wh[n][:, :, :], self.mem.raw[n][:, :, :], ACT.Copy).then_inc(self.hi_ready, 1)

    def split_lo_first(self, pool):
        pool.sem_inc(self.lo_ready, 2)
        for n in range(2):
            self.split_lo(pool, n, n)

    def wait_tile(self, eng, t):
        eng.wait_ge(self.unit_read, (t + 1) * self.units + 2)

    def multiply(self, pe, n, s, a, xh, xl, k0, first, last):
        pe.wait_ge(self.lo_ready, n + 3)
        self.products(a, s, xh, xl, k0, first, last)

    def products(self, a, s, xh, xl, k0, first, last, wait_block=None):
        nc, mem = self.nc, self.mem
        for k in range(8):
            if wait_block:
                wait_block(k0 + k)
            terms = ((mem.wh, xh), (mem.wh, xl), (mem.wl, xh))
            for i, (w, x) in enumerate(terms):
                for lo, hi in CUTS:
                    ins = nc.tensor.matmul(
                        mem.acc[a][:, 256 + lo:256 + hi], w[s][:, k, :], x[:, k0 + k, lo:hi],
                        start=first and k == 0 and i == 0, stop=last and k == 7 and i == 2)
        ins.then_inc(self.unit_read, 1)

    def first_tiles(self, pe, xh, xl, wait_block):
        nc, mem = self.nc, self.mem
        for a in range(2):
            pe.wait_ge(self.acc_free[a], 1)
        pe.wait_ge(self.lo_ready, 4)
        for k in range(8):
            wait_block(k)
            for a in range(2):
                for i, (w, x) in enumerate(((mem.wh, xh), (mem.wh, xl), (mem.wl, xh))):
                    for lo, hi in CUTS:
                        ins = nc.tensor.matmul(mem.acc[a][:, 256 + lo:256 + hi], w[a][:, k, :], x[:, k, lo:hi],
                                               start=k == 0 and i == 0, stop=k == 7 and i == 2)
                if k == 7:
                    ins.then_inc(self.unit_read, 1)

    def early_tile(self, pe, xh, xl, wait_block):
        for u in range(2):
            pe.wait_ge(self.lo_ready, u + 3)
            self.products(0, u, xh, xl, 8 * u, u == 0, u == 1, wait_block)

    def tile(self, pe, t, a, turn, xh, xl):
        pe.wait_ge(self.acc_free[a], turn + 1)
        for u in range(self.units):
            slot = u if self.units == 2 else a
            self.multiply(pe, self.units * t + u, slot, a, xh, xl, 8 * u, u == 0, u == self.units - 1)


def columns(acc):
    return acc[:, 256:256 + TOK]


def blocks(w):
    return w.rearrange("(k p) m -> p k m", p=P)


def cols(i, n=P):
    return bass.ds(i * n, n)


def paired(eng, start, end, body):
    if start % 2:
        body(start, 1, start // 2)
        start += 1
    if end - start >= 4:
        with eng.Fori(start // 2, end // 2) as h:
            body(2 * h, 0, h)
            body(2 * h + 1, 1, h)
    else:
        for i in range(start, end // 2 * 2):
            body(i, i % 2, i // 2)
    if end % 2:
        body(end - 1, 0, end // 2)


def plan(nc):
    mem = Memory(nc)
    o = 0
    mem.ident, o = mem.at("ident", [P, P], o)
    mem.ones, o = mem.at("ones", [P, P], o)
    mem.vec, o = mem.at("vec", [P, NVEC], o)
    mem.cst, o = mem.at("cst", [P, 8], o)
    o = 2048
    mem.xT, o = mem.at("xT", [P, DT, TOK], o)
    mem.acth_at = o
    mem.acth, o = mem.at("act_hi", [P, WT, TOK], o, F32R)
    mem.actl_at = o
    mem.actl, o = mem.at("act_lo", [P, WT, TOK], o, F32R)
    mem.ring_at = o
    mem.raw, mem.wh, mem.wl = [], [], []
    for s in range(2):
        t, o = mem.at(f"raw{s}", [P, 8, P], o)
        mem.raw.append(t)
    for s in range(2):
        t, o = mem.at(f"w_hi{s}", [P, 8, P], o, F32R)
        mem.wh.append(t)
        t, o = mem.at(f"w_lo{s}", [P, 8, P], o, F32R)
        mem.wl.append(t)
    mem.rest = o
    return mem


def setup(nc, mem, ten, dram):
    R = mem.rest
    mem.XH, o = mem.at("XH", [P, C_LAST, 2, NP], R)
    mem.Ct, o = mem.at("Ct", [P, 2, NP, CH], o)
    mem.apow, o = mem.at("apow", [P, L + 1, 2, NP], o)
    mem.p3_at = o
    mem.Bt, o = mem.at("Bt", [P, 2, NP, CH], o)
    mem.cb, o = mem.at("cb", [P, L, 2, NP], o)
    mem.Xs, o = mem.at("Xs", [P, NS, 2, NP], o)
    mem.Ksb, o = mem.at("Ksb", [P, G, CH], o)
    mem.p1_at = o
    a = mem.acth_at
    xtok, a = mem.at("xtok", [P, SEQ // P, D], a)
    crow, a = mem.at("crow", [P, 2, 8, P], mem.acth_at + DT * TOK * 4)
    h0row, a = mem.at("h0row", [NP, 2, NS, P], a)
    assert a <= mem.actl_at
    mem.norm_a = nm = Norm(nc, mem, "norm_a", mem.actl_at + DT * TOK * 4)
    xsam, a = mem.at("xsam", [NS, D], nm.end)
    vrow, a = mem.at("vrow", [NVEC, P], mem.p1_at)
    lam, a = mem.at("lam", [NP, 2, P], a)
    ldt, a = mem.at("ldt", [NP, 2], a)
    dtr, a = mem.at("dtr", [NP, 2], a)
    lrow, a = mem.at("lrow", [NP, 4, P], a)
    ls, a = mem.at("ls", [P, 4, NP], a)
    dw, a = mem.at("disc", [P, 16, NP], a)
    tm, a = mem.at("powtmp", [P, 4, 4, NP], a)
    acc, aux = mem.acc, mem.aux
    w_in = blocks(ten["a_w_in"][0, :, :])
    mem.u_proj = dn = Dense(nc, mem, "u_proj", 1, [w_in[:, :, cols(n)] for n in range(2)])

    with ExitStack() as ctx:
        def sem(x):
            return nc.alloc_semaphore(f"setup_{x}")

        x_in, v_in, c_in, h_in, l_in, b_in = (sem(x) for x in ("x_in", "vec_in", "c_in", "h0_in", "lam_in", "b_in"))
        masks = sem("masks")
        full, free = sem("transposed"), sem("moved")
        rows = sem("rows")
        dve = sem("dve_chain")
        dt_ready, l_full, x_moved = sem("dt_ready"), sem("lam_transposed"), sem("x_moved")
        a_in, a_out = sem("act_ask"), sem("act_done")
        block = ctx.enter_context(nc.Block())

        @block.sync
        def _(sp):
            for ri, name in enumerate(("a_lam_re", "a_lam_im")):
                sp.dma_start(lam[:, ri, :], ten[name][0, :, :].rearrange("(c e) p -> c (e p)", e=2)).then_inc(l_in, 16)
            sp.dma_start(ldt[:, :], ten["a_log_dt"][0, :].rearrange("(c e) -> c e", e=2)).then_inc(l_in, 16)
            xp = ten["x_prompt"][0, :, :].rearrange("(c j) d -> j c d", j=L)
            for j in range(L):
                sp.dma_start(xtok[64 * (j % 2):64 * (j % 2) + 64, j // 2, :], xp[j]).then_inc(x_in, 16)
            sp.dma_start(xsam[:, :], ten["x_sample"][:, 0, :]).then_inc(x_in, 16)
            at = 0
            for name in ("a_norm_pre", "a_norm_post", "kv_norm", "b_norm_pre", "b_norm_post", "a_d", "a_b_glu"):
                v = ten[name] if name == "kv_norm" else ten[name][0, :]
                n = v.shape[0] // P
                sp.dma_start(vrow[at:at + n, :], v.rearrange("(f p) -> f p", p=P)).then_inc(v_in, 16)
                at += n
            dn.load_first(sp)
            for ri, name in enumerate(("a_c_re", "a_c_im")):
                c = ten[name][0, :, :, :].rearrange("(c e) o p -> e c o p", e=2)
                for t in range(8):
                    for e in range(2):
                        sp.dma_start(crow[:, ri, t, 64 * e:64 * e + 64], c[e, 8 * t:8 * t + 8, :, :]).then_inc(c_in, 16)
            for ri, name in enumerate(("state_s5_re", "state_s5_im")):
                sp.dma_start(h0row[:, ri, :, :], ten[name][0, :, :, :].rearrange("s (c e) p -> c s (e p)", e=2)).then_inc(h_in, 16)
            for ri, name in enumerate(("a_b_re", "a_b_im")):
                b = ten[name][0, :, :, :].rearrange("(c e) p i -> e p c i", e=2)
                for e in range(2):
                    sp.dma_start(mem.Bt[64 * e:64 * e + 64, ri, :, :], b[e]).then_inc(b_in, 16)
            sp.wait_ge(b_in, 64)

        @block.gpsimd
        def _(pool):
            pool.memset(mem.ident[:, :], 0.0).then_inc(masks, 1)
            pool.memset(mem.ones[:, :], 1.0)
            pool.memset(mem.cst[:, :], EPS)
            pool.memset(mem.XH[:, 0, :, :], 0.0).then_inc(masks, 1)
            pool.wait_ge(masks, 2)
            pool.affine_select(out=mem.ident[:, :], in_=mem.ident[:, :], compare_op=ALU.not_equal, fill=1.0,
                               base=0, pattern=[[-1, P]], channel_multiplier=1).then_inc(masks, 1)
            dn.split_lo_first(pool)

        @block.tensor
        def _(pe):
            dn.start(pe)
            nm.start(pe)
            pe.wait_ge(masks, 3)
            pe.wait_ge(rows, 1)
            for q in range(4):
                ins = nc.tensor.transpose(aux[2][:, NP * q:NP * q + NP], lrow[:, q, :], mem.ident[0:NP, 0:NP])
            ins.then_inc(l_full, 1)
            pe.wait_ge(x_in, 16 * 9)
            for f in range(DT):
                if f >= 2:
                    pe.wait_ge(x_moved, f - 1)
                for b in range(4):
                    nc.tensor.transpose(acc[f % 2][:, P * b:P * b + P], xtok[:, b, P * f:P * f + P], mem.ident[:, :])
                nc.tensor.transpose(acc[f % 2][:, SEQ:SEQ + NS], xsam[:, P * f:P * f + P],
                                    mem.ident[0:NS, 0:NS]).then_inc(full, 1)
            pe.wait_ge(v_in, 16 * 7)
            nc.tensor.transpose(aux[3][:, 0:NVEC], vrow[:, :], mem.ident[0:NVEC, 0:NVEC]).then_inc(full, 1)
            for f in range(DT):
                nm.add(pe, f, f % 2, f == 0, f == DT - 1)
            pe.wait_ge(x_moved, DT)
            dn.first_tiles(pe, mem.acth, mem.actl, lambda k: pe.wait_ge(nm.act_lo, k + 1))
            pe.wait_ge(c_in, 16 * 32)
            pe.wait_ge(free, 9)
            for r in range(4):
                if r >= 2:
                    pe.wait_ge(free, 8 + r)
                for t in range(4):
                    ins = nc.tensor.transpose(aux[2 + r % 2][:, P * t:P * t + P], crow[:, r // 2, 4 * (r % 2) + t, :],
                                              mem.ident[:, :])
                ins.then_inc(full, 1)
            pe.wait_ge(h_in, 32)
            for ri in range(2):
                pe.wait_ge(free, 12 + ri)
                for s in range(NS):
                    ins = nc.tensor.transpose(aux[2 + ri][:, NP * s:NP * s + NP], h0row[:, ri, s, :], mem.ident[0:NP, 0:NP])
                ins.then_inc(full, 1)

        @block.scalar
        def _(act):
            act.wait_ge(l_in, 48)
            act.activation(dtr[:, :], ldt[:, :], ACT.Exp).then_inc(dt_ready, 1)
            act.wait_ge(a_in, 1)
            act.activation(dw[:, 0, :], ls[:, 0, :], ACT.Exp).then_inc(a_out, 1)
            act.wait_ge(a_in, 2)
            act.activation(dw[:, 5:7, :], dw[:, 3:5, :], ACT.Sin).then_inc(a_out, 1)
            for f in range(DT):
                act.wait_ge(full, f + 1)
                act.activation(mem.xT[:, f, :], acc[f % 2][:, 0:TOK], ACT.Copy).then_inc(x_moved, 1)
            for f in range(DT):
                act.wait_ge(x_moved, f + 1)
                nm.square(act, f, f % 2, mem.xT[:, f, :])
            nm.take_root(act)
            dn.split_hi_first(act)
            nm.apply_hi(act, 0)

        @block.vector
        def _(v):
            count = [0]

            def link(ins):
                count[0] += 1
                ins.then_inc(dve, 1)
                v.wait_ge(dve, count[0])

            v.wait_ge(dt_ready, 1)
            dtb = dtr[:, :].unsqueeze(2).broadcast_to([NP, 2, ST])
            for q in range(2):
                v.tensor_tensor(lrow[:, q, :].rearrange("c (e p) -> c e p", e=2),
                                lam[:, q, :].rearrange("c (e p) -> c e p", e=2), dtb, ALU.mult)
            v.tensor_copy(lrow[:, 2:4, :], lam[:, :, :]).then_inc(rows, 1)
            v.wait_ge(l_full, 1)
            link(v.tensor_copy(ls[:, :, :], aux[2][:, 0:4 * NP].rearrange("p (q c) -> p q c", q=4)))
            v.sem_inc(a_in, 1)
            magic = 1.5 * 2.0 ** 23
            parts = (6.28125, 0.0019340515136718750, 2 * math.pi - 6.28125 - 0.0019340515136718750)
            link(v.tensor_scalar(dw[:, 1, :], ls[:, 1, :], 1.0 / (2 * math.pi), magic, ALU.mult, ALU.add))
            link(v.tensor_scalar(dw[:, 1, :], dw[:, 1, :], -magic, None, ALU.add))
            link(v.scalar_tensor_tensor(dw[:, 2, :], dw[:, 1, :], -parts[0], ls[:, 1, :], ALU.mult, ALU.add))
            link(v.scalar_tensor_tensor(dw[:, 2, :], dw[:, 1, :], -parts[1], dw[:, 2, :], ALU.mult, ALU.add))
            link(v.scalar_tensor_tensor(dw[:, 2, :], dw[:, 1, :], -parts[2], dw[:, 2, :], ALU.mult, ALU.add))
            top = 3.1415925
            link(v.tensor_scalar(dw[:, 3, :], dw[:, 2, :], top, -top, ALU.min, ALU.max))
            link(v.tensor_scalar(dw[:, 7, :], dw[:, 3, :], -1.0, None, ALU.mult))
            link(v.tensor_tensor(dw[:, 7, :], dw[:, 7, :], dw[:, 3, :], ALU.max))
            link(v.tensor_scalar(dw[:, 4, :], dw[:, 7, :], -1.0, math.pi / 2, ALU.mult, ALU.add))
            v.sem_inc(a_in, 1)
            v.memset(mem.apow[:, 0, 0, :], 1.0)
            link(v.memset(mem.apow[:, 0, 1, :], 0.0))
            v.wait_ge(a_out, 2)
            v.tensor_tensor(mem.apow[:, 1, 0, :], dw[:, 0, :], dw[:, 6, :], ALU.mult)
            link(v.tensor_tensor(mem.apow[:, 1, 1, :], dw[:, 0, :], dw[:, 5, :], ALU.mult))
            nr, ar, ai, lr, li = dw[:, 8, :], mem.apow[:, 1, 0, :], mem.apow[:, 1, 1, :], ls[:, 2, :], ls[:, 3, :]
            v.tensor_scalar(nr, ar, -1.0, None, ALU.add)
            v.tensor_tensor(dw[:, 9, :], lr, lr, ALU.mult)
            link(v.tensor_tensor(dw[:, 10, :], li, li, ALU.mult))
            link(v.tensor_tensor(dw[:, 9, :], dw[:, 9, :], dw[:, 10, :], ALU.add))
            v.reciprocal(dw[:, 11, :], dw[:, 9, :])
            v.tensor_tensor(dw[:, 12, :], nr, lr, ALU.mult)
            v.tensor_tensor(dw[:, 13, :], ai, li, ALU.mult)
            v.tensor_tensor(dw[:, 14, :], ai, lr, ALU.mult)
            link(v.tensor_tensor(dw[:, 15, :], nr, li, ALU.mult))
            v.tensor_tensor(dw[:, 12, :], dw[:, 12, :], dw[:, 13, :], ALU.add)
            link(v.tensor_tensor(dw[:, 14, :], dw[:, 14, :], dw[:, 15, :], ALU.subtract))
            cr, ci = dw[:, 1, :], dw[:, 2, :]
            v.tensor_tensor(cr, dw[:, 12, :], dw[:, 11, :], ALU.mult)
            link(v.tensor_tensor(ci, dw[:, 14, :], dw[:, 11, :], ALU.mult))
            for n in (1, 2, 4):
                ar, ai = mem.apow[:, 1:n + 1, 0, :], mem.apow[:, 1:n + 1, 1, :]
                br = mem.apow[:, n, 0, :].unsqueeze(1).broadcast_to([P, n, NP])
                bi = mem.apow[:, n, 1, :].unsqueeze(1).broadcast_to([P, n, NP])
                v.tensor_tensor(tm[:, 0, 0:n, :], ar, br, ALU.mult)
                v.tensor_tensor(tm[:, 1, 0:n, :], ai, bi, ALU.mult)
                v.tensor_tensor(tm[:, 2, 0:n, :], ar, bi, ALU.mult)
                link(v.tensor_tensor(tm[:, 3, 0:n, :], ai, br, ALU.mult))
                v.tensor_tensor(mem.apow[:, n + 1:2 * n + 1, 0, :], tm[:, 0, 0:n, :], tm[:, 1, 0:n, :], ALU.subtract)
                link(v.tensor_tensor(mem.apow[:, n + 1:2 * n + 1, 1, :], tm[:, 2, 0:n, :], tm[:, 3, 0:n, :], ALU.add))
            for j in range(L):
                ar, ai = mem.apow[:, L - 1 - j, 0, :], mem.apow[:, L - 1 - j, 1, :]
                v.tensor_tensor(tm[:, 0, 0, :], ar, cr, ALU.mult)
                v.tensor_tensor(tm[:, 1, 0, :], ai, ci, ALU.mult)
                v.tensor_tensor(tm[:, 2, 0, :], ar, ci, ALU.mult)
                link(v.tensor_tensor(tm[:, 3, 0, :], ai, cr, ALU.mult))
                v.tensor_tensor(mem.cb[:, j, 0, :], tm[:, 0, 0, :], tm[:, 1, 0, :], ALU.subtract)
                link(v.tensor_tensor(mem.cb[:, j, 1, :], tm[:, 2, 0, :], tm[:, 3, 0, :], ALU.add))
            v.sem_inc(free, 8)
            v.wait_ge(full, 9)
            v.tensor_copy(mem.vec[:, :], aux[3][:, 0:NVEC]).then_inc(free, 1)
            v.wait_ge(free, 9)
            v.wait_ge(x_moved, DT)
            nm.invert(v)
            nm.apply(v, V_APRE, 0)
            for r in range(4):
                v.wait_ge(full, 10 + r)
                pairs = slice(NP // 2 * (r % 2), NP // 2 * (r % 2) + NP // 2)
                v.tensor_copy(mem.Ct[:, r // 2, pairs, :], aux[2 + r % 2][:, :].rearrange("p (c o) -> p c o", o=CH)).then_inc(free, 1)
            for ri in range(2):
                v.wait_ge(full, 14 + ri)
                v.tensor_copy(mem.XH[:, C_FIRST:C_LAST, ri, :], aux[2 + ri][:, :].rearrange("p (s c) -> p s c", s=NS))


class Norm:

    def __init__(self, nc, mem, name, at):
        def sem(x):
            return nc.alloc_semaphore(f"{name}_{x}")

        self.nc, self.mem, self.name = nc, mem, name
        self.sq = []
        self.tmp = []
        for s in range(2):
            t, at = mem.at(f"{name}_sq{s}", [P, TOK], at)
            self.sq.append(t)
        for s in range(2):
            t, at = mem.at(f"{name}_tmp{s}", [P, TOK], at)
            self.tmp.append(t)
        self.root, at = mem.at(f"{name}_root", [P, TOK], at)
        self.rstd, at = mem.at(f"{name}_rstd", [P, TOK], at)
        self.end = at
        self.squared, self.summed = sem("squared"), sem("summed")
        self.rooted, self.rstd_ready = sem("rooted"), sem("rstd_ready")
        self.scaled, self.act_hi, self.act_lo = sem("scaled"), sem("act_hi"), sem("act_lo")

    def start(self, pe):
        pe.sem_inc(self.summed, 2)

    def square(self, act, f, q, x):
        act.wait_ge(self.summed, f + 1)
        act.activation(self.sq[q][:, :], x, ACT.Square).then_inc(self.squared, 1)

    def add(self, pe, f, q, first=False, last=False):
        pe.wait_ge(self.squared, f + 1)
        for h, (lo, hi) in enumerate(CUTS):
            ins = self.nc.tensor.matmul(self.mem.aux[h][:, 0:hi - lo], self.mem.ones[:, :],
                                        self.sq[q][:, lo:hi], start=first, stop=last)
        ins.then_inc(self.summed, 1)

    def take_root(self, act):
        act.wait_ge(self.summed, DT + 2)
        for h, (lo, hi) in enumerate(CUTS):
            ins = act.activation(self.root[:, lo:hi], self.mem.aux[h][:, 0:hi - lo], ACT.Sqrt,
                                 scale=1.0 / D, bias=self.mem.cst[:, 0:1])
        ins.then_inc(self.rooted, 1)

    def invert(self, v):
        v.wait_ge(self.rooted, 1)
        v.reciprocal(self.rstd[:, :], self.root[:, :]).then_inc(self.rstd_ready, 1)
        v.wait_ge(self.rstd_ready, 1)

    def apply(self, v, gains, first, n0=0):
        mem = self.mem

        def low(f):
            v.wait_ge(self.act_hi, n0 + f + 1)
            v.tensor_tensor(mem.actl[:, first + f, :], self.tmp[f % 2][:, :],
                            mem.acth[:, first + f, :].bitcast(F32), ALU.subtract).then_inc(self.act_lo, 1)

        for f in range(DT):
            if f >= 2:
                v.wait_ge(self.act_lo, n0 + f - 1)
            v.scalar_tensor_tensor(self.tmp[f % 2][:, :], mem.xT[:, f, :], mem.vec[:, gains + f:gains + f + 1],
                                   self.rstd[:, :], ALU.mult, ALU.mult).then_inc(self.scaled, 1)
            if f >= 1:
                low(f - 1)
        low(DT - 1)
        v.wait_ge(self.act_lo, n0 + DT)

    def apply_tile(self, v, gains, first, f, n0):
        mem = self.mem
        v.scalar_tensor_tensor(self.tmp[f % 2][:, :], mem.xT[:, f, :], mem.vec[:, gains + f:gains + f + 1],
                               self.rstd[:, :], ALU.mult, ALU.mult).then_inc(self.scaled, 1)
        v.wait_ge(self.act_hi, n0 + f + 1)
        v.tensor_tensor(mem.actl[:, first + f, :], self.tmp[f % 2][:, :],
                        mem.acth[:, first + f, :].bitcast(F32), ALU.subtract).then_inc(self.act_lo, 1)
        v.wait_ge(self.act_lo, n0 + f + 1)

    def apply_tile_hi(self, act, first, f, n0):
        act.wait_ge(self.scaled, n0 + f + 1)
        act.activation(self.mem.acth[:, first + f, :], self.tmp[f % 2][:, :], ACT.Copy).then_inc(self.act_hi, 1)

    def apply_hi(self, act, first, n0=0):
        for f in range(DT):
            act.wait_ge(self.scaled, n0 + f + 1)
            act.activation(self.mem.acth[:, first + f, :], self.tmp[f % 2][:, :], ACT.Copy).then_inc(self.act_hi, 1)


NB = 8
BG = G // NB
BP = BG // 2


def states(nc, mem, ten, dram):
    U = []
    o = mem.p1_at
    for s in range(2):
        t, o = mem.at(f"Ux{s}", [P, BG, UC], o)
        U.append(t)
    tab, o = mem.at("b_tab", [P, BP, 2, P], o)
    tabT, o = mem.at("b_tabT", [P, BP, 2, P], o)
    a = mem.acth_at + DT * TOK * 4
    cbd, a = mem.at("c_blockdiag", [P, BP, 2, 2, CH], a)
    ust = []
    for s in range(2):
        t, a = mem.at(f"u_out{s}", [P, TOK], a)
        ust.append(t)
    t1, a = mem.at("tab_t1", [P, BP, L, CH], a)
    t2, a = mem.at("tab_t2", [P, BP, L, CH], a)
    assert a <= mem.actl_at
    aux = mem.aux
    su, w = dram["u"], blocks(ten["a_w_in"][0, :, :])
    su_p = su[:, 0:SEQ].rearrange("(g i) (j c) -> j i g c", i=CH, j=L)
    su_s = su[:, SEQ:TOK].rearrange("(g i) s -> i g s", i=CH)

    with ExitStack() as ctx:
        def sem(x):
            return nc.alloc_semaphore(f"states_{x}")

        dn = mem.u_proj
        mem.z_proj = nxt = Dense(nc, mem, "z_proj", 1, [w[:, :, W2 + P * n:W2 + P * n + P] for n in range(2)])
        zeroed = sem("zeroed")
        u_copied, u_stored = sem("u_copied"), sem("u_stored")
        chunks_stored = [sem("chunks_stored0"), sem("chunks_stored1")]
        U_in = [sem("U_in0"), sem("U_in1")]
        tab_ready, mul_done = sem("tab_ready"), sem("mul_done")
        tr_full, tr_free = sem("tr_full"), sem("tr_free")
        k_full, k_free = sem("k_full"), sem("k_free")
        x_full, x_free = sem("x_full"), sem("x_free")
        block = ctx.enter_context(nc.Block())

        @block.sync
        def _(sp):
            def load(b):
                for i in range(2):
                    dn.load(sp, 2 * b + i, i, w[:, :, cols(2 * b + i)])

            def store_chunks(b, s, turn):
                sp.wait_ge(U_in[s], 160 * turn + 160)
                at = dram["u_chunks"][bass.ds(b, 1), :, :, :].rearrange("b p g n -> (b p) g n")
                sp.dma_start(at, U[s][:, :, 0:YC]).then_inc(chunks_stored[s], 16)

            def store_and_gather(b, s, turn):
                for i in range(2):
                    sp.wait_ge(u_copied, 2 * b + i + 1)
                    sp.dma_start(su[cols(2 * b + i), :], ust[i][:, :]).then_inc(u_stored, 16)
                sp.wait_ge(u_stored, 32 * b + 64)
                sp.wait_ge(x_full, 4 * b + 4)
                sp.wait_ge(chunks_stored[s], 16 * turn + 16)
                for j in range(L):
                    sp.dma_start(U[s][CH * j:CH * j + CH, :, 0:NC], su_p[j, :, cols(b, BG), :]).then_inc(U_in[s], 16)
                sp.dma_start(U[s][0:CH, :, C_FIRST:C_LAST], su_s[:, cols(b, BG), :]).then_inc(U_in[s], 16)
                sp.dma_start(U[s][P - CH:P, :, C_LAST:UC], su_s[:, cols(b, BG), :]).then_inc(U_in[s], 16)

            sp.sem_inc(u_stored, 32)
            for s in range(2):
                sp.sem_inc(chunks_stored[s], 16)
            sp.wait_ge(zeroed, 2)

            load(1)
            store_and_gather(0, 0, 0)

            def batch(b, q, h):
                load(b)
                store_chunks(b - 2, q, h - 1)
                store_and_gather(b - 1, 1 - q, h - 1 if q == 0 else h)
            paired(sp, 2, NB, batch)
            nxt.load_first(sp, dn, WT)
            store_chunks(NB - 2, 0, NB // 2 - 1)
            store_and_gather(NB - 1, 1, NB // 2 - 1)
            store_chunks(NB - 1, 1, NB // 2 - 1)
            for s in range(2):
                sp.wait_ge(chunks_stored[s], 16 * (NB // 2) + 16)

        @block.gpsimd
        def _(pool):
            for s in range(2):
                pool.memset(U[s][:, :, :], 0.0).then_inc(zeroed, 1)
            pool.memset(cbd[:, :, :, :, :], 0.0).then_inc(zeroed, 1)
            paired(pool, 2, WT, lambda n, q, h: dn.split_lo(pool, n, q))
            nxt.split_lo_first(pool)

        @block.scalar
        def _(act):

            def copy_u(m, i, b):
                dn.wait_tile(act, m)
                act.wait_ge(u_stored, 32 * b + 32)
                act.activation(ust[i][:, :], columns(mem.acc[i]), ACT.Copy).then_inc(u_copied, 1)
                act.wait_ge(u_copied, m + 1)
                act.sem_inc(dn.acc_free[i], 1)

            def copy_tab(b):
                for r in range(4):
                    act.wait_ge(tr_full, 4 * b + r + 1)
                    act.activation(tabT[:, 2 * r:2 * r + 2, :, :],
                                   aux[r % 2][:, :].rearrange("p (c z m) -> p c z m", c=2, z=2),
                                   ACT.Copy).then_inc(tr_free, 1)

            def batch(b, q, h):
                for i in range(2):
                    copy_u(2 * b - 2 + i, i, b - 1)
                    dn.split_hi(act, 2 * b + i, i, b)
                copy_tab(b - 1)
            paired(act, 1, NB, batch)
            for i in range(2):
                copy_u(WT - 2 + i, i, NB - 1)
            nxt.split_hi_first(act, dn, WT)
            copy_tab(NB - 1)

        @block.vector
        def _(v):
            v.sem_inc(mul_done, 1)
            v.wait_ge(zeroed, 3)

            def build(b):
                def coef(z):
                    return mem.cb[:, :, z, cols(b, BP)].rearrange("p j c -> p c j").unsqueeze(3).broadcast_to([P, BP, L, CH])

                def inp(z):
                    return mem.Bt[:, z, cols(b, BP), :].unsqueeze(2).broadcast_to([P, BP, L, CH])

                for z in range(2):
                    v.wait_ge(mul_done, 6 * b + 3 * z + 1)
                    v.tensor_tensor(t1[:, :, :, :], coef(0), inp(z), ALU.mult).then_inc(mul_done, 1)
                    v.tensor_tensor(t2[:, :, :, :], coef(1), inp(1 - z), ALU.mult).then_inc(mul_done, 1)
                    v.wait_ge(mul_done, 6 * b + 3 * z + 3)
                    v.tensor_tensor(tab[:, :, z, :], t1[:, :, :, :].rearrange("p c j i -> p c (j i)"),
                                    t2[:, :, :, :].rearrange("p c j i -> p c (j i)"),
                                    ALU.subtract if z == 0 else ALU.add).then_inc(mul_done, 1)
                v.wait_ge(mul_done, 6 * b + 7)
                for e in range(2):
                    q = slice(64 * e, 64 * e + 64)
                    v.tensor_copy(cbd[q, :, 0, e, :], mem.Ct[q, 0, cols(b, BP), :])
                    ins = v.tensor_scalar(cbd[q, :, 1, e, :], mem.Ct[q, 1, cols(b, BP), :], -1.0, None, ALU.mult)
                ins.then_inc(tab_ready, 1)

            def copy_k(b):
                v.wait_ge(k_full, b + 1)
                v.tensor_copy(mem.Ksb[:, cols(b, BG), :], aux[2][:, 0:BG * CH].rearrange("p (g o) -> p g o", o=CH)).then_inc(k_free, 1)

            def copy_x(b):
                for r in range(4):
                    v.wait_ge(x_full, 4 * (b + 2) + r + 1)
                    x = aux[2 + r % 2][:, 0:4 * UC].rearrange("p (c z n) -> p c z n", c=2, z=2)
                    for z in range(2):
                        pair = bass.ds(b * BP + 2 * r, 2)
                        v.tensor_copy(mem.XH[:, 1:NC + 1, z, pair].rearrange("p n c -> p c n"), x[:, :, z, 0:NC])
                        ins = v.tensor_copy(mem.Xs[:, :, z, pair].rearrange("p n c -> p c n"), x[:, :, z, C_LAST:UC])
                    ins.then_inc(x_free, 1)

            build(0)
            copy_k(0)

            def batch(b, q, h):
                build(b)
                copy_x(b - 1)
                copy_k(b)
            paired(v, 1, NB, batch)
            copy_x(NB - 1)

        @block.tensor
        def _(pe):
            pe.sem_inc(x_full, 8)
            pe.sem_inc(x_free, 2)
            pe.sem_inc(tr_free, 2)
            def tables(b):
                pe.wait_ge(tab_ready, b + 1)
                for r in range(4):
                    pe.wait_ge(tr_free, 4 * b + r + 1)
                    for c in range(2):
                        for z in range(2):
                            ins = nc.tensor.transpose(aux[r % 2][:, 256 * c + P * z:256 * c + P * z + P],
                                                      tab[:, 2 * r + c, z, :], mem.ident[:, :])
                    ins.then_inc(tr_full, 1)
                pe.wait_ge(x_free, 4 * b + 2)
                for c in range(BP):
                    for z in range(2):
                        ins = nc.tensor.matmul(aux[2][:, 32 * c:32 * c + 32], tab[:, c, z, :],
                                               cbd[:, c, z, :, :].rearrange("p e o -> p (e o)"), start=z == 0, stop=z == 1)
                ins.then_inc(k_full, 1)

            def inputs(b, s, turn):
                pe.wait_ge(U_in[s], 160 * turn + 160)
                pe.wait_ge(tr_free, 4 * b + 6)
                pe.wait_ge(k_free, b + 1)
                for r in range(4):
                    pe.wait_ge(x_free, 4 * b + r + 1)
                    for c in range(2 * r, 2 * r + 2):
                        for z in range(2):
                            for e in range(2):
                                at = UC * (2 * (c % 2) + z)
                                ins = nc.tensor.matmul(aux[2 + r % 2][64 * e:64 * e + 64, at:at + UC],
                                                       tabT[:, c, z, 64 * e:64 * e + 64], U[s][:, 2 * c + e, :],
                                                       start=True, stop=True)
                    ins.then_inc(x_full, 1)

            def u_tiles(b):
                for i in range(2):
                    dn.tile(pe, 2 * b + i, i, b, mem.acth, mem.actl)

            def batch(b, q, h):
                u_tiles(b)
                inputs(b - 1, 1 - q, h if q == 1 else h - 1)
                tables(b)
            u_tiles(1)
            tables(0)
            inputs(0, 0, 0)
            tables(1)
            paired(pe, 2, NB, batch)
            inputs(NB - 1, 1, NB // 2 - 1)


def gate_and_scan(nc, mem, ten, dram):
    o = mem.p1_at
    zst = []
    for s in range(2):
        t, o = mem.at(f"z_out{s}", [P, TOK], o)
        zst.append(t)
    a8i, o = mem.at("a8_im_signed", [P, 2, NP], o)
    m1, o = mem.at("scan_m1", [P, 2, NP], o)
    m2, o = mem.at("scan_m2", [P, 2, NP], o)
    so, o = mem.at("state_out", [P, 2, NS + 1, NP], o)
    s1, o = mem.at("state_t1", [P, NS, NP], o)
    s2, o = mem.at("state_t2", [P, NS, NP], o)
    srow, o = mem.at("state_rows", [NP, 2, NS + 1, P], o)
    zer = mem.Bt
    aux = mem.aux
    w = blocks(ten["a_w_in"][0, :, :])
    kk = dram["k"].rearrange("i g (t o) -> i g t o", o=CH)
    with ExitStack() as ctx:
        def sem(x):
            return nc.alloc_semaphore(f"scan_{x}")

        dn = mem.z_proj
        z_copied, k_stored = sem("z_copied"), sem("k_stored")
        z_stored = [sem("z_stored0"), sem("z_stored1")]
        zeroed, step, fin, ended = sem("zeroed"), sem("step"), sem("final"), sem("states_ready")
        s_full, s_free, s_out = sem("rows_full"), sem("rows_moved"), sem("rows_stored")
        block = ctx.enter_context(nc.Block())

        @block.sync
        def _(sp):
            for s in range(2):
                sp.sem_inc(z_stored[s], 16)
            for j in range(L):
                sp.dma_start(kk[:, :, 14 - j, :], mem.Ksb[CH * j:CH * j + CH, :, :]).then_inc(k_stored, 16)
            sp.wait_ge(zeroed, 1)
            for t in range(7):
                sp.dma_start(kk[:, :, t, :], zer[0:CH, :, :, :].rearrange("p z c o -> p (z c) o")).then_inc(k_stored, 16)

            def store(m, i):
                sp.wait_ge(z_copied, m + 1)
                sp.dma_start(dram["z"][cols(m), :], zst[i][:, :]).then_inc(z_stored[i], 16)

            def tile(m, i, h):
                dn.load(sp, m, i, w[:, :, bass.ds(W2 + m * P, P)])
                store(m - 2, i)
            paired(sp, 2, WT, tile)
            for i in range(2):
                store(WT - 2 + i, i)
            sp.wait_ge(s_free, 5)
            for z, (pn, sn) in enumerate((("p_re", "s_re"), ("p_im", "s_im"))):
                sp.dma_start(ten[pn][0, 0, :, :].rearrange("(c e) p -> c (e p)", e=2), srow[:, z, 0, :]).then_inc(s_out, 16)
                sp.dma_start(ten[sn][0, :, :, :].rearrange("s (c e) p -> c s (e p)", e=2), srow[:, z, 1:NS + 1, :]).then_inc(s_out, 16)
            sp.wait_ge(s_out, 64)
            sp.wait_ge(k_stored, 16 * 15)
            for s in range(2):
                sp.wait_ge(z_stored[s], 16 * (WT // 2) + 16)

        @block.gpsimd
        def _(pool):
            pool.memset(zer[0:CH, :, :, :], 0.0).then_inc(zeroed, 1)
            paired(pool, 2, WT, lambda n, q, h: dn.split_lo(pool, n, q))

        @block.scalar
        def _(act):
            def silu(m, i, h):
                dn.wait_tile(act, m)
                act.wait_ge(z_stored[i], 16 * h + 16)
                act.activation(zst[i][:, :], columns(mem.acc[i]), ACT.Silu).then_inc(z_copied, 1)
                act.wait_ge(z_copied, m + 1)
                act.sem_inc(dn.acc_free[i], 1)

            def tile(m, i, h):
                silu(m - 2, i, h - 1)
                dn.split_hi(act, m, i, h)
            paired(act, 2, WT, tile)
            for i in range(2):
                silu(WT - 2 + i, i, WT // 2 - 1)

        @block.vector
        def _(v):
            a8 = mem.apow[:, L, 0, :].unsqueeze(1).broadcast_to([P, 2, NP])
            v.tensor_scalar(a8i[:, 0, :], mem.apow[:, L, 1, :], -1.0, None, ALU.mult)
            v.tensor_copy(a8i[:, 1, :], mem.apow[:, L, 1, :]).then_inc(step, 1)
            v.wait_ge(step, 1)
            with v.Fori(0, NC // 4) as h:
                for q in range(4):
                    c = 4 * h + q
                    was = mem.XH[:, bass.ds(c, 1), :, :].rearrange("p n z c -> p (n z) c")
                    now = mem.XH[:, bass.ds(c + 1, 1), :, :].rearrange("p n z c -> p (n z) c")
                    v.tensor_tensor(m1[:, :, :], was, a8, ALU.mult)
                    v.tensor_tensor(m2[:, 0, :], was[:, 1, :], a8i[:, 0, :], ALU.mult)
                    v.tensor_tensor(m2[:, 1, :], was[:, 0, :], a8i[:, 1, :], ALU.mult).then_inc(step, 1)
                    v.wait_ge(step, 3 * c + 2)
                    v.tensor_tensor(m1[:, :, :], m1[:, :, :], m2[:, :, :], ALU.add).then_inc(step, 1)
                    v.wait_ge(step, 3 * c + 3)
                    v.tensor_tensor(now, now, m1[:, :, :], ALU.add).then_inc(step, 1)
                    v.wait_ge(step, 3 * c + 4)
            count = [0]

            def link(ins):
                count[0] += 1
                ins.then_inc(fin, 1)
                v.wait_ge(fin, count[0])

            hr = mem.XH[:, C_FIRST:C_LAST, 0, :]
            hi = mem.XH[:, C_FIRST:C_LAST, 1, :]
            ar = mem.apow[:, 1, 0, :].unsqueeze(1).broadcast_to([P, NS, NP])
            ai = mem.apow[:, 1, 1, :].unsqueeze(1).broadcast_to([P, NS, NP])
            for z, (x, y, op) in enumerate(((hr, hi, ALU.subtract), (hi, hr, ALU.add))):
                v.tensor_copy(so[:, z, 0, :], mem.XH[:, NC, z, :])
                v.tensor_tensor(s1[:, :, :], x, ar, ALU.mult)
                link(v.tensor_tensor(s2[:, :, :], y, ai, ALU.mult))
                link(v.tensor_tensor(s1[:, :, :], s1[:, :, :], s2[:, :, :], op))
                link(v.tensor_tensor(so[:, z, 1:NS + 1, :], s1[:, :, :], mem.Xs[:, :, z, :], ALU.add))
            v.sem_inc(ended, 1)
            rows = srow[:, :, :, :].rearrange("p z s m -> p (z s) m")
            for r in range(5):
                n = min(4, 18 - 4 * r)
                v.wait_ge(s_full, r + 1)
                v.tensor_copy(rows[:, 4 * r:4 * r + n, :],
                              aux[r % 4][0:NP, 0:P * n].rearrange("p (s m) -> p s m", m=P)).then_inc(s_free, 1)

        @block.tensor
        def _(pe):
            dn.start(pe)
            paired(pe, 0, WT, lambda m, a, h: dn.tile(pe, m, a, h, mem.acth, mem.actl))
            pe.wait_ge(ended, 1)
            flat = so[:, :, :, :].rearrange("p z s c -> p (z s) c")
            for r in range(5):
                if r == 4:
                    pe.wait_ge(s_free, 1)
                for q in range(4 * r, min(4 * r + 4, 18)):
                    ins = nc.tensor.transpose(aux[r % 4][0:NP, P * (q % 4):P * (q % 4) + P], flat[:, q, :], mem.ident[:, :])
                ins.then_inc(s_full, 1)


def outputs(nc, mem, ten, dram):
    o = mem.p3_at
    T, U, C8, Y, hb, yt, ut = [], [], [], [], [], [], []
    for s in range(2):
        for name, shape, l in (("toeplitz", [P, BG, P], T), ("Uy", [P, BG, YC], U), ("Y", [P, BG, YC], Y),
                               ("h_spread", [P, 2, BP // 2, 2, YC], hb), ("y_in", [P, TOK], yt), ("u_in", [P, TOK], ut)):
            t, o = mem.at(f"{name}{s}", shape, o)
            l.append(t)
    o = mem.ring_at
    t1, o = mem.at("c_t1", [P, BP, L, CH], o)
    t2, o = mem.at("c_t2", [P, BP, L, CH], o)
    for s in range(2):
        t, o = mem.at(f"c_tab{s}", [P, BP, 2, P], o)
        C8.append(t)
    w_glu = blocks(ten["a_w_glu"][0, :, :])
    mem.glu = nxt = Dense(nc, mem, "glu", 2, [w_glu[:, 8 * n:8 * n + 8, W2:W2 + P] for n in range(2)])
    assert o <= mem.rest
    aux = mem.aux
    kk, su, sy = dram["k"], dram["u"], dram["y"]
    sy_p = sy[:, 0:SEQ].rearrange("(g i) (j c) -> j i g c", i=CH, j=L)
    sy_s = sy[:, SEQ:TOK].rearrange("(g i) s -> i g s", i=CH)
    with ExitStack() as ctx:
        def sem(x):
            return nc.alloc_semaphore(f"outputs_{x}")

        zeroed = sem("zeroed")
        T_in = [sem("T_in0"), sem("T_in1")]
        U_in = [sem("U_in0"), sem("U_in1")]
        y_full, y_copied = sem("y_full"), sem("y_copied")
        y_stored = [sem("y_stored0"), sem("y_stored1")]
        y_in, u_in = [sem("y_in0"), sem("y_in1")], [sem("u_in0"), sem("u_in1")]
        mul, tab, dense = sem("mul_done"), sem("tab_ready"), sem("h_dense")
        skip, gel, hi_r, lo_r = sem("skip_added"), sem("gelu_done"), sem("hi_ready"), sem("lo_ready")
        block = ctx.enter_context(nc.Block())

        @block.sync
        def _(sp):
            for s in range(2):
                sp.sem_inc(y_stored[s], 16)

            def load(b, s):
                sp.wait_ge(y_full, 2 * b + 2)
                for j in range(L):
                    sp.dma_start(T[s][CH * j:CH * j + CH, :, :], kk[:, cols(b, BG), CH * (7 - j):CH * (15 - j)]).then_inc(T_in[s], 16)
                u = dram["u_chunks"][bass.ds(b, 1), :, :, :].rearrange("b p g n -> (b p) g n")
                sp.dma_start(U[s][:, :, :], u).then_inc(U_in[s], 16)

            def fetch(b, s, turn):
                sp.wait_ge(y_stored[s], 144 * turn + 160)
                for i in range(2):
                    m = 2 * b + i
                    sp.wait_ge(lo_r, m + 1)
                    sp.dma_start(yt[i][:, :], sy[cols(m), :]).then_inc(y_in[i], 16)
                    sp.dma_start(ut[i][:, :], su[cols(m), :]).then_inc(u_in[i], 16)

            def store_y(b, s):
                sp.wait_ge(y_copied, 4 * b + 8)
                for j in range(L):
                    sp.dma_start(sy_p[j, :, cols(b, BG), :], Y[s][CH * j:CH * j + CH, :, 0:NC]).then_inc(y_stored[s], 16)
                sp.dma_start(sy_s[:, cols(b, BG), :], Y[s][0:CH, :, C_FIRST:C_LAST]).then_inc(y_stored[s], 16)

            load(0, 0)
            load(1, 1)
            store_y(0, 0)

            def batch(b, q, h):
                load(b, q)
                fetch(b - 2, q, h - 1)
                store_y(b - 1, 1 - q)
            paired(sp, 2, NB, batch)
            sp.wait_ge(mul, 6 * NB + 1)
            nxt.load_first(sp)
            fetch(NB - 2, 0, NB // 2 - 1)
            store_y(NB - 1, 1)
            fetch(NB - 1, 1, NB // 2 - 1)
            nxt.load_second(sp, [w_glu[:, 8 * n:8 * n + 8, 0:P] for n in range(2)])

        @block.gpsimd
        def _(pool):
            for s in range(2):
                pool.memset(hb[s][:, :, :, :, :], 0.0).then_inc(zeroed, 1)
            nxt.split_lo_first(pool)

        @block.tensor
        def _(pe):
            pe.sem_inc(y_full, 4)

            def batch(b, s, turn):
                pe.wait_ge(T_in[s], 128 * turn + 128)
                pe.wait_ge(U_in[s], 16 * turn + 16)
                pe.wait_ge(tab, b + 1)
                for r in range(2):
                    pe.wait_ge(dense, 2 * b + r + 1)
                    pe.wait_ge(y_copied, 4 * b + 2 * r + 2)
                    for c in range(4 * r, 4 * r + 4):
                        y = aux[2 * r + c % 4 // 2][:, 256 * (c % 2):256 * (c % 2) + 2 * YC]
                        for z in range(2):
                            nc.tensor.matmul(y, C8[s][:, c, z, :], hb[r][:, z, c % 4, :, :].rearrange("p e n -> p (e n)"),
                                             start=z == 0, stop=False)
                        for e in range(2):
                            ins = nc.tensor.matmul(y[:, YC * e:YC * e + YC], T[s][:, 2 * c + e, :], U[s][:, 2 * c + e, 0:YC],
                                                   start=False, stop=e == 1)
                    ins.then_inc(y_full, 1)
            paired(pe, 0, NB, batch)
            nxt.start(pe)
            nxt.early_tile(pe, mem.acth, mem.actl, lambda k: pe.wait_ge(lo_r, k + 3))

        @block.scalar
        def _(act):
            def copy_y(b, s, turn):
                act.wait_ge(y_stored[s], 144 * turn + 16)
                for r in range(2):
                    act.wait_ge(y_full, 2 * b + 5 + r)
                    for e in range(2):
                        first = 8 * r + 4 * e
                        act.activation(Y[s][:, first:first + 4, :].rearrange("p (c g) n -> p c (g n)", g=2),
                                       aux[2 * r + e][:, :].rearrange("p (c n) -> p c n", c=2)[:, :, 0:2 * YC],
                                       ACT.Copy).then_inc(y_copied, 1)

            def gelu(m, i):
                act.wait_ge(skip, m + 2)
                act.activation(yt[i][:, :], yt[i][:, :], ACT.Gelu_apprx_tanh).then_inc(gel, 1)
                act.wait_ge(gel, m + 1)
                act.activation(mem.acth[:, bass.ds(m, 1), :].rearrange("p o n -> p (o n)"), yt[i][:, :], ACT.Copy).then_inc(hi_r, 1)

            act.sem_inc(y_copied, 4)
            for b in range(2):
                copy_y(b, b, 0)

            def batch(b, q, h):
                for i in range(2):
                    gelu(2 * b - 4 + i, i)
                copy_y(b, q, h)
            paired(act, 2, NB, batch)
            act.wait_ge(y_full, 2 * NB + 4)
            nxt.split_hi_first(act)
            for m in range(WT - 4, WT):
                gelu(m, m % 2)

        @block.vector
        def _(v):
            v.sem_inc(lo_r, 2)
            v.sem_inc(skip, 1)
            v.sem_inc(mul, 1)
            v.wait_ge(zeroed, 2)

            def build(b, s):
                def power(z):
                    return mem.apow[:, 1:L + 1, z, cols(b, BP)].rearrange("p j c -> p c j").unsqueeze(3).broadcast_to([P, BP, L, CH])

                def c(z):
                    return mem.Ct[:, z, cols(b, BP), :].unsqueeze(2).broadcast_to([P, BP, L, CH])

                v.wait_ge(y_full, 2 * b + 2)
                for z in range(2):
                    v.wait_ge(mul, 6 * b + 3 * z + 1)
                    v.tensor_tensor(t1[:, :, :, :], c(z), power(0), ALU.mult).then_inc(mul, 1)
                    v.tensor_tensor(t2[:, :, :, :], c(1 - z), power(1), ALU.mult).then_inc(mul, 1)
                    v.wait_ge(mul, 6 * b + 3 * z + 3)
                    a, d = (x[:, :, :, :].rearrange("p c j i -> p c (j i)") for x in (t1, t2))
                    if z == 0:
                        v.tensor_tensor(C8[s][:, :, 0, :], a, d, ALU.subtract).then_inc(mul, 1)
                    else:
                        v.scalar_tensor_tensor(C8[s][:, :, 1, :], a, -1.0, d, ALU.mult, ALU.subtract).then_inc(mul, 1)
                v.wait_ge(mul, 6 * b + 7)
                v.sem_inc(tab, 1)
                for r in range(2):
                    v.wait_ge(y_full, 2 * b + r + 3)
                    pairs = bass.ds(b * BP + BP // 2 * r, BP // 2)
                    for z in range(2):
                        for e in range(2):
                            q = slice(64 * e, 64 * e + 64)
                            ins = v.tensor_copy(hb[r][q, z, :, e, :], mem.XH[q, 0:YC, z, pairs].rearrange("p n c -> p c n"))
                    ins.then_inc(dense, 1)

            def add_skip(m, i, turn):
                v.wait_ge(y_in[i], 16 * turn + 16)
                v.wait_ge(u_in[i], 16 * turn + 16)
                v.scalar_tensor_tensor(yt[i][:, :], ut[i][:, :], mem.vec[:, bass.ds(V_D + m, 1)], yt[i][:, :],
                                       ALU.mult, ALU.add).then_inc(skip, 1)

            def low(m, i):
                v.wait_ge(hi_r, m + 1)
                at = bass.ds(m, 1)
                v.tensor_tensor(mem.actl[:, at, :].rearrange("p o n -> p (o n)"), yt[i][:, :],
                                mem.acth[:, at, :].rearrange("p o n -> p (o n)").bitcast(F32), ALU.subtract).then_inc(lo_r, 1)

            build(0, 0)
            build(1, 1)

            def batch(b, q, h, first=False):
                if not first:
                    for i in range(2):
                        low(2 * b - 6 + i, i)
                build(b, q)
                for i in range(2):
                    add_skip(2 * b - 4 + i, i, b - 2)
            batch(2, 0, 1, True)
            paired(v, 3, NB, batch)
            for m in range(WT - 6, WT, 2):
                for i in range(2):
                    low(m + i, i)
                if m < WT - 2:
                    for i in range(2):
                        add_skip(m + 2 + i, i, m // 2 + 1)


def glu(nc, mem, ten, dram):
    o = mem.rest
    mem.yh, o = mem.at("y_hi", [P, WT, TOK], o, F32R)
    mem.yl, o = mem.at("y_lo", [P, WT, TOK], o, F32R)
    mem.glu_end = o
    sg, zt, yt = [], [], []
    for s in range(2):
        for name, l in (("sig", sg), ("z_in", zt), ("y_f32", yt)):
            t, o = mem.at(f"{name}{s}", [P, TOK], o)
            l.append(t)
    w = blocks(ten["a_w_glu"][0, :, :])
    with ExitStack() as ctx:
        def sem(x):
            return nc.alloc_semaphore(f"gate_{x}")

        dn = mem.glu
        w_out = blocks(ten["a_w_out"][0, :, :])
        mem.a_out = nxt = Dense(nc, mem, "a_out", 2, [w_out[:, 8 * n:8 * n + 8, 0:P] for n in range(2)])
        z_in = [sem("z_in0"), sem("z_in1")]
        gated, prod = sem("gated"), sem("product")
        hi_r, lo_r = sem("hi_ready"), sem("lo_ready")
        block = ctx.enter_context(nc.Block())

        @block.sync
        def _(sp):
            def tile(i, s, h, have=0):
                for a in range(have, 2):
                    for u in range(2):
                        at = bass.ds((i + WT) * P - a * W2, P)
                        dn.load(sp, 4 * i + 2 * a + u, u, w[:, 8 * u:8 * u + 8, at])
                sp.wait_ge(prod, i + 1)
                sp.dma_start(zt[s][:, :], dram["z"][cols(i), :]).then_inc(z_in[s], 16)
            sp.sem_inc(prod, 2)
            tile(0, 0, 0, 2)
            paired(sp, 1, WT, tile)
            nxt.load_first(sp, dn, 4 * WT)
            nxt.load_second(sp, [w_out[:, 8 * n:8 * n + 8, P:2 * P] for n in range(2)])

        @block.gpsimd
        def _(pool):
            paired(pool, 2, 4 * WT, lambda n, q, h: dn.split_lo(pool, n, q))
            nxt.split_lo_first(pool)

        @block.tensor
        def _(pe):
            paired(pe, 1, 2 * WT, lambda m, a, h: dn.tile(pe, m, a, h, mem.acth, mem.actl))
            nxt.start(pe)
            pe.wait_ge(dn.acc_free[0], WT + 1)
            nxt.early_tile(pe, mem.yh, mem.yl, lambda k: pe.wait_ge(lo_r, k + 3))

        @block.scalar
        def _(act):
            def high(i, s):
                act.wait_ge(prod, i + 3)
                act.activation(mem.yh[:, bass.ds(i, 1), :].rearrange("p o n -> p (o n)"), yt[s][:, :], ACT.Copy).then_inc(hi_r, 1)

            def tile(i, s, h, first=False):
                if not first:
                    dn.split_hi(act, 4 * i, 0, 2 * i)
                    dn.split_hi(act, 4 * i + 1, 1, 2 * i)
                    high(i - 1, 1 - s)
                dn.split_hi(act, 4 * i + 2, 0, 2 * i + 1)
                dn.wait_tile(act, 2 * i)
                act.wait_ge(gated, i)
                act.activation(sg[s][:, :], columns(mem.acc[0]), ACT.Sigmoid,
                               bias=mem.vec[:, bass.ds(V_BGLU + WT + i, 1)]).then_inc(dn.acc_free[0], 1)
                dn.split_hi(act, 4 * i + 3, 1, 2 * i + 1)
            act.sem_inc(gated, 1)
            tile(0, 0, 0, True)
            paired(act, 1, WT, tile)
            high(WT - 1, 1)
            nxt.split_hi_first(act, dn, 4 * WT)

        @block.vector
        def _(v):
            def tile(i, s, h):
                dn.wait_tile(v, 2 * i + 1)
                v.wait_ge(dn.acc_free[0], i + 2)
                v.scalar_tensor_tensor(sg[s][:, :], columns(mem.acc[1]), mem.vec[:, bass.ds(V_BGLU + i, 1)],
                                       sg[s][:, :], ALU.add, ALU.mult).then_inc(dn.acc_free[1], 1)
                v.wait_ge(dn.acc_free[1], i + 2)
                v.sem_inc(gated, 1)
                v.wait_ge(z_in[s], 16 * h + 16)
                v.wait_ge(lo_r, i + 1)
                v.tensor_tensor(yt[s][:, :], sg[s][:, :], zt[s][:, :], ALU.mult).then_inc(prod, 1)
                v.wait_ge(hi_r, i + 1)
                at = bass.ds(i, 1)
                v.tensor_tensor(mem.yl[:, at, :].rearrange("p o n -> p (o n)"), yt[s][:, :],
                                mem.yh[:, at, :].rearrange("p o n -> p (o n)").bitcast(F32), ALU.subtract).then_inc(lo_r, 1)
            v.sem_inc(lo_r, 2)
            paired(v, 0, WT, tile)


def residual(nc, mem, name, dn, ten_w, units, xh, xl, gains, o_at, norm_at, natural=False, next_norm=None,
             nxt=None):
    ot, _ = mem.at(f"{name}_o", [P, DT, TOK], o_at)
    w = blocks(ten_w)
    with ExitStack() as ctx:
        def sem(x):
            return nc.alloc_semaphore(f"{name}_{x}")

        nm = Norm(nc, mem, name + "_post", norm_at)
        added = sem("added")
        block = ctx.enter_context(nc.Block())

        @block.sync
        def _(sp):
            def tile(m, a, h):
                for u in range(units):
                    s = u if units == 2 else a
                    dn.load(sp, units * m + u, s, w[:, 8 * u:8 * u + 8, cols(m)])
            paired(sp, 2, DT, tile)
            if nxt:
                nxt.load_first(sp, dn, units * DT)

        @block.gpsimd
        def _(pool):
            paired(pool, 2, units * DT, lambda n, q, h: dn.split_lo(pool, n, q))
            if nxt:
                nxt.split_lo_first(pool)

        @block.scalar
        def _(act):
            def square(m, q, h):
                act.wait_ge(dn.acc_free[q], h + 2)
                nm.square(act, m, q, ot[:, bass.ds(m, 1), :].rearrange("p o n -> p (o n)"))

            def tile(m, a, h, first=False):
                if units == 2:
                    dn.split_hi(act, 2 * m, 0, m)
                else:
                    dn.split_hi(act, m, a, h)
                if not first:
                    square(m - 2, a, h - 1)
                if units == 2:
                    dn.split_hi(act, 2 * m + 1, 1, m)
            if units == 2:
                tile(1, 1, 0, True)
            paired(act, 2, DT, tile)
            if nxt:
                nxt.split_hi_first(act, dn, units * DT)
            for m in range(DT - 2, DT):
                square(m, m % 2, m // 2)
            nm.take_root(act)
            if next_norm:
                for f in range(DT):
                    act.wait_ge(added, 2 * f + 2)
                    next_norm.square(act, f, f % 2, mem.xT[:, f, :])
                next_norm.take_root(act)

        @block.tensor
        def _(pe):
            if units == 1:
                dn.start(pe)
            nm.start(pe)

            def tile(m, a, h):
                dn.tile(pe, m, a, h, xh, xl)
                nm.add(pe, m - 1, 1 - a)
            if units == 1:
                dn.tile(pe, 0, 0, 0, xh, xl)
            dn.tile(pe, 1, 1, 0, xh, xl)
            nm.add(pe, 0, 0, first=True)
            paired(pe, 2, DT, tile)
            nm.add(pe, DT - 1, (DT - 1) % 2, last=True)
            if next_norm:
                next_norm.start(pe)
                pe.wait_ge(nm.rooted, 1)
                for f in range(DT):
                    next_norm.add(pe, f, f % 2, f == 0, f == DT - 1)

        @block.vector
        def _(v):
            def tile(m, a, h):
                dn.wait_tile(v, m)
                x = ot[:, bass.ds(m, 1), :].rearrange("p o n -> p (o n)")
                if natural:
                    v.tensor_copy(x[:, 0:SEQ].rearrange("p (j c) -> p j c", j=L),
                                  columns(mem.acc[a])[:, 0:SEQ].rearrange("p (c j) -> p j c", j=L))
                    v.tensor_copy(x[:, SEQ:TOK], columns(mem.acc[a])[:, SEQ:TOK]).then_inc(dn.acc_free[a], 1)
                else:
                    v.tensor_copy(x, columns(mem.acc[a])).then_inc(dn.acc_free[a], 1)
            paired(v, 0, DT, tile)
            nm.invert(v)
            for f in range(DT):
                if f >= 2:
                    v.wait_ge(added, 2 * f - 2)
                v.scalar_tensor_tensor(nm.tmp[f % 2][:, :], ot[:, f, :], mem.vec[:, gains + f:gains + f + 1],
                                       nm.rstd[:, :], ALU.mult, ALU.mult).then_inc(added, 1)
                v.wait_ge(added, 2 * f + 1)
                v.tensor_tensor(mem.xT[:, f, :], mem.xT[:, f, :], nm.tmp[f % 2][:, :], ALU.add).then_inc(added, 1)
            v.wait_ge(added, 2 * DT)


def ssm_out(nc, mem, ten, dram):
    mem.kv_norm = Norm(nc, mem, "norm_kv", mem.glu_end + 6 * TOK * 4)
    wk = blocks(ten["w_kv"])
    mem.proj = Dense(nc, mem, "proj", 1, [wk[:, :, cols(n)] for n in range(2)])
    residual(nc, mem, "a_out", mem.a_out, ten["a_w_out"][0, :, :], 2, mem.yh, mem.yl, V_APOST, mem.acth_at, mem.glu_end,
             next_norm=mem.kv_norm, nxt=mem.proj)


def project(nc, mem, ten, dram):
    o = mem.rest
    mem.kv, o = mem.at("kvT", [P, 2 * DT, TOK], o)
    mem.v_at = mem.rest + DT * TOK * 4
    mem.q_at = o
    mem.q, o = mem.at("qT", [P, 3 * DT, TOK], o)
    mem.zb, o = mem.at("zb", [P, DT, TOK], o)
    mem.stat_at = o
    wk, wb = blocks(ten["w_kv"]), blocks(ten["b_w_in"][0, :, :])

    def in_token_order(op, out, tile, a, dn, *func, **scale):
        x = out[:, bass.ds(tile, 1), :].rearrange("p o n -> p (o n)")
        y = columns(mem.acc[a])
        op(x[:, 0:SEQ].rearrange("p (c j) -> p j c", j=L), y[:, 0:SEQ].rearrange("p (j c) -> p j c", j=L), *func, **scale)
        op(x[:, SEQ:TOK], y[:, SEQ:TOK], *func, **scale).then_inc(dn.acc_free[a], 1)

    with ExitStack() as ctx:
        def sem(x):
            return nc.alloc_semaphore(f"proj_{x}")

        dn = mem.proj
        nm = mem.kv_norm
        block = ctx.enter_context(nc.Block())

        @block.sync
        def _(sp):
            paired(sp, 2, 2 * DT, lambda m, s, h: dn.load(sp, m, s, wk[:, :, cols(m)]))
            paired(sp, 2 * DT, 6 * DT, lambda m, s, h: dn.load(sp, m, s, wb[:, :, bass.ds(m * P - 2 * D, P)]))

        @block.gpsimd
        def _(pool):
            paired(pool, 2, 6 * DT, lambda n, q, h: dn.split_lo(pool, n, q))

        @block.tensor
        def _(pe):
            dn.start(pe)
            dn.first_tiles(pe, mem.acth[:, 0:DT, :], mem.actl[:, 0:DT, :], lambda k: pe.wait_ge(nm.act_lo, k + 1))
            paired(pe, 2, 2 * DT, lambda m, a, h: dn.tile(pe, m, a, h, mem.acth[:, 0:DT, :], mem.actl[:, 0:DT, :]))
            pe.wait_ge(nm.act_lo, 2 * DT)
            paired(pe, 2 * DT, 6 * DT, lambda m, a, h: dn.tile(pe, m, a, h, mem.acth[:, DT:, :], mem.actl[:, DT:, :]))

        @block.scalar
        def _(act):
            nm.apply_hi(act, 0)
            for f in range(DT):
                dn.split_hi(act, f + 2, f % 2, f // 2 + 1)
                nm.apply_tile_hi(act, DT, f, DT)
            paired(act, DT + 2, 2 * DT + 2, lambda n, q, h: dn.split_hi(act, n, q, h))

            def q_tile(m, a, h):
                dn.wait_tile(act, m - 2)
                in_token_order(act.activation, mem.q, m - 2 - 2 * DT, a, dn, ACT.Copy, scale=HD ** -0.5)
                dn.split_hi(act, m, a, h)

            def z_tile(m, a):
                dn.wait_tile(act, m)
                in_token_order(act.activation, mem.zb, m - 5 * DT, a, dn, ACT.Silu)

            def z_next(m, a, h):
                z_tile(m - 2, a)
                dn.split_hi(act, m, a, h)
            paired(act, 2 * DT + 2, 5 * DT + 2, q_tile)
            paired(act, 5 * DT + 2, 6 * DT, z_next)
            z_tile(6 * DT - 2, 0)
            z_tile(6 * DT - 1, 1)

        @block.vector
        def _(v):
            nm.invert(v)
            nm.apply(v, V_KV, 0)

            def kv_tile(m, a, h):
                dn.wait_tile(v, m)
                in_token_order(v.tensor_copy, mem.kv, m, a, dn)
            for f in range(DT):
                kv_tile(f, f % 2, f // 2)
                nm.apply_tile(v, V_BPRE, DT, f, DT)
            paired(v, DT, 2 * DT, kv_tile)


def block_tokens(x, b):
    return x[:, P * b:P * b + P]


def residue_tokens(x, r):
    return x[:, r:r + 4 * (P - 1) + 1:4]


def token_rows(nc, mem, ten, dram):
    o = mem.acth_at
    mem.vnat, o = mem.at("v_block", [P, 4, D], o)
    mem.vres, o = mem.at("v_residue", [P, 4, D], o)
    mem.attn_at = o
    knat, o = mem.at("k_block", [P, 4, D], o)
    kvnew, o = mem.at("kv_new", [NS, 2, D], o)
    qsplit, o = mem.at("q_new", [NS, 2, 3, D], o, F32R)
    assert o <= mem.rest
    acc = mem.acc
    with ExitStack() as ctx:
        def sem(x):
            return nc.alloc_semaphore(f"rows_{x}")

        full, moved_a, moved_v, stored = sem("full"), sem("moved_act"), sem("moved_dve"), sem("stored")
        q_hi, q_lo = sem("q_hi_ready"), sem("q_lo_ready")
        block = ctx.enter_context(nc.Block())

        rounds = [("kb", b) for b in range(4)] + [("vb", b) for b in range(4)] + [("vr", r) for r in range(4)] + \
                 [("new", z) for z in range(2)] + [("q", g) for g in range(3)]

        def target(kind, i):
            return {"kb": knat, "vb": mem.vnat, "vr": mem.vres, "new": kvnew}[kind][:, i, :]

        @block.tensor
        def _(pe):
            for n, (kind, i) in enumerate(rounds):
                if n == len(rounds) - 1:
                    pe.wait_ge(q_lo, 1)
                elif n >= 2:
                    pe.wait_ge(moved_a if n % 2 == 0 else moved_v, n // 2)
                for f in range(DT):
                    if kind == "q":
                        src = mem.q[:, DT * i + f, :]
                    else:
                        src = mem.kv[:, f + (DT if kind[0] == "v" or (kind, i) == ("new", 1) else 0), :]
                    if kind in ("new", "q"):
                        out, src = acc[n % 2][0:NS, P * f:P * f + P], src[:, SEQ:TOK]
                    else:
                        out = acc[n % 2][:, P * f:P * f + P]
                        src = residue_tokens(src[:, 0:SEQ], i) if kind == "vr" else block_tokens(src[:, 0:SEQ], i)
                    ins = nc.tensor.transpose(out, src, mem.ident[:, :])
                ins.then_inc(full, 1)

        @block.scalar
        def _(act):
            for n in range(0, len(rounds) - 3, 2):
                rows = NS if rounds[n][0] in ("new", "q") else P
                act.wait_ge(full, n + 1)
                act.activation(target(*rounds[n]), acc[0][0:rows, :], ACT.Copy).then_inc(moved_a, 1)
            for g in range(3):
                n = len(rounds) - 3 + g
                act.wait_ge(full, n + 1)
                act.activation(qsplit[:, 0, g, :], acc[n % 2][0:NS, :], ACT.Copy).then_inc(q_hi, 1)

        @block.vector
        def _(v):
            for n in range(1, len(rounds) - 3, 2):
                rows = NS if rounds[n][0] in ("new", "q") else P
                v.wait_ge(full, n + 1)
                v.tensor_copy(target(*rounds[n]), acc[1][0:rows, :]).then_inc(moved_v, 1)
            for g in range(3):
                n = len(rounds) - 3 + g
                v.wait_ge(q_hi, g + 1)
                v.tensor_tensor(qsplit[:, 1, g, :], acc[n % 2][0:NS, :], qsplit[:, 0, g, :].bitcast(F32),
                                ALU.subtract).then_inc(q_lo, 1)

        @block.sync
        def _(sp):
            out = ten["p_kv"][0, :, :, :, :].rearrange("t z h d -> z t (h d)")
            for z, x in enumerate((knat, mem.vnat)):
                sp.wait_ge(moved_a, 2 * z + 2)
                sp.wait_ge(moved_v, 2 * z + 2)
                for b in range(4):
                    sp.dma_start(out[z, P * b:P * b + P, :], x[:, b, :]).then_inc(stored, 16)
            sp.wait_ge(moved_a, 7)
            sp.wait_ge(moved_v, 7)
            sp.dma_start(ten["s_kv"][:, SEQ - 1, :, :, :].rearrange("s z h d -> s z (h d)"), kvnew[:, :, :]).then_inc(stored, 16)
            sp.wait_ge(q_lo, 3)
            sp.dma_start(dram["q"], qsplit[:, :, :, :].bitcast(F32)).then_inc(stored, 16)
            sp.wait_ge(stored, 16 * 10)


HALVES = ((0, 12), (12, N_HEADS))


def attention(nc, mem, ten, dram):
    o = mem.attn_at
    far, o = mem.at("far_res", [P, 4, N_HEADS, HD + 2], o)
    near, o = mem.at("far_nat", [P, 4, N_HEADS, HD + 2], o)
    S, PT = [], []
    for s in range(2):
        t, o = mem.at(f"scores{s}", [P, 4, 2, P], o)
        S.append(t)
    for s in range(2):
        t, o = mem.at(f"probsT{s}", [P, 8, P], o)
        PT.append(t)
    dist, o = mem.at("distances", [P, 4, P], o)
    slope, o = mem.at("slopes", [P, 3 * N_HEADS], o)
    assert o <= mem.rest
    mem.o_nat, _ = mem.at("o_nat", [P, 4, D], mem.v_at)
    o = mem.stat_at
    nmax, o = mem.at("neg_max", [P, 4, 4], o)
    e12, o = mem.at("far_scale", [P, 4, 4], o)
    l0, o = mem.at("near_sum", [P, 4, 4], o)
    den, o = mem.at("denominator", [P, 2, 4], o)
    on, o = mem.at("joined", [P, 4, HD], o)
    aux, acc = mem.aux, mem.acc
    const = ten["constants"]

    with ExitStack() as ctx:
        def sem(x):
            return nc.alloc_semaphore(f"attn_{x}")

        c_in = sem("constants_in")
        s_full, biased, maxed, exped, summed = sem("scores"), sem("biased"), sem("maxed"), sem("exped"), sem("summed")
        t_full, t_moved, o_full, o_moved = sem("transposed"), sem("t_moved"), sem("out_full"), sem("out_moved")
        moved = [sem("far_moved0"), sem("far_moved1")]
        dve = sem("dve_chain")
        block = ctx.enter_context(nc.Block())
        units = [("far", h) for h in range(N_HEADS)] + [("near", h) for h in range(N_HEADS)]

        @block.sync
        def _(sp):
            sp.dma_start(dist[:, :, :], const[:, 0:4 * P].rearrange("p (a k) -> p a k", a=4)).then_inc(c_in, 16)
            sp.dma_start(slope[:, :], const[:, 4 * P:4 * P + 3 * N_HEADS]).then_inc(c_in, 16)
            for part, (h0, h1) in enumerate(HALVES):
                sp.wait_ge(o_moved, h1)
                for r in range(4):
                    for b in range(4):
                        sp.dma_start(near[r:r + 4 * 31 + 1:4, b, h0:h1, :],
                                     far[32 * b:32 * b + 32, r, h0:h1, :]).then_inc(moved[part], 16)

        @block.tensor
        def _(pe):
            def rows(h):
                return slice(HD * (h % 2), HD * (h % 2) + HD)

            def scores(n):
                kind, h = units[n]
                if n >= 2:
                    pe.wait_ge(biased, n - 1)
                q, k = mem.q[rows(h), :, 0:SEQ], mem.kv[rows(h), h // 2, 0:SEQ]
                out = acc[n % 2][:, :].rearrange("p (i g k) -> p i g k", i=4, g=2)
                for i in range(4):
                    if kind == "far":
                        for g in range(2):
                            ins = nc.tensor.matmul(out[:, i, g, :], residue_tokens(q[:, DT * (1 + g) + h // 2, :], i),
                                                   residue_tokens(k, i), start=True, stop=True)
                    else:
                        if i == 0:
                            ins = nc.tensor.matmul(out[:, 0, 1, :], block_tokens(q[:, h // 2, :], 0),
                                                   block_tokens(k, 0), start=True, stop=True)
                        else:
                            ins = nc.tensor.matmul(out[:, i, :, :], block_tokens(q[:, h // 2, :], i),
                                                   k[:, P * i - P:P * i + P], start=True, stop=True)
                ins.then_inc(s_full, 1)

            def transposes(n):
                kind, h = units[n]
                s = n % 2
                probs = S[s]
                far_unit = kind == "far"
                pe.wait_ge(summed, n + 1)
                if n >= 1:
                    pe.wait_ge(t_moved, 2 * n)
                for i in range(4):
                    nc.tensor.transpose(aux[0][:, P * i:P * i + P], probs[:, i, 0 if far_unit else 1, :], mem.ident[:, :])
                ins = None
                if not far_unit:
                    for i in range(1, 4):
                        ins = nc.tensor.transpose(aux[1][:, P * i:P * i + P], probs[:, i, 0, :], mem.ident[:, :])
                else:
                    ins = nc.tensor.transpose(aux[1][:, 0:P], probs[:, 0, 0, :], mem.ident[:, :])
                ins.then_inc(t_full, 1)

            def products(n):
                kind, h = units[n]
                s = n % 2
                far_unit = kind == "far"
                pe.wait_ge(t_moved, 2 * n + 2)
                if n >= 2:
                    pe.wait_ge(o_moved, n - 1)
                v = mem.vres if far_unit else mem.vnat
                for i in range(4):
                    out = aux[2 + s][:, HD * i:HD * i + HD]
                    two_blocks = not far_unit and i > 0
                    ins = nc.tensor.matmul(out, PT[s][:, i, :], v[:, i, HD * h:HD * h + HD], start=True, stop=not two_blocks)
                    if two_blocks:
                        ins = nc.tensor.matmul(out, PT[s][:, 4 + i, :], v[:, i - 1, HD * h:HD * h + HD], start=False, stop=True)
                ins.then_inc(o_full, 1)

            scores(0)
            scores(1)
            for n in range(len(units)):
                transposes(n)
                if n + 2 < len(units):
                    scores(n + 2)
                products(n)

        @block.vector
        def _(v):
            count = [0]

            def link(ins):
                count[0] += 1
                ins.then_inc(dve, 1)
                v.wait_ge(dve, count[0])

            v.wait_ge(c_in, 32)

            def bias(n):
                kind, h = units[n]
                s = n % 2
                src = acc[s][:, :].rearrange("p (i g k) -> p i g k", i=4, g=2)
                v.wait_ge(s_full, n + 1)
                if n >= 2:
                    v.wait_ge(t_full, n - 1)
                if kind == "near":
                    link(v.memset(S[s][:, 0, 0, :], -1e30))
                for g in range(2):
                    if kind == "far":
                        d, sl, i0 = dist[:, 2 + g, :], slope[:, N_HEADS * (1 + g) + h:N_HEADS * (1 + g) + h + 1], 0
                    else:
                        d, sl, i0 = dist[:, 1 - g, :], slope[:, h:h + 1], 1 - g
                    ins = v.scalar_tensor_tensor(S[s][:, i0:4, g, :], d.unsqueeze(1).broadcast_to([P, 4 - i0, P]), sl,
                                                 src[:, i0:4, g, :], ALU.mult, ALU.add)
                ins.then_inc(biased, 1)
                v.wait_ge(biased, n + 1)
                flat = S[s][:, :, :, :].rearrange("p i g k -> p i (g k)")
                if kind == "far":
                    m = far[:, :, h, HD:HD + 1].rearrange("p i o -> p (i o)")
                    link(v.tensor_reduce(m, flat, AX_X, ALU.max))
                else:
                    if h in HALVES[0][:1] + HALVES[1][:1]:
                        v.wait_ge(moved[h > 0], 16 * 16)
                    m = nmax[:, n % 4, :]
                    link(v.tensor_reduce(m, flat, AX_X, ALU.max))
                    link(v.tensor_tensor(m, m, near[:, :, h, HD:HD + 1].rearrange("p i o -> p (i o)"), ALU.max))
                    link(v.tensor_tensor(e12[:, n % 4, :], near[:, :, h, HD:HD + 1].rearrange("p i o -> p (i o)"), m, ALU.subtract))
                link(v.tensor_scalar(nmax[:, n % 4, :], m, -1.0, None, ALU.mult))
                v.sem_inc(maxed, 1)

            def add_far(n):
                kind, h = units[n]
                s = n % 2
                v.wait_ge(exped, n + 1)
                if kind == "far":
                    link(v.tensor_tensor(S[s][:, :, 0, :], S[s][:, :, 0, :], S[s][:, :, 1, :], ALU.add))
                v.sem_inc(summed, 1)

            def move(n):
                kind, h = units[n]
                s = n % 2
                v.wait_ge(t_full, n + 1)
                if kind == "near":
                    v.tensor_copy(PT[s][:, 5:8, :], aux[1][:, P:4 * P].rearrange("p (i q) -> p i q", i=3)).then_inc(t_moved, 1)
                else:
                    v.sem_inc(t_moved, 1)

            def finish(n):
                kind, h = units[n]
                s = n % 2
                v.wait_ge(o_full, n + 1)
                out = aux[2 + s][:, 0:4 * HD].rearrange("p (i d) -> p i d", i=4)
                if kind == "far":
                    v.tensor_copy(far[:, :, h, 0:HD], out).then_inc(o_moved, 1)
                    return
                link(v.tensor_tensor(den[:, s, :], e12[:, n % 4, :], near[:, :, h, HD + 1:HD + 2].rearrange("p i o -> p (i o)"), ALU.mult))
                link(v.tensor_tensor(den[:, s, :], den[:, s, :], l0[:, n % 4, :], ALU.add))
                v.tensor_tensor(on[:, :, :], near[:, :, h, 0:HD], e12[:, n % 4, :].unsqueeze(2).broadcast_to([P, 4, HD]), ALU.mult)
                link(v.reciprocal(den[:, s, :], den[:, s, :]))
                link(v.tensor_tensor(on[:, :, :], on[:, :, :], out, ALU.add))
                link(v.tensor_tensor(mem.o_nat[:, :, HD * h:HD * h + HD], on[:, :, :],
                                     den[:, s, :].unsqueeze(2).broadcast_to([P, 4, HD]), ALU.mult))
                v.sem_inc(o_moved, 1)

            bias(0)
            for n in range(len(units)):
                add_far(n)
                if n + 1 < len(units):
                    bias(n + 1)
                move(n)
                if n >= 1:
                    finish(n - 1)
            finish(len(units) - 1)

        @block.scalar
        def _(act):
            act.wait_ge(c_in, 32)
            for q in range(NS):
                act.dma_start(ten["s_kv"][q, 0:SEQ - 1, :, :, :], ten["cache_kv"][q, 1:SEQ, :, :, :]).then_inc(mem.cache_moved, 16)
            for n, (kind, h) in enumerate(units):
                s = n % 2
                act.wait_ge(maxed, n + 1)
                for i in range(4):
                    acc_out = far[:, i, h, HD + 1:HD + 2] if kind == "far" else l0[:, n % 4, i:i + 1]
                    ins = act.activation(S[s][:, i, :, :].rearrange("p g k -> p (g k)"), S[s][:, i, :, :].rearrange("p g k -> p (g k)"),
                                         ACT.Exp, bias=nmax[:, n % 4, i:i + 1], accum_out=acc_out)
                if kind == "near":
                    ins = act.activation(e12[:, n % 4, :], e12[:, n % 4, :], ACT.Exp)
                ins.then_inc(exped, 1)
                act.wait_ge(t_full, n + 1)
                act.activation(PT[s][:, 0:4, :], aux[0][:, :].rearrange("p (i q) -> p i q", i=4), ACT.Copy).then_inc(t_moved, 1)


NV = 4
KEYS = 2 * (P + 1) + 33


def decode_attention(nc, mem, ten, dram):
    o = mem.acth_at
    krow, qrow, prod, vring = [], [], [], []
    for s in range(2):
        t, o = mem.at(f"k_rows{s}", [P, 2, D], o)
        krow.append(t)
        t, o = mem.at(f"q_rows{s}", [P, 3, D], o)
        qrow.append(t)
    for s in range(3):
        t, o = mem.at(f"qk{s}", [P, D], o)
        prod.append(t)
    at = mem.q_at
    for s in range(NV):
        t, at = mem.at(f"v_rows{s}", [P, 2, D], at)
        vring.append(t)
    qhi, _ = mem.at("q_new_hi", [NS, 3, D], at, F32R)
    qlo, o = mem.at("q_new_lo", [NS, 3, D], o, F32R)
    pickq, o = mem.at("row_of_sequence", [NS, NS, P], o, F32R)
    pv = prod[2]
    vnew, o = mem.at("v_new", [NS, D], o)
    scT, o = mem.at("d_scoresT", [P, 3, NS, N_HEADS], o)
    ptz, o = mem.at("d_probsT", [P, 2, NS, P], o)
    qkz, o = mem.at("qk_new", [P, 3, P], o)
    drow, o = mem.at("distance_row", [P, P + 1], o)
    scol, o = mem.at("slope_column", [P, 3], o)
    pick, o = mem.at("sequence_of_row", [P, NS], o)
    sc, o = mem.at("d_scores", [P, KEYS], o)
    st, o = mem.at("d_stats", [P, 4], o)
    diag, o = mem.at("p_new_diagonal", [P, P], o)
    pnew, o = mem.at("p_new", [NS, P], o)
    assert o <= mem.rest
    mem.od, _ = mem.at("d_out", [P, DT, NS], mem.stat_at)
    acc, aux = mem.acc, mem.aux
    spans = ((0, P + 1, 1), (P + 1, P + 1, 1), (2 * (P + 1), 33, 4))
    with ExitStack() as ctx:
        def sem(x):
            return nc.alloc_semaphore(f"decode_{x}")

        c_in, zeroed = sem("constants_in"), sem("zeroed")
        v_in = [sem(f"v_rows_in{s}") for s in range(NV)]
        q_in, q_full, q_copied, picked = sem("q_rows_in"), sem("q_spread"), sem("q_copied"), sem("pick_ready")
        d_in, new_in = [sem("k_rows_in0"), sem("k_rows_in1")], sem("v_new_in")
        by_pool, by_dve, summed = sem("qk_by_pool"), sem("qk_by_dve"), sem("qk_summed")
        qk, s_full, maxed, exped, normed = sem("qk_new"), sem("scores"), sem("maxed"), sem("exped"), sem("normed")
        p_full, p_moved, v_used = sem("probs_transposed"), sem("probs_moved"), sem("v_used")
        o_moved, t_full = sem("out_moved"), sem("out_transposed")
        dve = sem("dve_chain")
        block = ctx.enter_context(nc.Block())

        @block.sync
        def _(sp):
            const, at = ten["constants"], 4 * P + 3 * N_HEADS
            sp.dma_start(drow[:, 0:P], const[:, at:at + P]).then_inc(c_in, 16)
            sp.dma_start(scol[:, :], const[:, at + P:at + P + 3]).then_inc(c_in, 16)
            sp.dma_start(pick[:, :], const[:, at + P + 3:at + P + 3 + NS]).then_inc(c_in, 16)
            cache = ten["cache_kv"].rearrange("s t z h d -> s t z (h d)")

            def load_v(s):
                sp.dma_start(vring[s % NV][:, 0, :], cache[s, SEQ - P:SEQ, 1, :]).then_inc(v_in[s % NV], 16)
                sp.dma_start(vring[s % NV][:, 1, :], cache[s, 0:SEQ - 3:4, 1, :]).then_inc(v_in[s % NV], 16)

            sp.dma_start(qlo[:, :, :].bitcast(F32), dram["q"][:, 1, :, :]).then_inc(q_in, 16)
            sp.wait_ge(qk, 1)
            sp.dma_start(qhi[:, :, :].bitcast(F32), dram["q"][:, 0, :, :]).then_inc(q_in, 16)
            for s in range(NS):
                if s >= 2:
                    sp.wait_ge(by_pool, 2 * s - 2)
                    sp.wait_ge(by_dve, s - 1)
                sp.dma_start(krow[s % 2][:, 0, :], cache[s, SEQ - P:SEQ, 0, :]).then_inc(d_in[s % 2], 16)
                sp.dma_start(krow[s % 2][:, 1, :], cache[s, 0:SEQ - 3:4, 0, :]).then_inc(d_in[s % 2], 16)
            sp.dma_start(vnew[:, :], ten["s_kv"][:, SEQ - 1, 1, :, :].rearrange("s h d -> s (h d)")).then_inc(new_in, 16)
            for s in range(NS):
                if s >= NV:
                    sp.wait_ge(v_used, s - NV + 1)
                load_v(s)

        @block.gpsimd
        def _(pool):
            pool.memset(qkz[:, :, :], 0.0).then_inc(zeroed, 1)
            pool.memset(drow[:, P:P + 1], 0.0).then_inc(zeroed, 1)
            pool.memset(ptz[:, :, :, :], 0.0).then_inc(zeroed, 1)
            for s in range(NS):
                pool.wait_ge(d_in[s % 2], 32 * (s // 2) + 32)
                for g in range(2):
                    pool.wait_ge(q_copied, 3 * s + g + 1)
                    if s >= 1:
                        pool.wait_ge(summed, 3 * s - 2 + g)
                    pool.tensor_tensor(prod[g][:, :], krow[s % 2][:, g, :], qrow[s % 2][:, g, :], ALU.mult).then_inc(by_pool, 1)

        @block.tensor
        def _(pe):
            pe.wait_ge(q_in, 32)
            pe.wait_ge(picked, 1)
            for n in range(3 * NS):
                if n >= 2:
                    pe.wait_ge(q_copied, n - 1)
                for c in (slice(0, 512), slice(512, 1024)):
                    for x in (qhi, qlo):
                        ins = nc.tensor.matmul(acc[n % 2][:, c], pickq[:, n // 3, :], x[:, n % 3, c],
                                               start=x is qhi, stop=x is qlo)
                ins.then_inc(q_full, 1)
            pe.wait_ge(qk, 1)
            pe.wait_ge(summed, 3 * NS)
            for g in range(3):
                at = g * (P + 1)
                nc.tensor.transpose(aux[0][:, at:at + P], scT[:, g, :, :].rearrange("p s h -> p (s h)"), mem.ident[:, :])
                ins = nc.tensor.matmul(aux[0][:, at + P:at + P + 1], qkz[:, g, :], mem.ones[:, 0:1], start=True, stop=True)
            ins.then_inc(s_full, 1)
            pe.wait_ge(normed, 1)
            nc.tensor.transpose(aux[1][:, 0:P], sc[:, 0:P], mem.ident[:, :])
            nc.tensor.transpose(aux[1][:, P:2 * P], sc[:, P + 1:2 * P + 1], mem.ident[:, :])
            nc.tensor.matmul(aux[1][0:NS, 2 * P:3 * P], pick[:, :], diag[:, :], start=True, stop=True).then_inc(p_full, 1)
            pe.wait_ge(p_moved, 3)
            pe.wait_ge(new_in, 16)
            halves = (slice(0, 512), slice(512, 1024))
            for c in halves:
                nc.tensor.matmul(acc[0][:, c], pnew[:, :], vnew[:, c], start=True, stop=False)
            for s in range(NS):
                pe.wait_ge(v_in[s % NV], 32 * (s // NV) + 32)
                for which in range(2):
                    for c in halves:
                        ins = nc.tensor.matmul(acc[0][:, c], ptz[:, which, s, :], vring[s % NV][:, which, c],
                                               start=False, stop=s == NS - 1 and which == 1)
                ins.then_inc(v_used, 1)
            pe.wait_ge(o_moved, 2)
            for f in range(DT):
                ins = nc.tensor.transpose(aux[2 + f // 4][:, P * (f % 4):P * (f % 4) + P], pv[:, P * f:P * f + P], mem.ident[:, :])
            ins.then_inc(t_full, 1)

        @block.scalar
        def _(act):
            for n in range(3 * NS):
                q = n // 3
                if q >= 2 and n % 3 == 0:
                    act.wait_ge(by_pool, 2 * q - 2)
                    act.wait_ge(by_dve, q - 1)
                act.wait_ge(q_full, n + 1)
                act.activation(qrow[q % 2][:, n % 3, :], acc[n % 2][:, :], ACT.Copy).then_inc(q_copied, 1)
            act.wait_ge(maxed, 1)
            act.activation(sc[:, :], sc[:, :], ACT.Exp, bias=st[:, 1:2], accum_out=st[:, 2:3]).then_inc(exped, 1)
            act.wait_ge(v_used, NS)
            act.activation(pv[:, 0:512], acc[0][:, 0:512], ACT.Copy).then_inc(o_moved, 1)

        @block.vector
        def _(v):
            count = [0]

            def link(ins):
                count[0] += 1
                ins.then_inc(dve, 1)
                v.wait_ge(dve, count[0])

            v.tensor_copy(pickq[:, :, :], mem.ident[0:NS, 0:NS].unsqueeze(2).broadcast_to([NS, NS, P])).then_inc(picked, 1)
            v.wait_ge(zeroed, 1)
            for g in range(3):
                for e in range(2):
                    half = slice(64 * e, 64 * e + 64)
                    ins = v.tensor_tensor(qkz[half, g, :].rearrange("p (s f e) -> p e f s", e=2, f=DT)[:, e, :, :],
                                          mem.q[half, DT * g:DT * g + DT, SEQ:TOK], mem.kv[half, 0:DT, SEQ:TOK], ALU.mult)
            ins.then_inc(qk, 1)
            v.wait_ge(zeroed, 3)

            def total(s, g):
                v.tensor_reduce(scT[:, g, s, :], prod[g][:, :].rearrange("p (h d) -> p h d", d=HD),
                                AX_X, ALU.add).then_inc(summed, 1)

            for s in range(NS):
                v.wait_ge(d_in[s % 2], 32 * (s // 2) + 32)
                v.wait_ge(q_copied, 3 * s + 3)
                if s >= 1:
                    v.wait_ge(summed, 3 * s)
                v.tensor_tensor(prod[2][:, :], krow[s % 2][:, 1, :], qrow[s % 2][:, 2, :], ALU.mult).then_inc(by_dve, 1)
                for g in range(2):
                    v.wait_ge(by_pool, 2 * s + g + 1)
                    total(s, g)
                v.wait_ge(by_dve, s + 1)
                total(s, 2)
            v.wait_ge(c_in, 48)
            v.wait_ge(s_full, 1)
            for g, (at, n, step) in enumerate(spans):
                x = aux[0][:, g * (P + 1):g * (P + 1) + (n - 1) * step + 1:step]
                ins = v.scalar_tensor_tensor(sc[:, at:at + n], drow[:, 0:(n - 1) * step + 1:step], scol[:, g:g + 1], x,
                                             ALU.mult, ALU.add)
            link(ins)
            link(v.tensor_reduce(st[:, 0:1], sc[:, :], AX_X, ALU.max))
            link(v.tensor_scalar(st[:, 1:2], st[:, 0:1], -1.0, None, ALU.mult))
            v.sem_inc(maxed, 1)
            v.wait_ge(exped, 1)
            link(v.reciprocal(st[:, 3:4], st[:, 2:3]))
            link(v.tensor_tensor(sc[:, P + 1:2 * (P + 1):4], sc[:, P + 1:2 * (P + 1):4], sc[:, 2 * (P + 1):KEYS], ALU.add))
            link(v.tensor_tensor(sc[:, P:P + 1], sc[:, P:P + 1], sc[:, 2 * P + 1:2 * P + 2], ALU.add))
            link(v.tensor_scalar(sc[:, 0:2 * P + 1], sc[:, 0:2 * P + 1], st[:, 3:4], None, ALU.mult))
            link(v.tensor_scalar(diag[:, :], mem.ident[:, :], sc[:, P:P + 1], None, ALU.mult))
            v.sem_inc(normed, 1)
            v.wait_ge(p_full, 1)
            v.tensor_copy(pnew[:, :], aux[1][0:NS, 2 * P:3 * P]).then_inc(p_moved, 1)
            for which in range(2):
                for s in range(NS):
                    ins = v.tensor_copy(ptz[:, which, s, N_HEADS * s:N_HEADS * s + N_HEADS],
                                        aux[1][:, P * which + N_HEADS * s:P * which + N_HEADS * s + N_HEADS])
                ins.then_inc(p_moved, 1)
            v.wait_ge(v_used, NS)
            v.tensor_copy(pv[:, 512:1024], acc[0][:, 512:1024]).then_inc(o_moved, 1)
            v.wait_ge(t_full, 1)
            for part in range(2):
                for e in range(2):
                    half = slice(64 * e, 64 * e + 64)
                    for f in range(4 * part, 4 * part + 4):
                        ins = v.tensor_copy(mem.od[half, f, :], aux[2 + part][half, P * (f % 4) + 2 * f + e:P * (f % 4) + P:N_HEADS])
            link(ins)


def gate_output(nc, mem, ten, dram):
    o = mem.actl_at + DT * TOK * 4
    y = []
    for s in range(2):
        t, o = mem.at(f"gated{s}", [P, TOK], o)
        y.append(t)
    aux = mem.aux
    w_out = blocks(ten["b_w_out"][0, :, :])
    mem.b_out = nxt = Dense(nc, mem, "b_out", 1, [w_out[:, :, cols(n)] for n in range(2)])
    with ExitStack() as ctx:
        def sem(x):
            return nc.alloc_semaphore(f"gate_o_{x}")

        full, prod, hi, lo = sem("transposed"), sem("product"), sem("hi_ready"), sem("lo_ready")
        block = ctx.enter_context(nc.Block())

        @block.sync
        def _(sp):
            nxt.load_first(sp)

        @block.gpsimd
        def _(pool):
            nxt.split_lo_first(pool)

        @block.tensor
        def _(pe):
            for f in range(DT):
                if f >= 4:
                    pe.wait_ge(prod, f - 3)
                for b in range(4):
                    ins = nc.tensor.transpose(aux[f % 4][:, P * b:P * b + P], mem.o_nat[:, b, P * f:P * f + P], mem.ident[:, :])
                ins.then_inc(full, 1)

        @block.vector
        def _(v):
            def low(f):
                v.wait_ge(hi, f + 1)
                v.tensor_tensor(mem.actl[:, f, :], y[f % 2][:, :], mem.acth[:, f, :].bitcast(F32), ALU.subtract).then_inc(lo, 1)

            for f in range(DT):
                v.wait_ge(full, f + 1)
                if f >= 2:
                    v.wait_ge(lo, f - 1)
                v.tensor_tensor(y[f % 2][:, SEQ:TOK], mem.od[:, f, :], mem.zb[:, f, SEQ:TOK], ALU.mult)
                v.tensor_tensor(y[f % 2][:, 0:SEQ], aux[f % 4][:, :], mem.zb[:, f, 0:SEQ], ALU.mult).then_inc(prod, 1)
                if f >= 1:
                    low(f - 1)
            low(DT - 1)

        @block.scalar
        def _(act):
            for f in range(DT):
                if f == 2:
                    nxt.split_hi_first(act)
                act.wait_ge(prod, f + 1)
                act.activation(mem.acth[:, f, :], y[f % 2][:, :], ACT.Copy).then_inc(hi, 1)


def attn_out(nc, mem, ten, dram):
    residual(nc, mem, "b_out", mem.b_out, ten["b_w_out"][0, :, :], 1, mem.acth[:, 0:DT, :], mem.actl[:, 0:DT, :], V_BPOST,
             mem.rest, mem.rest + DT * TOK * 4, natural=True)


def write_y(nc, mem, ten, dram):
    yo, o = mem.at("y_rows", [P, 4, D], mem.acth_at)
    ys, o = mem.at("y_sample_rows", [NS, D], o)
    acc = mem.acc
    with ExitStack() as ctx:
        def sem(x):
            return nc.alloc_semaphore(f"write_{x}")

        full, moved_a, moved_v, stored = sem("transposed"), sem("moved_act"), sem("moved_dve"), sem("stored")
        block = ctx.enter_context(nc.Block())

        @block.tensor
        def _(pe):
            for n in range(5):
                if n >= 2:
                    pe.wait_ge(moved_a if n % 2 == 0 else moved_v, n // 2)
                for f in range(DT):
                    if n < 4:
                        out, src = acc[n % 2][:, P * f:P * f + P], mem.xT[:, f, P * n:P * n + P]
                    else:
                        out, src = acc[0][0:NS, P * f:P * f + P], mem.xT[:, f, SEQ:TOK]
                    ins = nc.tensor.transpose(out, src, mem.ident[:, :])
                ins.then_inc(full, 1)

        @block.scalar
        def _(act):
            for n in (0, 2, 4):
                act.wait_ge(full, n + 1)
                if n < 4:
                    act.activation(yo[:, n, :], acc[0][:, :], ACT.Copy).then_inc(moved_a, 1)
                else:
                    act.activation(ys[:, :], acc[0][0:NS, :], ACT.Copy).then_inc(moved_a, 1)

        @block.vector
        def _(v):
            for n in (1, 3):
                v.wait_ge(full, n + 1)
                v.tensor_copy(yo[:, n, :], acc[1][:, :]).then_inc(moved_v, 1)

        @block.sync
        def _(sp):
            yp = ten["y_prompt"][0, :, :].rearrange("(c j) d -> j c d", j=L)
            for n in range(4):
                sp.wait_ge(moved_a if n % 2 == 0 else moved_v, n // 2 + 1)
                for i in range(2):
                    sp.dma_start(yp[2 * n + i], yo[64 * i:64 * i + 64, n, :]).then_inc(stored, 16)
            sp.wait_ge(moved_a, 3)
            sp.dma_start(ten["y_sample"][:, 0, :], ys[:, :]).then_inc(stored, 16)
            sp.wait_ge(stored, 16 * 9)
            sp.wait_ge(mem.cache_moved, 16 * NS)


INS = ["x_prompt", "x_sample", "state_s5_re", "state_s5_im", "cache_kv", "a_norm_pre", "a_w_in", "a_lam_re",
       "a_lam_im", "a_log_dt", "a_b_re", "a_b_im", "a_c_re", "a_c_im", "a_d", "a_w_glu", "a_b_glu", "a_w_out",
       "a_norm_post", "kv_norm", "w_kv", "b_norm_pre", "b_w_in", "b_w_out", "b_norm_post"]
OUTS = [("y_prompt", (1, SEQ, D)), ("y_sample", (NS, 1, D)), ("p_re", (1, 1, G, ST)), ("p_im", (1, 1, G, ST)),
        ("p_kv", (1, SEQ, 2, N_HEADS, HD)), ("s_re", (1, NS, G, ST)), ("s_im", (1, NS, G, ST)),
        ("s_kv", (NS, SEQ, 2, N_HEADS, HD))]


def trunk(nc, ten, phases=99):
    mem = plan(nc)
    dram = {
        "u": nc.dram_tensor("scratch_u", (W2, TOK), F32, kind="Internal").ap(),
        "y": nc.dram_tensor("scratch_y", (W2, TOK), F32, kind="Internal").ap(),
        "z": nc.dram_tensor("scratch_z", (W2, TOK), F32, kind="Internal").ap(),
        "u_chunks": nc.dram_tensor("scratch_u_chunks", (NB, P, BG, YC), F32, kind="Internal").ap(),
        "q": nc.dram_tensor("scratch_q", (NS, 2, 3, D), F32, kind="Internal").ap(),
        "k": nc.dram_tensor("scratch_k", (CH, G, 15 * CH), F32, kind="Internal").ap(),
    }
    with ExitStack() as ctx:
        mem.acc = [ctx.enter_context(nc.psum_tensor(f"acc{a}", [P, 1024], F32)) for a in range(2)]
        mem.aux = [ctx.enter_context(nc.psum_tensor(f"aux{a}", [P, 512], F32)) for a in range(4)]
        mem.cache_moved = nc.alloc_semaphore("cache_moved")
        parts = (setup, states, gate_and_scan, outputs, glu, ssm_out,
                 project, token_rows, attention, decode_attention, gate_output, attn_out, write_y)[:phases]
        for group in (parts[:3], parts[3:]):
            with nc.cleanup_on_exit():
                for f in group:
                    f(nc, mem, ten, dram)
    return mem


def constants(np):
    far = np.float32(-1e30)
    n = np.arange(P)
    own = n[None, :] - n[:, None]
    prev = own - P
    tabs = [np.where(own <= 0, own, far), np.where(prev >= -P, prev, far),
            np.where(own <= 0, 4 * own, far),
            np.where((own <= 0) & (own % 4 == 0), 4 * own, far)]
    slopes = np.broadcast_to(np.array(SLOPE, np.float64).reshape(1, 3 * N_HEADS), (P, 3 * N_HEADS))
    row = np.broadcast_to((n[None, :] - P), (P, P))
    steps = np.array([1.0, 4.0, 4.0]).reshape(3, 1)
    d_slopes = np.tile((np.array(SLOPE, np.float64) * steps).T, (NS, 1))
    pick = (n[:, None] // N_HEADS == np.arange(NS)[None, :]).astype(np.float32)
    return np.concatenate(tabs + [slopes, row, d_slopes, pick], axis=1).astype(np.float32)


def kernel(**inputs):
    import numpy as np
    import concourse.bacc as bacc
    from concourse.bass_utils import run_bass_kernel_spmd

    nc = bacc.Bacc("TRN2", target_bir_lowering=False, num_devices=1)
    arrays, ten = {}, {}
    for name in INS:
        a = np.ascontiguousarray(inputs[name])
        arrays[name] = a
        ten[name] = nc.dram_tensor(name, a.shape, mybir.dt.from_np(a.dtype), kind="ExternalInput").ap()
    arrays["constants"] = constants(np)
    ten["constants"] = nc.dram_tensor("constants", arrays["constants"].shape, F32, kind="ExternalInput").ap()
    for name, shape in OUTS:
        ten[name] = nc.dram_tensor(name, shape, F32, kind="ExternalOutput").ap()
    trunk(nc, ten)
    r = run_bass_kernel_spmd(nc, [arrays], core_ids=[0])
    return tuple(r.results[0][name] for name, _ in OUTS)
```
